# Optimizing a Trainium2 kernel written in Bass

```python
import jax, jax.numpy as jnp
from jax import lax
import numpy as np

D_MODEL = 1024
BATCH = 1
SEQ = 256
DEPTH = 2

HEAD_DIM = 64
N_MIX_HEADS = D_MODEL // HEAD_DIM
A_Q_HEADS = N_MIX_HEADS // 2
A_KV_HEADS = 2
B_Q_HEADS = N_MIX_HEADS - A_Q_HEADS
B_KV_HEADS = 2
MIX_WIDTH = (A_Q_HEADS + B_Q_HEADS) * HEAD_DIM
QA_W = A_Q_HEADS * HEAD_DIM
KVA_W = A_KV_HEADS * HEAD_DIM
QB_W = B_Q_HEADS * HEAD_DIM
KVB_W = B_KV_HEADS * HEAD_DIM
IN_WIDTH = QA_W + 2 * KVA_W + QB_W + 2 * KVB_W
SPLITS = [QA_W, QA_W + KVA_W, QA_W + 2 * KVA_W, QA_W + 2 * KVA_W + QB_W,
          QA_W + 2 * KVA_W + QB_W + KVB_W]

BLOCK = 128
WINDOW = 128
GRID_W = 64
ROPE_THETA = 10000.0
ROPE_FREQS = HEAD_DIM // 4

PEER_HEADS = 8
PEER_NKEYS = 128
PEER_EXPERTS = PEER_NKEYS * PEER_NKEYS
PEER_DKEY = 256
PEER_TOPK = 16
PEER_CHUNK = 128

DEEPNORM_ALPHA = (2.0 * DEPTH) ** 0.25
DEEPNORM_BETA = (8.0 * DEPTH) ** -0.25
LN_EPS = 1e-5
RMS_EPS = 1e-6
NEG_INF = -1e30


def alibi_slopes(n):
    return (2.0 ** (-(np.arange(1, n + 1, dtype=np.float32) * 8.0 / n))).astype(np.float32)

def layer_norm(x, g, b):
    xf = x.astype(jnp.float32)
    mu = xf.mean(-1, keepdims=True)
    var = jnp.square(xf - mu).mean(-1, keepdims=True)
    return ((xf - mu) * lax.rsqrt(var + LN_EPS) * g + b).astype(x.dtype)

def rms_norm(x, g):
    xf = x.astype(jnp.float32)
    return (xf * lax.rsqrt(jnp.square(xf).mean(-1, keepdims=True) + RMS_EPS) * g).astype(x.dtype)

def axial_rope_tables(S):
    rows = S // GRID_W
    row = jnp.repeat(jnp.arange(rows), GRID_W)
    col = jnp.tile(jnp.arange(GRID_W), rows)
    pos = jnp.stack([row, col], axis=-1).astype(jnp.float32)
    inv_freq = ROPE_THETA ** (-jnp.arange(ROPE_FREQS, dtype=jnp.float32) / ROPE_FREQS)
    ang = pos[:, :, None] * inv_freq
    return jnp.cos(ang), jnp.sin(ang)

def apply_axial_rope(x, cos, sin):
    B, S, H, dh = x.shape
    xr = x.astype(jnp.float32).reshape(B, S, H, 2, 2, ROPE_FREQS)
    x1, x2 = xr[..., 0, :], xr[..., 1, :]
    c, s = cos[None, :, None], sin[None, :, None]
    out = jnp.stack([x1 * c - x2 * s, x1 * s + x2 * c], axis=-2)
    return out.reshape(B, S, H, dh).astype(x.dtype)

def global_attention(q, k, v):
    B, S, Hq, dh = q.shape
    Hkv = k.shape[2]
    G = Hq // Hkv
    nb = S // BLOCK
    scale = dh ** -0.5
    qb = q.reshape(B, nb, BLOCK, Hkv, G, dh).transpose(1, 0, 2, 3, 4, 5)

    def one_block(qblk):
        sc = jnp.einsum('bqkgd,bskd->bkgqs', qblk, k, preferred_element_type=jnp.float32) * scale
        p = jax.nn.softmax(sc, axis=-1).astype(v.dtype)
        return jnp.einsum('bkgqs,bskd->bqkgd', p, v)

    o = lax.map(one_block, qb)
    return o.transpose(1, 0, 2, 3, 4, 5).reshape(B, S, Hq, dh)

def window_sink_attention(q, k, v, sink, slopes):
    B, S, Hq, dh = q.shape
    Hkv = k.shape[2]
    G = Hq // Hkv
    nb = S // BLOCK
    span = BLOCK + 2 * WINDOW
    scale = dh ** -0.5
    qb = q.reshape(B, nb, BLOCK, Hkv, G, dh).transpose(1, 0, 2, 3, 4, 5)
    pad = ((0, 0), (WINDOW, WINDOW), (0, 0), (0, 0))
    kp = jnp.pad(k, pad)
    vp = jnp.pad(v, pad)
    slope = slopes.reshape(Hkv, G, 1, 1)
    sink_l = sink.astype(jnp.float32).reshape(Hkv, G, 1)
    q_off = jnp.arange(BLOCK)
    k_off = jnp.arange(span) - WINDOW

    def one_block(args):
        qblk, j = args
        start = j * BLOCK
        kb = lax.dynamic_slice_in_dim(kp, start, span, axis=1)
        vb = lax.dynamic_slice_in_dim(vp, start, span, axis=1)
        t = start + q_off
        s_pos = start + k_off
        dist = jnp.abs(t[:, None] - s_pos[None, :])
        valid = (dist <= WINDOW) & (s_pos >= 0)[None, :] & (s_pos < S)[None, :]
        sc = jnp.einsum('bqkgd,bskd->bkgqs', qblk, kb, preferred_element_type=jnp.float32) * scale
        sc = sc - slope * dist.astype(jnp.float32)
        sc = jnp.where(valid, sc, NEG_INF)
        m = jnp.maximum(sc.max(-1), sink_l)
        p = jnp.exp(sc - m[..., None])
        denom = p.sum(-1) + jnp.exp(sink_l - m)
        p = (p / denom[..., None]).astype(v.dtype)
        return jnp.einsum('bkgqs,bskd->bqkgd', p, vb)

    o = lax.map(one_block, (qb, jnp.arange(nb)))
    return o.transpose(1, 0, 2, 3, 4, 5).reshape(B, S, Hq, dh)

def peer_ffn(x, wq, sub_keys, u, v):
    B, S, D = x.shape
    xt = x.reshape(-1, PEER_CHUNK, D)
    half = PEER_DKEY // 2

    def chunk(xc):
        q = (xc @ wq).reshape(PEER_CHUNK, PEER_HEADS, 2, half)
        sc = jnp.einsum('chpd,hpnd->chpn', q, sub_keys, preferred_element_type=jnp.float32)
        s1, i1 = lax.top_k(sc[:, :, 0], PEER_TOPK)
        s2, i2 = lax.top_k(sc[:, :, 1], PEER_TOPK)
        cand = (s1[..., :, None] + s2[..., None, :]).reshape(PEER_CHUNK, PEER_HEADS, PEER_TOPK * PEER_TOPK)
        cidx = (i1[..., :, None] * PEER_NKEYS + i2[..., None, :]).reshape(PEER_CHUNK, PEER_HEADS, PEER_TOPK * PEER_TOPK)
        top_s, pos = lax.top_k(cand, PEER_TOPK)
        eidx = jnp.take_along_axis(cidx, pos, axis=-1)
        g = jax.nn.softmax(top_s, axis=-1)
        u_sel = jnp.take(u, eidx, axis=0)
        a = jax.nn.gelu(jnp.einsum('chkd,cd->chk', u_sel, xc, preferred_element_type=jnp.float32), approximate=False)
        w = (g * a).astype(x.dtype)
        v_sel = jnp.take(v, eidx, axis=0)
        return jnp.einsum('chk,chkd->cd', w, v_sel)

    return lax.map(chunk, xt).reshape(B, S, D)

def first_inputs(seed: int = 0) -> dict:
    key = jax.random.key(seed)
    ks = jax.random.split(key, 24)
    L, D = DEPTH, D_MODEL
    beta = DEEPNORM_BETA

    def nrm(k, shape, std):
        return jax.random.normal(k, shape, jnp.float32) * std

    x = nrm(ks[0], (BATCH, SEQ, D), 1.0)
    ln_in_g = 1.0 + nrm(ks[1], (D,), 0.02)
    ln_in_b = nrm(ks[2], (D,), 0.02)
    col_scale = jnp.concatenate([
        jnp.ones((QA_W + KVA_W,), jnp.float32), jnp.full((KVA_W,), beta, jnp.float32),
        jnp.ones((QB_W + KVB_W,), jnp.float32), jnp.full((KVB_W,), beta, jnp.float32)])
    w_in = nrm(ks[3], (L, D, IN_WIDTH), D ** -0.5) * col_scale
    qn_g = 1.0 + nrm(ks[4], (L, HEAD_DIM), 0.02)
    kn_g = 1.0 + nrm(ks[5], (L, HEAD_DIM), 0.02)
    sink = nrm(ks[6], (L, B_Q_HEADS), 0.5)
    gn_a_g = 1.0 + nrm(ks[7], (L, QA_W), 0.02)
    gn_b_g = 1.0 + nrm(ks[8], (L, QB_W), 0.02)
    w_o = nrm(ks[9], (L, MIX_WIDTH, D), beta * MIX_WIDTH ** -0.5)
    ln1_g = 1.0 + nrm(ks[10], (L, D), 0.02)
    ln1_b = nrm(ks[11], (L, D), 0.02)
    peer_wq = nrm(ks[12], (L, D, PEER_HEADS * PEER_DKEY), D ** -0.5)
    peer_keys = nrm(ks[13], (L, PEER_HEADS, 2, PEER_NKEYS, PEER_DKEY // 2), (PEER_DKEY // 2) ** -0.5)
    peer_u = nrm(ks[14], (L, PEER_EXPERTS, D), D ** -0.5)
    peer_v = nrm(ks[15], (L, PEER_EXPERTS, D), beta * (PEER_HEADS * PEER_TOPK) ** -0.5)
    ln2_g = 1.0 + nrm(ks[16], (L, D), 0.02)
    ln2_b = nrm(ks[17], (L, D), 0.02)
    return {'x': x, 'ln_in_g': ln_in_g, 'ln_in_b': ln_in_b, 'w_in': w_in,
            'qn_g': qn_g, 'kn_g': kn_g, 'sink': sink, 'gn_a_g': gn_a_g, 'gn_b_g': gn_b_g,
            'w_o': w_o, 'ln1_g': ln1_g, 'ln1_b': ln1_b, 'peer_wq': peer_wq,
            'peer_keys': peer_keys, 'peer_u': peer_u, 'peer_v': peer_v,
            'ln2_g': ln2_g, 'ln2_b': ln2_b}

def first_block(x, ln_in_g, ln_in_b, w_in, qn_g, kn_g, sink, gn_a_g, gn_b_g, w_o,
              ln1_g, ln1_b, peer_wq, peer_keys, peer_u, peer_v, ln2_g, ln2_b):
    B, S, D = x.shape
    cos, sin = axial_rope_tables(S)
    slopes = jnp.asarray(alibi_slopes(B_Q_HEADS))
    h = layer_norm(x, ln_in_g, ln_in_b)
    for l in range(DEPTH):
        proj = h @ w_in[l]
        qa, ka, va, qb, kb, vb = jnp.split(proj, SPLITS, axis=-1)
        qa = qa.reshape(B, S, A_Q_HEADS, HEAD_DIM)
        ka = ka.reshape(B, S, A_KV_HEADS, HEAD_DIM)
        va = va.reshape(B, S, A_KV_HEADS, HEAD_DIM)
        qb = qb.reshape(B, S, B_Q_HEADS, HEAD_DIM)
        kb = kb.reshape(B, S, B_KV_HEADS, HEAD_DIM)
        vb = vb.reshape(B, S, B_KV_HEADS, HEAD_DIM)
        qa = apply_axial_rope(rms_norm(qa, qn_g[l]), cos, sin)
        ka = apply_axial_rope(rms_norm(ka, kn_g[l]), cos, sin)
        oa = global_attention(qa, ka, va)
        ob = window_sink_attention(qb, kb, vb, sink[l], slopes)
        oa = rms_norm(oa, gn_a_g[l].reshape(A_Q_HEADS, HEAD_DIM)).reshape(B, S, QA_W)
        ob = rms_norm(ob, gn_b_g[l].reshape(B_Q_HEADS, HEAD_DIM)).reshape(B, S, QB_W)
        mix = jnp.concatenate([oa, ob], axis=-1) @ w_o[l]
        h = layer_norm(DEEPNORM_ALPHA * h + mix, ln1_g[l], ln1_b[l])
        ffn = peer_ffn(h, peer_wq[l], peer_keys[l], peer_u[l], peer_v[l])
        h = layer_norm(DEEPNORM_ALPHA * h + ffn, ln2_g[l], ln2_b[l])
    return h


DEPTH_2 = 1

MEM_LEN = 256
CONV_WIDTH = D_MODEL // 2
CONV_K = 3
ATT_HEADS = 8
ATT_WIDTH = ATT_HEADS * HEAD_DIM
KV_GROUPS = 2
Q_PER_KV = ATT_HEADS // KV_GROUPS
KV_WIDTH = KV_GROUPS * HEAD_DIM
MIX_WIDTH_2 = CONV_WIDTH + ATT_WIDTH
CMP_BLOCK = 32
CMP_STRIDE = 16
CMP_HIDDEN = 256
SLC_BLOCK = 64
N_SELECT = 16
WINDOW_2 = 512
Q_BLOCK = 128
X_HEADS = 4
X_HEAD_DIM = D_MODEL // X_HEADS
D_FF = -(-8 * D_MODEL // (3 * 256)) * 256
EPS = 1e-6
FORCE = 1e4
W_IN_COLS = 3 * CONV_WIDTH + ATT_WIDTH + 6 * KV_WIDTH + 3 * ATT_HEADS


def rmsnorm(x, g):
    xf = x.astype(jnp.float32)
    y = xf * lax.rsqrt(jnp.mean(xf * xf, axis=-1, keepdims=True) + EPS)
    return (y * g.astype(jnp.float32)).astype(x.dtype)

def rope(x, pos):
    half = HEAD_DIM // 2
    inv = ROPE_THETA ** (-jnp.arange(half, dtype=jnp.float32) / half)
    ang = pos.astype(jnp.float32)[..., None] * inv
    cos = jnp.cos(ang)[:, :, None, :]
    sin = jnp.sin(ang)[:, :, None, :]
    xf = x.astype(jnp.float32)
    x1, x2 = xf[..., :half], xf[..., half:]
    return jnp.concatenate([x1 * cos - x2 * sin, x2 * cos + x1 * sin], axis=-1).astype(x.dtype)

def masked_softmax(s, mask):
    s = jnp.where(mask, s.astype(jnp.float32), -1e30)
    e = jnp.exp(s - jnp.max(s, axis=-1, keepdims=True)) * mask
    return e / jnp.maximum(jnp.sum(e, axis=-1, keepdims=True), 1e-30)

def compress(k, pe, w1, w2, n_cmp):
    b = k.shape[0]
    idx = np.arange(n_cmp)[:, None] * CMP_STRIDE + np.arange(CMP_BLOCK)[None, :]
    blocks = k[:, idx] + pe[None, None, :, None, :]
    flat = blocks.transpose(0, 1, 3, 2, 4).reshape(b, n_cmp, KV_GROUPS, CMP_BLOCK * HEAD_DIM)
    return jax.nn.silu(flat @ w1) @ w2

def short_conv_mixer(bg, cg, xin, conv_w):
    z = cg * xin
    zc = lax.conv_general_dilated(z, conv_w[:, None, :].astype(z.dtype), window_strides=(1,),
                                  padding=((CONV_K - 1, 0),), dimension_numbers=("NWC", "WIO", "NWC"),
                                  feature_group_count=CONV_WIDTH)
    return bg * zc

def nsa_mixer(q, k_cmp_raw, v_cmp_raw, k_slc, v_slc, k_win, v_win, gates, positions,
              pe_kc, w1_kc, w2_kc, pe_vc, w1_vc, w2_vc):
    b, s = q.shape[0], q.shape[1]
    n_cmp = (s - CMP_BLOCK) // CMP_STRIDE + 1
    n_slc = s // SLC_BLOCK
    n_sel = min(N_SELECT, n_slc)
    scale = HEAD_DIM ** -0.5

    q = rope(q, positions)
    cmp_end_np = np.arange(n_cmp) * CMP_STRIDE + CMP_BLOCK - 1
    cmp_end = jnp.asarray(cmp_end_np, dtype=jnp.int32)
    k_cmp = rope(compress(k_cmp_raw, pe_kc, w1_kc, w2_kc, n_cmp), positions[:, cmp_end_np])
    v_cmp = compress(v_cmp_raw, pe_vc, w1_vc, w2_vc, n_cmp)

    ci = np.arange(n_cmp)[:, None] * CMP_STRIDE
    sj = np.arange(n_slc)[None, :] * SLC_BLOCK
    ov = np.clip(np.minimum(ci + CMP_BLOCK, sj + SLC_BLOCK) - np.maximum(ci, sj), 0, None)
    slc_map = jnp.asarray(ov / CMP_BLOCK, dtype=jnp.float32)

    k_blocks = rope(k_slc, positions).reshape(b, n_slc, SLC_BLOCK, KV_GROUPS, HEAD_DIM).transpose(0, 3, 1, 2, 4)
    v_blocks = v_slc.reshape(b, n_slc, SLC_BLOCK, KV_GROUPS, HEAD_DIM).transpose(0, 3, 1, 2, 4)
    pad = ((0, 0), (WINDOW_2, 0), (0, 0), (0, 0))
    k_win_pad = jnp.pad(rope(k_win, positions), pad)
    v_win_pad = jnp.pad(v_win, pad)
    bi = jnp.arange(b)[:, None, None, None]
    gi = jnp.arange(KV_GROUPS)[None, :, None, None]
    blk = jnp.arange(n_slc)

    def block(i):
        s0 = i * Q_BLOCK
        t = s0 + jnp.arange(Q_BLOCK)
        qb = lax.dynamic_slice_in_dim(q, s0, Q_BLOCK, axis=1).reshape(b, Q_BLOCK, KV_GROUPS, Q_PER_KV, HEAD_DIM)
        gb = lax.dynamic_slice_in_dim(gates, s0, Q_BLOCK, axis=1).reshape(b, Q_BLOCK, KV_GROUPS, Q_PER_KV, 3)

        s_c = jnp.einsum("bqgrd,bkgd->bgrqk", qb, k_cmp) * scale
        p_c = masked_softmax(s_c, cmp_end[None, :] <= t[:, None])
        o_c = jnp.einsum("bgrqk,bkgd->bqgrd", p_c, v_cmp)

        imp = jnp.einsum("bgrqk,ks->bgqs", p_c, slc_map)
        cur = t // SLC_BLOCK
        forced = (blk[None, :] == 0) | (blk[None, :] == cur[:, None]) | (blk[None, :] == cur[:, None] - 1)
        future = blk[None, :] * SLC_BLOCK > t[:, None]
        imp = jnp.where(forced, FORCE, jnp.where(future, -FORCE, imp))
        _, sel = lax.top_k(imp, n_sel)
        ks = k_blocks[bi, gi, sel].reshape(b, KV_GROUPS, Q_BLOCK, n_sel * SLC_BLOCK, HEAD_DIM)
        vs = v_blocks[bi, gi, sel].reshape(b, KV_GROUPS, Q_BLOCK, n_sel * SLC_BLOCK, HEAD_DIM)
        kpos = (sel[..., None] * SLC_BLOCK + jnp.arange(SLC_BLOCK)).reshape(b, KV_GROUPS, Q_BLOCK, n_sel * SLC_BLOCK)
        s_s = jnp.einsum("bqgrd,bgqkd->bgrqk", qb, ks) * scale
        p_s = masked_softmax(s_s, (kpos <= t[None, None, :, None])[:, :, None])
        o_s = jnp.einsum("bgrqk,bgqkd->bqgrd", p_s, vs)

        kw = lax.dynamic_slice_in_dim(k_win_pad, s0, Q_BLOCK + WINDOW_2, axis=1)
        vw = lax.dynamic_slice_in_dim(v_win_pad, s0, Q_BLOCK + WINDOW_2, axis=1)
        wpos = s0 - WINDOW_2 + jnp.arange(Q_BLOCK + WINDOW_2)
        mask_w = (wpos[None, :] <= t[:, None]) & (wpos[None, :] > t[:, None] - WINDOW_2) & (wpos[None, :] >= 0)
        s_w = jnp.einsum("bqgrd,bkgd->bgrqk", qb, kw) * scale
        p_w = masked_softmax(s_w, mask_w)
        o_w = jnp.einsum("bgrqk,bkgd->bqgrd", p_w, vw)

        o = gb[..., 0:1] * o_c + gb[..., 1:2] * o_s + gb[..., 2:3] * o_w
        return o.reshape(b, Q_BLOCK, ATT_WIDTH).astype(q.dtype)

    out = lax.map(block, jnp.arange(s // Q_BLOCK))
    return out.transpose(1, 0, 2, 3).reshape(b, s, ATT_WIDTH)

def second_inputs(seed: int = 0) -> dict:
    key = jax.random.key(seed)
    ks = jax.random.split(key, 32)

    def w(k, shape, fan_in):
        return jax.random.normal(k, shape, jnp.float32) * fan_in ** -0.5

    def gain(k, n):
        return 1.0 + 0.05 * jax.random.normal(k, (n,), jnp.float32)

    offs = jax.random.randint(ks[2], (BATCH, 1), 0, 2048, dtype=jnp.int32)
    return {
        "x": jax.random.normal(ks[0], (BATCH, SEQ, D_MODEL), jnp.float32),
        "mem": jax.random.normal(ks[1], (BATCH, MEM_LEN, D_MODEL), jnp.float32),
        "positions": jnp.arange(SEQ, dtype=jnp.int32)[None, :] + offs,
        "norm_mix_pre": gain(ks[3], D_MODEL),
        "w_in": w(ks[4], (D_MODEL, W_IN_COLS), D_MODEL),
        "conv_w": w(ks[5], (CONV_K, CONV_WIDTH), CONV_K),
        "pe_kc": 0.1 * jax.random.normal(ks[6], (CMP_BLOCK, HEAD_DIM), jnp.float32),
        "w1_kc": w(ks[7], (CMP_BLOCK * HEAD_DIM, CMP_HIDDEN), CMP_BLOCK * HEAD_DIM),
        "w2_kc": w(ks[8], (CMP_HIDDEN, HEAD_DIM), CMP_HIDDEN),
        "pe_vc": 0.1 * jax.random.normal(ks[9], (CMP_BLOCK, HEAD_DIM), jnp.float32),
        "w1_vc": w(ks[10], (CMP_BLOCK * HEAD_DIM, CMP_HIDDEN), CMP_BLOCK * HEAD_DIM),
        "w2_vc": w(ks[11], (CMP_HIDDEN, HEAD_DIM), CMP_HIDDEN),
        "norm_conv_out": gain(ks[12], CONV_WIDTH),
        "norm_attn_out": gain(ks[13], ATT_WIDTH),
        "w_out": w(ks[14], (MIX_WIDTH_2, D_MODEL), MIX_WIDTH_2),
        "norm_mix_post": gain(ks[15], D_MODEL),
        "norm_x_pre": gain(ks[16], D_MODEL),
        "norm_mem": gain(ks[17], D_MODEL),
        "w_q_x": w(ks[18], (D_MODEL, D_MODEL), D_MODEL),
        "w_kv_x": w(ks[19], (D_MODEL, 2 * D_MODEL), D_MODEL),
        "w_o_x": w(ks[20], (D_MODEL, D_MODEL), D_MODEL),
        "norm_x_post": gain(ks[21], D_MODEL),
        "norm_ffn_pre": gain(ks[22], D_MODEL),
        "w_gate_up": w(ks[23], (D_MODEL, 2 * D_FF), D_MODEL),
        "w_down": w(ks[24], (D_FF, D_MODEL), D_FF),
        "norm_ffn_post": gain(ks[25], D_MODEL),
    }

def second_block(x, mem, positions, norm_mix_pre, w_in, conv_w, pe_kc, w1_kc, w2_kc, pe_vc, w1_vc, w2_vc,
              norm_conv_out, norm_attn_out, w_out, norm_mix_post, norm_x_pre, norm_mem, w_q_x, w_kv_x,
              w_o_x, norm_x_post, norm_ffn_pre, w_gate_up, w_down, norm_ffn_post):
    b, s, _ = x.shape
    h = x
    for _layer in range(DEPTH_2):
        u = rmsnorm(h, norm_mix_pre)
        proj = u @ w_in
        cuts = np.cumsum([CONV_WIDTH, CONV_WIDTH, CONV_WIDTH, ATT_WIDTH] + [KV_WIDTH] * 6)
        bg, cg, xin, q, kc, vc, ksl, vsl, kw, vw, gl = jnp.split(proj, cuts, axis=-1)
        kv_shape = (b, s, KV_GROUPS, HEAD_DIM)
        y_conv = short_conv_mixer(bg, cg, xin, conv_w)
        y_att = nsa_mixer(q.reshape(b, s, ATT_HEADS, HEAD_DIM), kc.reshape(kv_shape), vc.reshape(kv_shape),
                          ksl.reshape(kv_shape), vsl.reshape(kv_shape), kw.reshape(kv_shape), vw.reshape(kv_shape),
                          jax.nn.sigmoid(gl).reshape(b, s, ATT_HEADS, 3), positions,
                          pe_kc, w1_kc, w2_kc, pe_vc, w1_vc, w2_vc)
        mixed = jnp.concatenate([rmsnorm(y_conv, norm_conv_out), rmsnorm(y_att, norm_attn_out)], axis=-1)
        h = h + rmsnorm(mixed @ w_out, norm_mix_post)

        hn = rmsnorm(h, norm_x_pre)
        mn = rmsnorm(mem, norm_mem)
        qx = (hn @ w_q_x).reshape(b, s, X_HEADS, X_HEAD_DIM)
        kx, vx = jnp.split(mn @ w_kv_x, 2, axis=-1)
        kx = kx.reshape(b, MEM_LEN, X_HEADS, X_HEAD_DIM)
        vx = vx.reshape(b, MEM_LEN, X_HEADS, X_HEAD_DIM)
        sx = jnp.einsum("bshd,bmhd->bhsm", qx, kx).astype(jnp.float32) * X_HEAD_DIM ** -0.5
        px = jax.nn.softmax(sx, axis=-1)
        ox = jnp.einsum("bhsm,bmhd->bshd", px, vx).astype(h.dtype).reshape(b, s, D_MODEL)
        h = h + rmsnorm(ox @ w_o_x, norm_x_post)

        hn = rmsnorm(h, norm_ffn_pre)
        g, up = jnp.split(hn @ w_gate_up, 2, axis=-1)
        h = h + rmsnorm((jax.nn.silu(g) * up) @ w_down, norm_ffn_post)
    return h


def setup_inputs(seed=0):
    out = dict(first_inputs(seed))
    for name, value in second_inputs(seed + 1).items():
        if name != "x":
            out[name + "_2"] = value
    return out


def reference(
    x, ln_in_g, ln_in_b, w_in, qn_g, kn_g, sink, gn_a_g, gn_b_g, w_o, ln1_g, ln1_b, peer_wq,
    peer_keys, peer_u, peer_v, ln2_g, ln2_b, mem_2, positions_2, norm_mix_pre_2, w_in_2,
    conv_w_2, pe_kc_2, w1_kc_2, w2_kc_2, pe_vc_2, w1_vc_2, w2_vc_2, norm_conv_out_2,
    norm_attn_out_2, w_out_2, norm_mix_post_2, norm_x_pre_2, norm_mem_2, w_q_x_2, w_kv_x_2,
    w_o_x_2, norm_x_post_2, norm_ffn_pre_2, w_gate_up_2, w_down_2, norm_ffn_post_2,
):
    x = first_block(
        x, ln_in_g, ln_in_b, w_in, qn_g, kn_g, sink, gn_a_g, gn_b_g, w_o, ln1_g, ln1_b, peer_wq,
        peer_keys, peer_u, peer_v, ln2_g, ln2_b,
    )
    return second_block(
        x, mem_2, positions_2, norm_mix_pre_2, w_in_2, conv_w_2, pe_kc_2, w1_kc_2, w2_kc_2,
        pe_vc_2, w1_vc_2, w2_vc_2, norm_conv_out_2, norm_attn_out_2, w_out_2, norm_mix_post_2,
        norm_x_pre_2, norm_mem_2, w_q_x_2, w_kv_x_2, w_o_x_2, norm_x_post_2, norm_ffn_pre_2,
        w_gate_up_2, w_down_2, norm_ffn_post_2,
    )


_drawn_inputs = setup_inputs


def setup_inputs(seed=0):
    import zlib

    import numpy as np

    out = dict(_drawn_inputs(seed))
    spreads = {}
    factors = {'qn_g': 8.0,
     'kn_g': 7.188,
     'sink': 8.0,
     'gn_a_g': 3.714,
     'gn_b_g': 5.013,
     'pe_kc_2': 7.963}
    for name, (base, spread) in spreads.items():
        noise = np.random.default_rng([zlib.crc32(name.encode()), seed]).standard_normal(out[name].shape)
        drawn = base * np.exp(spread * noise) if base else spread * noise
        out[name] = __import__('jax').numpy.asarray(drawn.astype(out[name].dtype))
    for name, factor in factors.items():
        out[name] = (out[name] * factor).astype(out[name].dtype)
    return out
```

```python
import math

import numpy as np
import concourse.bass as bass
from concourse import mybir
from contextlib import ExitStack

P = 128
D = 1024
S = 256
DEPTH = 2
KB = D // P
TT = S // P
HD = 64
CW = 256
CHUNK = KB * CW
N_IN, N_O, N_WQ = 6, 4, 8
NK = 128
NPAIR = NK // 2
PH, TOPK = 8, 16
N_CONV, N_PROJ2 = 6, 6
P2W = 1304
NCMP = 15
CMPJ = 32
FF = 2816
NFB = FF // P
XH = 4
ALPHA = (2.0 * DEPTH) ** 0.25
NEG = -1e30
ARENA = NK * S
SQ = 0.125
PERM = [0, 4, 1, 5, 2, 6, 3, 7]


def build(nc, A, out):
    F32, U32, I32 = mybir.dt.float32, mybir.dt.uint32, mybir.dt.int32
    ALU, ACT, AX = mybir.AluOpType, mybir.ActivationFunctionType, mybir.AxisListType
    MUL, ADD, SUB, MAX = ALU.mult, ALU.add, ALU.subtract, ALU.max
    ctx = ExitStack()
    with ctx:
        def sb(name, shape, dt=F32):
            return ctx.enter_context(nc.sbuf_tensor(name, shape, dt))

        def sem(name):
            return ctx.enter_context(nc.semaphore(name))

        arena = sb("arena", [P, ARENA])

        def region(off, *shape):
            n = int(np.prod(shape))
            assert off + n <= ARENA
            v = arena[:, off:off + n]
            if len(shape) == 2:
                v = v.rearrange("p (a b) -> p a b", a=shape[0])
            if len(shape) == 3:
                v = v.rearrange("p (a b c) -> p a b c", a=shape[0], b=shape[1])
            return v

        ring = sb("ring", [P, 2, CHUNK])
        h = sb("h", [P, TT, D])
        xT = sb("xT", [P, KB, S])
        gains = sb("gains", [P, 4, D])
        ident = sb("ident", [P, P])
        identa = sb("identa", [P, P])
        iota = sb("iota", [P, P])
        iota16 = sb("iota16", [P, TOPK])
        mhalf = sb("mhalf", [P, 1])
        ones = sb("ones", [P, P])
        qkg = sb("qkg", [P, DEPTH, 2 * HD])
        sinks = sb("sinks", [P, DEPTH, 8])
        ropeA = sb("ropeA", [P, 2, TT, HD])
        stats = sb("stats", [P, TT, 2, 6])
        mv = sb("mv", [P, TT, 2])
        ve = sb("ve", [P, 20])
        rstd = sb("rstd", [P, 20])
        peer_k = sb("peer_k", [P, PH, 2 * NK])
        qTc = sb("qTc", [P, 2, S])
        scc = sb("scc", [P, 4, NK])
        scr = sb("scr", [P, 4, NK])
        s16c = sb("s16c", [P, 4, TOPK])
        i16c = sb("i16c", [P, 4, TOPK], U32)
        s16 = sb("s16", [P, PH, 4 * TOPK])
        i16 = sb("i16", [P, PH, 4 * TOPK])
        cand = peer_k[:, 0:2, :].rearrange("p t (i k) -> p t i k", i=1)[:, :, 0, :]
        candr = peer_k[:, 2:4, :].rearrange("p t (i k) -> p t i k", i=1)[:, :, 0, :]
        oneh = peer_k[:, 4:6, :].rearrange("p a b -> p (a b)").rearrange("p (a b) -> p a b", b=TOPK)
        t16 = sb("t16", [P, TT * TOPK])
        p16 = sb("p16", [P, TT * TOPK], U32)
        pj = sb("pj", [P, 2, TT * TOPK], U32)
        pf = sb("pf", [P, 2, TT * TOPK])
        sel = sb("sel", [P, 3, TT, PH * TOPK])
        selT = sb("selT", [P, 3, S])
        gsm = sb("gsm", [P, TT * PH])
        ohA = xT[:, 0:4, :].rearrange("p a b -> p (a b)").rearrange("p (s n k) -> p s n k", s=2, n=4)
        ohB = xT[:, 4:8, :].rearrange("p a b -> p (a b)").rearrange("p (s n k) -> p s n k", s=2, n=4)
        wst = xT[:, 0:4, :].rearrange("p a b -> p (a b)").rearrange("p (s j n) -> p s j n", s=2, j=2)
        PS = ctx.enter_context(nc.psum_tensor("PS", [P, 8, 512], F32))

        def ps2(s):
            return PS[:, 2 * s:2 * s + 2, :].rearrange("p a b -> p (a b)")

        acc = PS[:, 4:8, :].rearrange("p (t c) n -> p t (c n)", t=TT)

        chunk_in = [sem(f"chunk_in{s}") for s in (0, 1)]
        chunk_free = [sem(f"chunk_free{s}") for s in (0, 1)]
        act_full = [sem(f"act_full{s}") for s in (0, 1)]
        dve_full = [sem(f"dve_full{s}") for s in (0, 1)]
        slot_free = [sem(f"slot_free{s}") for s in (0, 1)]
        src_ready = sem("src_ready")
        var_ready = sem("var_ready")
        rstd_ready = sem("rstd_ready")
        gain_in = [sem(f"gain_in{s}") for s in range(4)]
        gain_free = [sem(f"gain_free{s}") for s in (0, 1)]
        consts_in = [sem(f"consts_in{i}") for i in range(24)]
        consts_dve, consts_pe = sem("consts_dve"), sem("consts_pe")
        keys_in, keys_free = sem("keys_in"), sem("keys_free")
        bias_in, arena_free, arena_free2 = sem("bias_in"), sem("arena_free"), sem("arena_free2")
        shifted_ready = sem("shifted_ready")
        probs_ready = sem("probs_ready")
        sinkarg_ready, sinkexp_ready = sem("sinkarg_ready"), sem("sinkexp_ready")
        vals_ready = sem("vals_ready")
        evac_done = sem("evac_done")
        oneh_ready = sem("oneh_ready")
        wst_ready = [sem(f"wst_ready{s}") for s in (0, 1)]
        wst_used = [sem(f"wst_used{s}") for s in (0, 1)]
        acc_ready = sem("acc_ready")
        h_ready = sem("h_ready")
        gelu_done = sem("gelu_done")
        smarg_ready, smexp_ready = sem("smarg_ready"), sem("smexp_ready")
        mem_in, pos_in = sem("mem_in"), sem("pos_in")
        ang_ready, trig_ready = sem("ang_ready"), sem("trig_ready")
        gate_arg, gate_exp = sem("gate_arg"), sem("gate_exp")
        kb_ready = sem("kb_ready")
        pcT_ready, cmp_exp = sem("pcT_ready"), sem("cmp_exp")
        var2_ready, std2_ready = sem("var2_ready"), sem("std2_ready")
        silu_done, act_used = sem("silu_done"), sem("act_used")
        ffn_ready = sem("ffn_ready")
        out_ready, out_done = sem("out_ready"), sem("out_done")
        x_in = sem("x_in")
        dve_own, act_own, pool_own = sem("dve_own"), sem("act_own"), sem("pool_own")

        proj = region(0, TT, 1536)
        qkr = region(3072, TT, 640)
        tmp1 = region(28672, TT, D)
        tmp2 = region(30720, TT, D)
        qkT = region(8448, 2, 6, S)
        vaug = region(11520, TT, 4, 65)
        biasB = region(12288, TT, 8, S)
        o_all = region(16384, TT, D)
        shf = region(18432, 2, 4, S)
        prb = region(20480, 2, 4, S)
        prT = region(22528, 2, 8, P)
        mx = region(24576, 2, 4)
        den = region(24592, 2, 4)
        snk = region(24608, 2, 4)
        esk = region(24624, 2, 4)
        zT = region(0, 4, S)
        convT = region(1024, 12, S)
        proj2 = region(4096, TT, P2W)
        qkr2 = region(6704, TT, 768)
        kcvT = region(8240, 2, S)
        w2k = region(8752, 2, 2, HD)
        qk2T = region(26560, 6, S)
        causal = region(12288, TT, S)
        cmpbias = region(12800, TT, NCMP)
        cmpmask = region(12830, TT, NCMP)
        hmask = region(12860, 8)
        peT = region(12868, 2, CMPJ)
        convw = region(12932, 4, 4)
        rope2 = region(12948, 2, 3, HD)
        angs = region(13332, 8, 96)
        pos_f = region(14100, 3)
        invf = region(14103, 32)
        gate = region(14135, TT, 24)
        hidT = region(14183, 2, 2, 2 * NCMP)
        hidx = region(14303, 2, 120)
        kcmp = region(14543, 2 * HD)
        kcT = region(9144, 2 * NCMP)
        sc_c = region(14686, TT, 120)
        pr_c = region(14926, TT, 120)
        prT_c = region(15166, TT, P)
        mx_c = region(15422, TT, 8)
        dn_c = region(15438, TT, 8)
        bd = region(15454, 512)
        v120 = region(15966, HD)
        ss = region(16030, S)
        posv = region(16290, 3)
        krow = region(9008, 2 * HD)
        coef = region(9136, 8)
        kblk = region(24640, 2, CMPJ, 2 * NCMP)
        memr = region(0, TT, D)
        memT = region(2048, KB, S)
        qxT = region(4096, KB, S)
        kxT = region(6144, KB, S)
        vx = region(8192, TT, D)
        ffT = region(0, NFB, S)
        sil = region(6144, 2, S)

        block = ctx.enter_context(nc.Block())

        @block.sync
        def _(sp):
            def stream(src, n):
                with sp.Fori(0, n // 2) as i:
                    for s in (0, 1):
                        sp.wait_ge(chunk_free[s], 1)
                        sp.sem_inc(chunk_free[s], -1)
                        sp.dma_start(ring[:, s, :], src(2 * i + s)).then_inc(chunk_in[s], 16)

            def gain(at, *rows):
                sp.wait_ge(gain_free[at], 1)
                sp.sem_inc(gain_free[at], -1)
                for i, g in enumerate(rows):
                    sp.dma_start(gains[:, 2 * at + i, 0:g.shape[-1]],
                                 g.partition_broadcast(P)).then_inc(gain_in[2 * at + i], 16)

            for s in (0, 1):
                sp.sem_inc(chunk_free[s], 1)
            gain(0, A["ln_in_g"], A["ln_in_b"])
            with sp.Fori(0, DEPTH) as l:
                gain(1, A["gn_g"][l])
                stream(lambda c: A["w_in"][l, c], N_IN)
                sp.wait_ge(arena_free, 1)
                sp.sem_inc(arena_free, -1)
                sp.dma_start(biasB[:, :, :, :], A["c_biasB"]).then_inc(bias_in, 16)
                sp.wait_ge(keys_free, 1)
                sp.sem_inc(keys_free, -1)
                sp.dma_start(peer_k[:, :, :], A["peer_keys"][l]).then_inc(keys_in, 16)
                stream(lambda c: A["w_o"][l, c], N_O)
                gain(1, A["ln1_g"][l], A["ln1_b"][l])
                stream(lambda c: A["peer_wq"][l, c], N_WQ)
                gain(0, A["ln2_g"][l], A["ln2_b"][l])
                stream(lambda c: A["peer_u"][l, c], NPAIR)
                stream(lambda c: A["peer_v"][l, c], NPAIR)
            gain(1, A["norm_mix_pre_2"])
            stream(lambda c: A["w_in_2"][c], N_CONV + N_PROJ2)
            gain(0, A["norm_attn_out_2"])
            stream(lambda c: A["w1_2"][c], 8)
            gain(1, A["norm_mix_post_2"])
            stream(lambda c: A["w_out_2"][c], 4)
            gain(0, A["norm_x_pre_2"])
            stream(lambda c: A["w_q_x_2"][c], 4)
            gain(1, A["norm_mem_2"])
            stream(lambda c: A["w_kv_x_2"][c], 8)
            gain(0, A["norm_x_post_2"])
            stream(lambda c: A["w_o_x_2"][c], 4)
            gain(1, A["norm_ffn_pre_2"])
            stream(lambda c: A["w_gate_up_2"][c], NFB)
            gain(0, A["norm_ffn_post_2"])
            stream(lambda c: A["w_down_2"][c], NFB // 2 - 1)
            sp.wait_ge(chunk_free[0], 1)
            sp.sem_inc(chunk_free[0], -1)
            sp.dma_start(ring[:, 0, :], A["w_down_2"][NFB // 2 - 1]).then_inc(chunk_in[0], 16)
            sp.wait_ge(out_ready, 1)
            sp.sem_inc(out_ready, -1)
            sp.dma_start(out.rearrange("b (t p) d -> p (b t) d", p=P), h[:, :, :]).then_inc(out_done, 16)
            sp.wait_ge(out_done, 16)

        @block.gpsimd
        def _(pool):
            def own(ins):
                ins.then_inc(pool_own, 1)
                pool.wait_ge(pool_own, 1)
                pool.sem_inc(pool_own, -1)

            own(pool.memset(mhalf[:, :], -0.5))
            own(pool.memset(ones[:, :], 1.0))
            own(pool.memset(ident[:, :], 0.0))
            own(pool.memset(identa[:, :], 0.0))
            for m, v in ((ident, 1.0), (identa, ALPHA)):
                own(pool.affine_select(out=m[:, :], in_=m[:, :], compare_op=ALU.not_equal, fill=v,
                                       base=0, pattern=[[-1, P]], channel_multiplier=1))
            own(pool.iota(iota[:, :], pattern=[[1, P]], base=0, channel_multiplier=0,
                          allow_small_or_imprecise_dtypes=True))
            own(pool.iota(iota16[:, :], pattern=[[1, TOPK]], base=0, channel_multiplier=0,
                          allow_small_or_imprecise_dtypes=True))
            pool.sem_inc(consts_dve, 1)
            pool.sem_inc(consts_pe, 1)

            def power(n):
                pool.wait_ge(var_ready, 1)
                pool.sem_inc(var_ready, -1)
                pool.tensor_tensor(rstd[:, 0:n], ve[:, 0:n], mhalf[:, :].to_broadcast([P, n]),
                                   ALU.pow).then_inc(rstd_ready, 1)

            power(TT)
            with pool.Fori(0, DEPTH):
                power(20)
                power(16)
                power(16)
                power(TT)
                power(TT)
            pool.wait_ge(arena_free2, 1)
            pool.sem_inc(arena_free2, -1)
            for i, (dst, src) in enumerate((
                    (causal[:, :, :], A["c_causal"]), (cmpbias[:, :, :], A["c_cmpbias"]),
                    (cmpmask[:, :, :], A["c_cmpmask"]), (hmask[:, :], A["c_hmask"]),
                    (peT[:, :, :], A["pe_2"]), (convw[:, :, :], A["conv_2"]),
                    (w2k[:, :, :, :], A["w2_2"]), (invf[:, :], A["c_invf"].partition_broadcast(P)))):
                pool.dma_start(dst, src).then_inc(consts_in[i], 16)
            pool.dma_start(pos_f[:, :].bitcast(I32), A["pos_2"]).then_inc(consts_in[8], 16)
            power(TT)
            power(TT)
            power(TT)
            power(TT)
            pool.wait_ge(arena_free2, 1)
            pool.sem_inc(arena_free2, -1)
            pool.dma_start(memr[:, :, :], A["mem_2"][0].rearrange("(t p) d -> p t d", p=P)).then_inc(mem_in, 16)
            power(TT)
            power(TT)
            power(TT)
            power(TT)

        @block.tensor
        def _(pe):
            def evacuated():
                for s in (0, 1):
                    pe.wait_ge(slot_free[s], 1)

            def transposes(s, full, pairs):
                pe.wait_ge(slot_free[s], 1)
                pe.sem_inc(slot_free[s], -1)
                for dst, src in pairs:
                    n = src.shape[0]
                    last = pe.transpose(dst, src, ident[0:n, 0:n])
                last.then_inc(full[s], 1)

            def to_xT(src):
                pe.wait_ge(src_ready, 1)
                pe.sem_inc(src_ready, -1)
                for t in range(TT):
                    transposes(t, act_full, [(ps2(t)[:, k * P:(k + 1) * P], src[:, t, k * P:(k + 1) * P])
                                             for k in range(KB)])
                evacuated()

            def rows_by_chunk(s, left, full, width=CW):
                pe.wait_ge(chunk_in[s], 16)
                pe.sem_inc(chunk_in[s], -16)
                pe.wait_ge(slot_free[s], 1)
                pe.sem_inc(slot_free[s], -1)
                for t in range(TT):
                    for k in range(KB):
                        last = pe.matmul(PS[:, 2 * s, t * CW:t * CW + width], left[:, k, t * P:(t + 1) * P],
                                         ring[:, s, k * CW:k * CW + width], start=k == 0, stop=k == KB - 1)
                last.then_inc(full[s], 1)

            def chunk_by_cols(s, right, full):
                pe.wait_ge(chunk_in[s], 16)
                pe.sem_inc(chunk_in[s], -16)
                pe.wait_ge(slot_free[s], 1)
                pe.sem_inc(slot_free[s], -1)
                for b in range(2):
                    for k in range(KB):
                        last = pe.matmul(PS[:, 2 * s, b * S:(b + 1) * S],
                                         ring[:, s, k * CW + b * P:k * CW + (b + 1) * P],
                                         right[:, k, :], start=k == 0, stop=k == KB - 1)
                last.then_inc(full[s], 1)

            def loop2(n, f, *a):
                with pe.Fori(0, n // 2):
                    for s in (0, 1):
                        f(s, *a)

            def attention(units, score, sums=None, value=None):
                n = [0]

                def slot():
                    n[0] += 1
                    return (n[0] - 1) % 2

                def scores(u):
                    s = slot()
                    pe.wait_ge(slot_free[s], 1)
                    pe.sem_inc(slot_free[s], -1)
                    for r in range(4):
                        prods = score(u, r)
                        for i, (a, b) in enumerate(prods):
                            last = pe.matmul(ps2(s)[:, r * S:(r + 1) * S], a, b, start=i == 0,
                                             stop=i == len(prods) - 1)
                    last.then_inc(dve_full[s], 1)

                scores(0)
                for u in range(units):
                    if u + 1 < units:
                        scores(u + 1)
                    pe.wait_ge(probs_ready, 1)
                    pe.sem_inc(probs_ready, -1)
                    s = slot()
                    transposes(s, act_full, [(ps2(s)[:, i * P:(i + 1) * P],
                                              prb[:, u % 2, i // 2, (i % 2) * P:(i % 2 + 1) * P])
                                             for i in range(8)])
                    pe.wait_ge(slot_free[s], 1)
                    s = slot()
                    pe.wait_ge(slot_free[s], 1)
                    pe.sem_inc(slot_free[s], -1)
                    for r in range(4):
                        for o, v in value(u, s, r):
                            for st in range(TT):
                                last = pe.matmul(o, prT[:, u % 2, 2 * r + st, :], v(st), start=st == 0,
                                                 stop=st == TT - 1)
                    last.then_inc(dve_full[s], 1)

            pe.wait_ge(consts_pe, 1)
            pe.sem_inc(consts_pe, -1)
            with pe.Fori(0, DEPTH):
                to_xT(h)
                loop2(N_IN, rows_by_chunk, xT, dve_full)
                for ab in (1, 0):
                    pe.wait_ge(src_ready, 1)
                    pe.sem_inc(src_ready, -1)
                    for t in range(TT):
                        src = proj[:, t, 768:1408] if ab else qkr[:, t, :]
                        transposes(t, act_full, [(ps2(t)[:, j * P:(j + 1) * P], src[:, j * P:(j + 1) * P])
                                                 for j in range(5)])
                evacuated()
                pe.wait_ge(vals_ready, 1)
                pe.sem_inc(vals_ready, -1)

                def score(u, r):
                    ab, g, t = u // 4, u // 2 % 2, u % 2
                    rows = slice(HD * g, HD * g + HD)
                    return [(qkT[rows, ab, r, t * P:(t + 1) * P], qkT[rows, ab, 4, :])]

                def value(u, s, r):
                    return [(ps2(s)[:, r * 65:(r + 1) * 65], lambda st: vaug[:, st, u // 2, :])]

                attention(8, score, value=value)
                to_xT(o_all)
                loop2(N_O, rows_by_chunk, xT, dve_full)
                to_xT(h)
                pe.wait_ge(keys_in, 16)
                with pe.Fori(0, N_WQ // 2) as i:
                    for s in (0, 1):
                        pe.wait_ge(chunk_in[s], 16)
                        pe.sem_inc(chunk_in[s], -16)
                        pe.wait_ge(slot_free[0], 1)
                        pe.sem_inc(slot_free[0], -1)
                        for b in range(2):
                            for k in range(KB):
                                last = pe.matmul(PS[:, 0, b * S:(b + 1) * S],
                                                 ring[:, s, k * CW + b * P:k * CW + (b + 1) * P],
                                                 xT[:, k, :], start=k == 0, stop=k == KB - 1)
                        last.then_inc(act_full[0], 1)
                        pe.wait_ge(slot_free[0], 1)
                        pe.wait_ge(slot_free[1], 1)
                        pe.sem_inc(slot_free[1], -1)
                        for t in range(TT):
                            for p in range(2):
                                last = pe.matmul(PS[:, 2, (2 * t + p) * NK:(2 * t + p + 1) * NK],
                                                 qTc[:, p, t * P:(t + 1) * P],
                                                 peer_k[:, 2 * i + s, p * NK:(p + 1) * NK], start=True, stop=True)
                        last.then_inc(dve_full[1], 1)
                pe.wait_ge(keys_in, 16)
                pe.sem_inc(keys_in, -16)
                def experts(s):
                    pe.wait_ge(chunk_in[s], 16)
                    pe.sem_inc(chunk_in[s], -16)
                    pe.wait_ge(slot_free[s], 1)
                    pe.sem_inc(slot_free[s], -1)
                    for j in range(2):
                        for k in range(KB):
                            last = pe.matmul(PS[:, 2 * s, j * S:(j + 1) * S],
                                             ring[:, s, (j * KB + k) * P:(j * KB + k + 1) * P],
                                             xT[:, k, :], start=k == 0, stop=k == KB - 1)
                    last.then_inc(act_full[s], 1)

                loop2(NPAIR, experts)
                pe.wait_ge(src_ready, 1)
                pe.sem_inc(src_ready, -1)
                for t in range(TT):
                    transposes(t, dve_full, [(ps2(t)[:, i * P:(i + 1) * P], sel[:, i, t, :]) for i in range(3)])
                with pe.Fori(0, S // 8):
                    for s in (0, 1):
                        pe.wait_ge(oneh_ready, 1)
                        pe.sem_inc(oneh_ready, -1)
                        pe.wait_ge(slot_free[s], 1)
                        pe.sem_inc(slot_free[s], -1)
                        for n in range(4):
                            last = pe.matmul(PS[:, 2 * s, n * P:(n + 1) * P], ohA[:, s, n, :], ohB[:, s, n, :],
                                             start=True, stop=True)
                        last.then_inc(dve_full[s], 1)
                for t in range(TT):
                    for c in range(2):
                        pe.matmul(acc[:, t, c * 512:(c + 1) * 512], identa[:, :], h[:, t, c * 512:(c + 1) * 512],
                                  start=True, stop=False)
                def weigh(s, end=False):
                    pe.wait_ge(chunk_in[s], 16)
                    pe.sem_inc(chunk_in[s], -16)
                    pe.wait_ge(wst_ready[s], 1)
                    pe.sem_inc(wst_ready[s], -1)
                    for j in range(2):
                        for t in range(TT):
                            for c in range(2):
                                last = pe.matmul(acc[:, t, c * 512:(c + 1) * 512],
                                                 wst[:, s, j, t * P:(t + 1) * P],
                                                 ring[:, s, j * D + c * 512:j * D + (c + 1) * 512],
                                                 start=False, stop=end and j == 1)
                    last.then_inc(wst_used[s], 1)

                with pe.Fori(0, NPAIR // 2 - 1):
                    for s in (0, 1):
                        weigh(s)
                weigh(0)
                weigh(1, True)
                pe.drain().then_inc(acc_ready, 1)

            to_xT(tmp1)
            loop2(N_CONV, chunk_by_cols, xT, dve_full)
            loop2(N_PROJ2 - 2, rows_by_chunk, xT, dve_full)
            rows_by_chunk(0, xT, dve_full)
            rows_by_chunk(1, xT, dve_full, 24)
            pe.wait_ge(src_ready, 1)
            pe.sem_inc(src_ready, -1)
            for t in range(TT):
                transposes(t, act_full, [(ps2(t)[:, i * P:(i + 1) * P], proj2[:, t, 512 + i * P:512 + (i + 1) * P])
                                         for i in range(2)])
            for kv in range(2):
                pe.wait_ge(kb_ready, 1)
                pe.sem_inc(kb_ready, -1)
                pe.wait_ge(slot_free[kv], 1)
                pe.sem_inc(slot_free[kv], -1)
                for c in range(4):
                    s = c % 2
                    pe.wait_ge(chunk_in[s], 16)
                    pe.sem_inc(chunk_in[s], -16)
                    for hb in range(2):
                        for j in range(8):
                            last = pe.matmul(PS[:, 2 * kv + hb, 0:2 * NCMP],
                                             ring[:, s, j * CW + hb * P:j * CW + (hb + 1) * P],
                                             kblk[:, kv, 8 * c + j, :], start=c + j == 0, stop=c + j == 10)
                    if c < 3:
                        last.then_inc(chunk_free[s], 1)
                last.then_inc(act_full[kv], 1)
            pe.wait_ge(src_ready, 1)
            pe.sem_inc(src_ready, -1)
            evacuated()
            for t in range(TT):
                transposes(t, act_full, [(ps2(t)[:, j * P:(j + 1) * P], qkr2[:, t, j * P:(j + 1) * P])
                                         for j in range(6)])
            pe.wait_ge(kb_ready, 1)
            pe.sem_inc(kb_ready, -1)
            pe.wait_ge(slot_free[0], 1)
            pe.sem_inc(slot_free[0], -1)
            for g in range(2):
                for hb in range(2):
                    last = pe.matmul(PS[0:NCMP, 0, g * HD:(g + 1) * HD], hidT[:, 0, hb, g * NCMP:(g + 1) * NCMP],
                                     w2k[:, 0, hb, :], start=hb == 0, stop=hb == 1)
            last.then_inc(dve_full[0], 1)
            pe.wait_ge(slot_free[1], 1)
            pe.sem_inc(slot_free[1], -1)
            for hb in range(2):
                last = pe.matmul(PS[0:120, 2, 0:HD], hidx[:, hb, :], w2k[:, 1, hb, :], start=hb == 0, stop=hb == 1)
            last.then_inc(dve_full[1], 1)
            pe.wait_ge(src_ready, 1)
            pe.sem_inc(src_ready, -1)
            transposes(0, act_full, [(PS[:, 0, 0:NCMP], kcmp[0:NCMP, :])])
            pe.wait_ge(slot_free[1], 1)
            pe.sem_inc(slot_free[1], -1)
            pe.wait_ge(slot_free[0], 1)
            for t in range(TT):
                o = PS[:, 2, t * 120:(t + 1) * 120].rearrange("p (g r n) -> p g r n", g=2, r=4)
                for r in range(4):
                    last = pe.matmul(o[:, :, r, :], qk2T[:, r, t * P:(t + 1) * P], kcT[:, :],
                                     start=True, stop=True)
            last.then_inc(dve_full[1], 1)
            pe.wait_ge(pcT_ready, 1)
            pe.sem_inc(pcT_ready, -1)
            transposes(0, act_full, [(PS[0:120, 0, t * P:(t + 1) * P], pr_c[:, t, :]) for t in range(TT)])
            pe.wait_ge(slot_free[0], 1)
            for t, s in ((0, 1), (1, 0)):
                pe.wait_ge(slot_free[s], 1)
                pe.sem_inc(slot_free[s], -1)
                pe.matmul(PS[:, 2 * s, :], prT_c[0:120, t, :], bd[0:120, :], start=True, stop=True)
                pe.matmul(PS[:, 2 * s + 1, 0:8], prT_c[0:120, t, :], hmask[0:120, :], start=True,
                          stop=True).then_inc(dve_full[s], 1)
            pe.wait_ge(src_ready, 1)
            pe.sem_inc(src_ready, -1)
            pe.wait_ge(slot_free[1], 1)
            pe.sem_inc(slot_free[1], -1)
            for b in range(4):
                last = pe.matmul(PS[:, 2, 0:S], ones[:, :], convT[:, b, :], start=b == 0, stop=b == 3)
            last.then_inc(dve_full[1], 1)

            def score2(u, r):
                w, g, t = u // 4, u // 2 % 2, u % 2
                rows = slice(HD * g, HD * g + HD)
                return [(qk2T[rows, r, t * P:(t + 1) * P], qk2T[rows, 4 + w, :])]

            pe.wait_ge(vals_ready, 1)
            pe.sem_inc(vals_ready, -1)
            attention(8, score2, value=lambda u, s, r: [(ps2(s)[:, r * 65:(r + 1) * 65],
                                                         lambda st: vaug[:, st, u // 2, :])])
            pe.wait_ge(src_ready, 1)
            pe.sem_inc(src_ready, -1)
            for t in range(TT):
                transposes(t, act_full, [(ps2(t)[:, k * P:(k + 1) * P], o_all[:, t, k * P:(k + 1) * P])
                                         for k in range(4)])
            evacuated()
            loop2(4, rows_by_chunk, xT, dve_full)
            to_xT(tmp1)
            loop2(4, chunk_by_cols, xT, act_full)
            to_xT(o_all)
            loop2(4, chunk_by_cols, memT, act_full)
            loop2(4, rows_by_chunk, memT, act_full)
            evacuated()

            def score3(t, r):
                return [(qxT[:, 2 * r + b, t * P:(t + 1) * P], kxT[:, 2 * r + b, :]) for b in range(2)]

            def value3(t, s, r):
                return [(PS[:, 4 + t, r:r + 1], lambda st: ones[:, 0:1]),
                        (ps2(s)[:, r * S:(r + 1) * S], lambda st: vx[:, st, r * S:(r + 1) * S])]

            attention(TT, score3, value=value3)
            to_xT(o_all)
            loop2(4, rows_by_chunk, xT, dve_full)
            to_xT(tmp1)
            loop2(NFB, chunk_by_cols, xT, act_full)
            pe.wait_ge(ffn_ready, 1)
            pe.sem_inc(ffn_ready, -1)
            for c in range(NFB // 2):
                s = c % 2
                pe.wait_ge(chunk_in[s], 16)
                pe.sem_inc(chunk_in[s], -16)
                for b in range(2):
                    for t in range(TT):
                        for q in range(2):
                            last = pe.matmul(acc[:, t, q * 512:(q + 1) * 512], ffT[:, 2 * c + b, t * P:(t + 1) * P],
                                             ring[:, s, b * D + q * 512:b * D + (q + 1) * 512],
                                             start=c + b == 0, stop=c + b == NFB // 2, skip_group_check=True)
                if c == NFB // 2 - 1:
                    last.then_inc(acc_ready, 1)
                else:
                    last.then_inc(chunk_free[s], 1)

        @block.scalar
        def _(act):
            def evac(s, dst, src, free_chunk=False):
                act.wait_ge(act_full[s], 1)
                act.sem_inc(act_full[s], -1)
                if free_chunk:
                    act.sem_inc(chunk_free[s], 1)
                act.activation(dst, src, ACT.Copy).then_inc(slot_free[s], 1)

            def to_xT(dst=xT, nk=KB, k0=0):
                for t in range(TT):
                    evac(t, dst[:, k0:k0 + nk, t * P:(t + 1) * P],
                         ps2(t)[:, 0:nk * P].rearrange("p (k n) -> p k n", k=nk))

            def attention(units, scale, sink=lambda u: False):
                n = [0]

                def slot():
                    n[0] += 1
                    return (n[0] - 1) % 2

                slot()
                for u in range(units):
                    if u + 1 < units:
                        slot()
                    act.wait_ge(shifted_ready, 1)
                    act.sem_inc(shifted_ready, -1)
                    act.activation(prb[:, u % 2, :, :], shf[:, u % 2, :, :], ACT.Exp,
                                   scale=scale(u)).then_inc(probs_ready, 1)
                    if sink(u):
                        act.wait_ge(sinkarg_ready, 1)
                        act.sem_inc(sinkarg_ready, -1)
                        act.activation(esk[:, u % 2, :], snk[:, u % 2, :], ACT.Exp).then_inc(sinkexp_ready, 1)
                    s = slot()
                    evac(s, prT[:, u % 2, :, :], ps2(s).rearrange("p (a b) -> p a b", a=8))
                    slot()

            act.dma_start(h[:, :, :], A["x"][0].rearrange("(t p) d -> p t d", p=P)).then_inc(x_in, 16)
            act.dma_start(qkg[:, :, :], A["qk_g"].partition_broadcast(P)).then_inc(consts_in[20], 16)
            act.dma_start(sinks[:, :, :], A["sink"].partition_broadcast(P)).then_inc(consts_in[21], 16)
            act.dma_start(ropeA[:, :, :, :], A["c_ropeA"]).then_inc(consts_in[22], 16)
            with act.Fori(0, DEPTH):
                to_xT()
                for ab in (1, 0):
                    for t in range(TT):
                        evac(t, qkT[:, ab, 0:5, t * P:(t + 1) * P],
                             ps2(t)[:, 0:640].rearrange("p (k n) -> p k n", k=5))
                attention(8, lambda u: SQ if u < 4 else 1.0, lambda u: u >= 4)
                to_xT()
                to_xT()
                with act.Fori(0, N_WQ // 2):
                    for s in (0, 1):
                        act.wait_ge(act_full[0], 1)
                        act.sem_inc(act_full[0], -1)
                        act.sem_inc(chunk_free[s], 1)
                        act.activation(qTc[:, :, :], PS[:, 0, :].rearrange("p (b n) -> p b n", b=2),
                                       ACT.Copy).then_inc(slot_free[0], 1)
                with act.Fori(0, NPAIR // 2) as i:
                    for s in (0, 1):
                        act.wait_ge(act_full[s], 1)
                        act.sem_inc(act_full[s], -1)
                        act.sem_inc(chunk_free[s], 1)
                        act.activation(arena[:, bass.ts(2 * i + s, 512)], PS[:, 2 * s, :],
                                       ACT.Gelu).then_inc(slot_free[s], 1)
                act.drain().then_inc(gelu_done, 1)
                act.wait_ge(smarg_ready, 1)
                act.sem_inc(smarg_ready, -1)
                act.activation(sel[:, 2, :, :], sel[:, 2, :, :], ACT.Exp).then_inc(smexp_ready, 1)
            to_xT()
            act.wait_ge(ang_ready, 1)
            act.sem_inc(ang_ready, -1)
            act.activation(angs[:, 6, :], angs[:, 2, :], ACT.Sin)
            act.activation(angs[:, 7, :], angs[:, 3, :], ACT.Sin).then_inc(trig_ready, 1)
            act.wait_ge(gate_arg, 1)
            act.sem_inc(gate_arg, -1)
            act.activation(gate[:, :, :], gate[:, :, :], ACT.Exp, scale=-1.0).then_inc(gate_exp, 1)
            for t in range(TT):
                evac(t, kcvT[:, :, t * P:(t + 1) * P], ps2(t)[:, 0:2 * P].rearrange("p (k n) -> p k n", k=2))
            act.drain().then_inc(evac_done, 1)
            for kv in range(2):
                act.wait_ge(act_full[kv], 1)
                act.sem_inc(act_full[kv], -1)
                act.sem_inc(chunk_free[1], 1)
                act.activation(hidT[:, kv, :, :], PS[:, 2 * kv:2 * kv + 2, 0:2 * NCMP],
                               ACT.Silu).then_inc(slot_free[kv], 1)
            act.drain().then_inc(evac_done, 1)
            for t in range(TT):
                evac(t, qk2T[:, :, t * P:(t + 1) * P], ps2(t)[:, 0:768].rearrange("p (k n) -> p k n", k=6))
            act.wait_ge(act_full[0], 1)
            act.sem_inc(act_full[0], -1)
            act.activation(kcT[0:HD, 0:NCMP], PS[0:HD, 0, 0:NCMP], ACT.Copy)
            act.activation(kcT[HD:P, NCMP:2 * NCMP], PS[HD:P, 0, 0:NCMP], ACT.Copy).then_inc(slot_free[0], 1)
            act.wait_ge(shifted_ready, 1)
            act.sem_inc(shifted_ready, -1)
            act.activation(pr_c[:, :, :], sc_c[:, :, :], ACT.Exp).then_inc(cmp_exp, 1)
            evac(0, prT_c[0:120, :, :], PS[0:120, 0, 0:2 * P].rearrange("p (t n) -> p t n", t=TT))
            act.wait_ge(var2_ready, 1)
            act.sem_inc(var2_ready, -1)
            act.activation(ss[:, :], ss[:, :], ACT.Sqrt).then_inc(std2_ready, 1)
            attention(8, lambda u: 1.0)
            to_xT(nk=4, k0=4)
            to_xT()
            with act.Fori(0, 2) as i:
                for s in (0, 1):
                    evac(s, qxT[:, bass.ds(4 * i + 2 * s, 2), :],
                         PS[:, 2 * s, :].rearrange("p (b n) -> p b n", b=2), True)
            to_xT(memT)
            with act.Fori(0, 2) as i:
                for s in (0, 1):
                    evac(s, kxT[:, bass.ds(4 * i + 2 * s, 2), :],
                         PS[:, 2 * s, :].rearrange("p (b n) -> p b n", b=2), True)
            with act.Fori(0, 2) as i:
                for s in (0, 1):
                    evac(s, vx[:, :, bass.ds(512 * i + 256 * s, 256)],
                         PS[:, 2 * s, :].rearrange("p (b n) -> p b n", b=2), True)
            attention(TT, lambda u: 1.0 / 16)
            to_xT()
            to_xT()
            with act.Fori(0, NFB // 2) as i:
                for s in (0, 1):
                    act.wait_ge(act_full[s], 1)
                    act.sem_inc(act_full[s], -1)
                    act.sem_inc(chunk_free[s], 1)
                    act.wait_ge(act_used, 1)
                    act.sem_inc(act_used, -1)
                    act.activation(sil[:, s, :], PS[:, 2 * s, 0:S], ACT.Silu).then_inc(silu_done, 1)

        @block.vector
        def _(dve):
            def own(ins):
                ins.then_inc(dve_own, 1)
                dve.wait_ge(dve_own, 1)
                dve.sem_inc(dve_own, -1)

            def bc(ap, *shape):
                return ap.to_broadcast([P, *shape])

            def power(n, scale, eps, sums):
                dve.tensor_scalar(ve[:, 0:n], sums, scale, eps, MUL, ADD).then_inc(var_ready, 1)
                dve.wait_ge(rstd_ready, 1)
                dve.sem_inc(rstd_ready, -1)

            def layer_norm(src, dst, at):
                for t in range(TT):
                    for c in range(2):
                        dve.bn_stats(stats[:, t, c, :], src[:, t, c * 512:(c + 1) * 512])
                own(dve.engine_nop())
                for t in range(TT):
                    dve.bn_aggr(mv[:, t, :], stats[:, t, :, :])
                own(dve.engine_nop())
                power(TT, 1.0, 1e-5, mv[:, :, 1])
                for t in range(TT):
                    dve.tensor_scalar(tmp2[:, t, :], src[:, t, :], mv[:, t, 0:1], rstd[:, t:t + 1], SUB, MUL)
                dve.wait_ge(gain_in[2 * at], 16)
                dve.sem_inc(gain_in[2 * at], -16)
                dve.wait_ge(gain_in[2 * at + 1], 16)
                dve.sem_inc(gain_in[2 * at + 1], -16)
                own(dve.engine_nop())
                own(dve.tensor_tensor(tmp2[:, :, :], tmp2[:, :, :], bc(gains[:, 2 * at, :].unsqueeze(1), TT, D), MUL))
                own(dve.tensor_tensor(dst[:, :, :], tmp2[:, :, :], bc(gains[:, 2 * at + 1, :].unsqueeze(1), TT, D),
                                      ADD))
                dve.sem_inc(gain_free[at], 1)

            def rms_norm(src, dst, at, width=D):
                for t in range(TT):
                    dve.tensor_tensor_reduce(out=tmp2[:, t, 0:width], in0=src[:, t, 0:width], in1=src[:, t, 0:width],
                                             scale=1.0, scalar=0.0, op0=MUL, op1=ADD, accum_out=mv[:, t, 0:1])
                own(dve.engine_nop())
                power(TT, 1.0 / width, 1e-6, mv[:, :, 0])
                dve.wait_ge(gain_in[2 * at], 16)
                dve.sem_inc(gain_in[2 * at], -16)
                for t in range(TT):
                    dve.scalar_tensor_tensor(dst[:, t, 0:width], src[:, t, 0:width], rstd[:, t:t + 1],
                                             gains[:, 2 * at, 0:width], MUL, MUL)
                own(dve.engine_nop())
                dve.sem_inc(gain_free[at], 1)

            def residual_rms(src, at):
                rms_norm(src, tmp1, at)
                own(dve.tensor_tensor(h[:, :, :], h[:, :, :], tmp1[:, :, :], ADD))

            def take_rows(s):
                dve.wait_ge(dve_full[s], 1)
                dve.sem_inc(dve_full[s], -1)
                dve.sem_inc(chunk_free[s], 1)

            def rope(x, y, cos, sin, a, f, t1, t2):
                n, nh = x.shape[0], x.shape[1]
                dve.tensor_tensor(t1, x, cos.unsqueeze(1).to_broadcast([n, nh, HD]), MUL)
                xs = x.rearrange("p h (a b f) -> p h a b f", a=a, b=2)
                ys = t2.rearrange("p h (a b f) -> p h a b f", a=a, b=2)
                sn = sin.rearrange("p (a b f) -> p a b f", a=a, b=2)
                for b in range(2):
                    dve.tensor_tensor(ys[:, :, :, b, :], xs[:, :, :, 1 - b, :],
                                      sn[:, :, b, :].unsqueeze(1).to_broadcast([n, nh, a, f]), MUL)
                own(dve.engine_nop())
                dve.tensor_tensor(y, t1, t2, ADD)

            def attention(units, first, finish):
                n = [0]

                def slot():
                    n[0] += 1
                    return (n[0] - 1) % 2

                def scores(u):
                    s = slot()
                    dve.wait_ge(dve_full[s], 1)
                    dve.sem_inc(dve_full[s], -1)
                    first(u, s)

                scores(0)
                for u in range(units):
                    if u + 1 < units:
                        scores(u + 1)
                    slot()
                    s = slot()
                    dve.wait_ge(dve_full[s], 1)
                    dve.sem_inc(dve_full[s], -1)
                    finish(u, s)

            def shift(u, s, biased=None, scale=1.0, sink=None):
                b = u % 2
                sc = ps2(s).rearrange("p (r n) -> p r n", r=4)
                if biased is None:
                    own(dve.tensor_reduce(mx[:, b, :], sc, AX.X, MAX))
                    own(dve.tensor_tensor(shf[:, b, :, :], sc, bc(mx[:, b, :].unsqueeze(2), 4, S), SUB))
                    dve.sem_inc(slot_free[s], 1)
                    dve.sem_inc(shifted_ready, 1)
                    return
                own(dve.scalar_tensor_tensor(shf[:, b, :, :], sc, scale, biased, MUL, ADD))
                dve.sem_inc(slot_free[s], 1)
                own(dve.tensor_reduce(mx[:, b, :], shf[:, b, :, :], AX.X, MAX))
                if sink is not None:
                    own(dve.tensor_tensor(mx[:, b, :], mx[:, b, :], sink, MAX))
                dve.tensor_tensor(shf[:, b, :, :], shf[:, b, :, :], bc(mx[:, b, :].unsqueeze(2), 4, S),
                                  SUB).then_inc(shifted_ready, 1)
                if sink is not None:
                    dve.tensor_tensor(snk[:, b, :], sink, mx[:, b, :], SUB).then_inc(sinkarg_ready, 1)

            dve.wait_ge(consts_dve, 1)
            dve.sem_inc(consts_dve, -1)
            for s in (0, 1):
                dve.sem_inc(slot_free[s], 1)
            for s in (0, 1):
                dve.sem_inc(gain_free[s], 1)
            dve.sem_inc(keys_free, 1)
            dve.wait_ge(x_in, 16)
            dve.sem_inc(x_in, -16)
            layer_norm(h, h, 0)
            for i in (20, 21, 22):
                dve.wait_ge(consts_in[i], 16)
                dve.sem_inc(consts_in[i], -16)
            with dve.Fori(0, DEPTH) as l:
                dve.sem_inc(src_ready, 1)
                dve.sem_inc(arena_free, 1)
                with dve.Fori(0, N_IN // 2) as i:
                    for s in (0, 1):
                        take_rows(s)
                        dve.tensor_copy(proj[:, :, bass.ds(512 * i + 256 * s, 256)],
                                        PS[:, 2 * s, :].rearrange("p (t n) -> p t n", t=TT)
                                        ).then_inc(slot_free[s], 1)
                own(dve.engine_nop())
                dve.sem_inc(src_ready, 1)
                qk = proj[:, :, 0:640]
                sq = tmp1[:, :, 0:640]
                own(dve.tensor_tensor(sq, qk, qk, MUL))
                own(dve.tensor_reduce(ve[:, 0:20].rearrange("p (t h) -> p t h", t=TT),
                                      sq.rearrange("p t (h d) -> p t h d", d=HD), AX.X, ADD))
                power(20, 1.0 / HD, 1e-6, ve[:, 0:20])
                own(dve.tensor_copy(scr[:, 0, :], qkg[:, l, :]))
                own(dve.tensor_copy(scr[:, 1, 0:8], sinks[:, l, :]))
                for t in range(TT):
                    x = qk[:, t, :].rearrange("p (h d) -> p h d", d=HD)
                    own(dve.tensor_tensor(x, x, bc(rstd[:, 10 * t:10 * t + 10].unsqueeze(2), 10, HD), MUL))
                    dve.tensor_tensor(x[:, 0:8, :], x[:, 0:8, :], bc(scr[:, 0, 0:HD].unsqueeze(1), 8, HD), MUL)
                    own(dve.tensor_tensor(x[:, 8:10, :], x[:, 8:10, :],
                                          bc(scr[:, 0, HD:2 * HD].unsqueeze(1), 2, HD), MUL))
                    rope(x, qkr[:, t, :].rearrange("p (h d) -> p h d", d=HD), ropeA[:, 0, t, :], ropeA[:, 1, t, :],
                         2, 16, tmp1[:, t, 0:640].rearrange("p (h d) -> p h d", d=HD),
                         tmp2[:, t, 0:640].rearrange("p (h d) -> p h d", d=HD))
                own(dve.engine_nop())
                dve.sem_inc(src_ready, 1)
                for ab in range(2):
                    at = 640 if ab == 0 else 1408
                    dve.tensor_copy(vaug[:, :, 2 * ab:2 * ab + 2, 0:HD],
                                    proj[:, :, at:at + 128].rearrange("p t (g d) -> p t g d", g=2))
                own(dve.memset(vaug[:, :, :, HD:HD + 1], 1.0))
                dve.sem_inc(vals_ready, 1)
                dve.wait_ge(bias_in, 16)
                dve.sem_inc(bias_in, -16)

                def first(u, s):
                    ab, g, t = u // 4, u // 2 % 2, u % 2
                    if ab == 0:
                        shift(u, s)
                    else:
                        shift(u, s, biasB[:, t, 4 * g:4 * g + 4, :], SQ, scr[:, 1, 4 * g:4 * g + 4])

                def finish(u, s):
                    ab, g, t = u // 4, u // 2 % 2, u % 2
                    v = ps2(s)[:, 0:260].rearrange("p (r n) -> p r n", r=4)
                    if ab:
                        dve.wait_ge(sinkexp_ready, 1)
                        dve.sem_inc(sinkexp_ready, -1)
                        own(dve.tensor_tensor(den[:, u % 2, :], v[:, :, HD], esk[:, u % 2, :], ADD))
                        own(dve.reciprocal(den[:, u % 2, :], den[:, u % 2, :]))
                    else:
                        own(dve.reciprocal(den[:, u % 2, :], v[:, :, HD]))
                    o = o_all[:, t, 512 * ab + 256 * g:512 * ab + 256 * g + 256].rearrange("p (r d) -> p r d", r=4)
                    dve.tensor_tensor(o, v[:, :, 0:HD], bc(den[:, u % 2, :].unsqueeze(2), 4, HD),
                                      MUL).then_inc(slot_free[s], 1)

                attention(8, first, finish)
                own(dve.engine_nop())
                for ab in range(2):
                    o = o_all[:, :, 512 * ab:512 * ab + 512]
                    own(dve.tensor_tensor(tmp1[:, :, 0:512], o, o, MUL))
                    own(dve.tensor_reduce(ve[:, 0:16].rearrange("p (t h) -> p t h", t=TT),
                                          tmp1[:, :, 0:512].rearrange("p t (h d) -> p t h d", d=HD), AX.X, ADD))
                    power(16, 1.0 / HD, 1e-6, ve[:, 0:16])
                    for t in range(TT):
                        x = o[:, t, :].rearrange("p (h d) -> p h d", d=HD)
                        dve.tensor_tensor(x, x, bc(rstd[:, 8 * t:8 * t + 8].unsqueeze(2), 8, HD), MUL)
                    own(dve.engine_nop())
                dve.wait_ge(gain_in[2], 16)
                dve.sem_inc(gain_in[2], -16)
                own(dve.tensor_tensor(o_all[:, :, :], o_all[:, :, :], bc(gains[:, 2, :].unsqueeze(1), TT, D), MUL))
                dve.sem_inc(gain_free[1], 1)
                dve.sem_inc(src_ready, 1)
                with dve.Fori(0, N_O // 2) as i:
                    for s in (0, 1):
                        take_rows(s)
                        c = bass.ds(512 * i + 256 * s, 256)
                        dve.scalar_tensor_tensor(h[:, :, c], h[:, :, c], ALPHA,
                                                 PS[:, 2 * s, :].rearrange("p (t n) -> p t n", t=TT), MUL,
                                                 ADD).then_inc(slot_free[s], 1)
                own(dve.engine_nop())
                layer_norm(h, h, 1)
                dve.sem_inc(src_ready, 1)
                with dve.Fori(0, N_WQ // 2) as i:
                    for s in (0, 1):
                        dve.wait_ge(dve_full[1], 1)
                        dve.sem_inc(dve_full[1], -1)
                        own(dve.tensor_copy(scc[:, :, :], PS[:, 2, :].rearrange("p (a n) -> p a n", a=4)))
                        dve.sem_inc(slot_free[1], 1)
                        for a in range(4):
                            dve.max(s16c[:, a, 0:8], scc[:, a, :])
                        own(dve.engine_nop())
                        for a in range(4):
                            dve.max_index(i16c[:, a, 0:8], s16c[:, a, 0:8], scc[:, a, :])
                            dve.match_replace(scr[:, a, :], s16c[:, a, 0:8], scc[:, a, :], -3e38)
                        own(dve.engine_nop())
                        for a in range(4):
                            dve.max(s16c[:, a, 8:16], scr[:, a, :])
                        own(dve.engine_nop())
                        for a in range(4):
                            dve.max_index(i16c[:, a, 8:16], s16c[:, a, 8:16], scr[:, a, :])
                        own(dve.engine_nop())
                        c = 2 * i + s
                        dve.tensor_copy(s16[:, c, :], s16c[:, :, :].rearrange("p a k -> p (a k)"))
                        own(dve.tensor_copy(i16[:, c, :], i16c[:, :, :].rearrange("p a k -> p (a k)")))
                with dve.Fori(0, PH) as c:
                    sv = s16[:, c, :].rearrange("p (t a k) -> p t a k", t=TT, a=2)
                    iv = i16[:, c, :].rearrange("p (t a k) -> p t a k", t=TT, a=2)
                    for t in range(TT):
                        dve.tensor_tensor(cand[:, t, :].rearrange("p (i j) -> p i j", i=TOPK),
                                          bc(sv[:, t, 0, :].unsqueeze(2), TOPK, TOPK),
                                          bc(sv[:, t, 1, :].unsqueeze(1), TOPK, TOPK), ADD)
                    own(dve.engine_nop())
                    for t in range(TT):
                        k = TOPK * t
                        own(dve.max(t16[:, k:k + 8], cand[:, t, :]))
                        dve.max_index(p16[:, k:k + 8], t16[:, k:k + 8], cand[:, t, :])
                        own(dve.match_replace(candr[:, t, :], t16[:, k:k + 8], cand[:, t, :], -3e38))
                        own(dve.max(t16[:, k + 8:k + 16], candr[:, t, :]))
                        own(dve.max_index(p16[:, k + 8:k + 16], t16[:, k + 8:k + 16], candr[:, t, :]))
                    dve.tensor_scalar(pj[:, 0, :], p16[:, :], 4, None, ALU.logical_shift_right)
                    own(dve.tensor_scalar(pj[:, 1, :], p16[:, :], 15, None, ALU.bitwise_and))
                    own(dve.tensor_copy(pf[:, :, :], pj[:, :, :]))
                    for a in range(2):
                        own(dve.tensor_tensor(oneh[:, :, :], bc(iota16[:, :].unsqueeze(1), TT * TOPK, TOPK),
                                              bc(pf[:, a, :].unsqueeze(2), TT * TOPK, TOPK), ALU.is_equal))
                        for t in range(TT):
                            x = oneh[:, TOPK * t:TOPK * t + TOPK, :]
                            dve.tensor_tensor(x, x, bc(iv[:, t, a, :].unsqueeze(1), TOPK, TOPK), MUL)
                        own(dve.engine_nop())
                        own(dve.tensor_reduce(sel[:, a, :, bass.ts(c, TOPK)],
                                              oneh[:, :, :].rearrange("p (t k) j -> p t k j", t=TT), AX.X, ADD))
                    for t in range(TT):
                        dve.tensor_scalar(sel[:, 2, t, bass.ts(c, TOPK)], t16[:, TOPK * t:TOPK * t + TOPK],
                                          t16[:, TOPK * t:TOPK * t + 1], None, SUB)
                    own(dve.engine_nop())
                dve.sem_inc(keys_free, 1)
                dve.sem_inc(smarg_ready, 1)
                dve.wait_ge(smexp_ready, 1)
                dve.sem_inc(smexp_ready, -1)
                g3 = sel[:, 2, :, :].rearrange("p t (h k) -> p (t h) k", h=PH)
                own(dve.tensor_reduce(gsm[:, :], g3, AX.X, ADD))
                own(dve.reciprocal(gsm[:, :], gsm[:, :]))
                own(dve.tensor_tensor(g3, g3, bc(gsm[:, :].unsqueeze(2), TT * PH, TOPK), MUL))
                dve.sem_inc(src_ready, 1)
                for t in range(TT):
                    dve.wait_ge(dve_full[t], 1)
                    dve.sem_inc(dve_full[t], -1)
                    dve.tensor_copy(selT[:, :, t * P:(t + 1) * P],
                                    ps2(t)[:, 0:3 * P].rearrange("p (i n) -> p i n", i=3)).then_inc(slot_free[t], 1)
                own(dve.engine_nop())
                dve.wait_ge(gelu_done, 1)
                dve.sem_inc(gelu_done, -1)
                av = arena[:, :].rearrange("p (e n) -> p n e", n=S)

                def onehots(i, s):
                    for n in range(4):
                        at = 8 * i + 4 * s + n
                        dve.tensor_scalar(ohA[:, s, n, :], iota[:, :], selT[:, 0, bass.ds(at, 1)],
                                          selT[:, 2, bass.ds(at, 1)], ALU.is_equal, MUL)
                        last = dve.tensor_scalar(ohB[:, s, n, :], iota[:, :], selT[:, 1, bass.ds(at, 1)], None,
                                                 ALU.is_equal)
                    last.then_inc(oneh_ready, 1)

                def gate_in(i, s):
                    dve.wait_ge(dve_full[s], 1)
                    dve.sem_inc(dve_full[s], -1)
                    a = av[:, bass.ds(8 * i + 4 * s, 4), :]
                    dve.tensor_tensor(a, a, PS[:, 2 * s, :].rearrange("p (n e) -> p n e", n=4),
                                      MUL).then_inc(slot_free[s], 1)

                onehots(0, 0)
                with dve.Fori(0, S // 8 - 1) as i:
                    onehots(i, 1)
                    gate_in(i, 0)
                    onehots(i + 1, 0)
                    gate_in(i, 1)
                onehots(S // 8 - 1, 1)
                gate_in(S // 8 - 1, 0)
                gate_in(S // 8 - 1, 1)
                own(dve.engine_nop())

                def stage(i, s):
                    dve.tensor_copy(wst[:, s, :, :].rearrange("p j n -> p (j n)"),
                                    arena[:, bass.ts(2 * i + s, 2 * S)]).then_inc(wst_ready[s], 1)

                stage(0, 0)
                stage(0, 1)
                with dve.Fori(1, NPAIR // 2) as i:
                    for s in (0, 1):
                        dve.wait_ge(wst_used[s], 1)
                        dve.sem_inc(wst_used[s], -1)
                        dve.sem_inc(chunk_free[s], 1)
                        stage(i, s)
                for s in (0, 1):
                    dve.wait_ge(wst_used[s], 1)
                    dve.sem_inc(wst_used[s], -1)
                    dve.sem_inc(chunk_free[s], 1)
                dve.wait_ge(acc_ready, 1)
                dve.sem_inc(acc_ready, -1)
                layer_norm(acc, h, 0)

            dve.sem_inc(arena_free2, 1)
            rms_norm(h, tmp1, 1)
            dve.sem_inc(src_ready, 1)
            for i in range(9):
                dve.wait_ge(consts_in[i], 16)
            own(dve.tensor_copy(posv[:, :], pos_f[:, :].bitcast(I32)))
            a3 = angs[:, :, :].rearrange("p q (a f) -> p q a f", a=3)
            own(dve.tensor_tensor(a3[:, 0, :, :], bc(posv[:, :].unsqueeze(2), 3, 32),
                                  bc(invf[:, :].unsqueeze(1), 3, 32), MUL))
            magic = 1.5 * 2.0 ** 23
            own(dve.tensor_scalar(angs[:, 1, :], angs[:, 0, :], 1 / (2 * math.pi), magic, MUL, ADD))
            own(dve.tensor_scalar(angs[:, 1, :], angs[:, 1, :], magic, None, SUB))
            c1 = 6.28125
            c2 = round((2 * math.pi - c1) * 2 ** 20) / 2 ** 20
            c3 = 2 * math.pi - c1 - c2
            for at, (src, c) in enumerate(((0, c1), (2, c2), (3, c3))):
                own(dve.scalar_tensor_tensor(angs[:, 2 + at, :], angs[:, 1, :], -c, angs[:, src, :], MUL, ADD))
            pi = float(np.float32(3.1415925))
            own(dve.tensor_scalar(angs[:, 2, :], angs[:, 4, :], pi, -pi, ALU.min, MAX))
            own(dve.tensor_scalar(angs[:, 3, :], angs[:, 4, :], math.pi / 2, None, ADD))
            own(dve.tensor_scalar(angs[:, 5, :], angs[:, 3, :], math.pi, -2 * math.pi, ALU.is_gt, MUL))
            own(dve.tensor_tensor(angs[:, 3, :], angs[:, 3, :], angs[:, 5, :], ADD))
            own(dve.tensor_scalar(angs[:, 3, :], angs[:, 3, :], pi, -pi, ALU.min, MAX))
            dve.sem_inc(ang_ready, 1)
            dve.wait_ge(trig_ready, 1)
            dve.sem_inc(trig_ready, -1)
            for half in range(2):
                c = slice(32 * half, 32 * half + 32)
                dve.tensor_copy(rope2[:, 0, :, c], a3[:, 7, :, :])
                dve.tensor_scalar(rope2[:, 1, :, c], a3[:, 6, :, :], 1.0 if half else -1.0, None, MUL)
            own(dve.engine_nop())
            with dve.Fori(0, N_CONV // 2) as i:
                for s in (0, 1):
                    take_rows(s)
                    dve.tensor_copy(convT[:, bass.ds(4 * i + 2 * s, 2), :],
                                    PS[:, 2 * s, :].rearrange("p (b n) -> p b n", b=2)).then_inc(slot_free[s], 1)
            with dve.Fori(0, (N_PROJ2 - 2) // 2) as i:
                for s in (0, 1):
                    take_rows(s)
                    dve.tensor_copy(proj2[:, :, bass.ds(512 * i + 256 * s, 256)],
                                    PS[:, 2 * s, :].rearrange("p (t n) -> p t n", t=TT)).then_inc(slot_free[s], 1)
            for s, w in ((0, CW), (1, 24)):
                take_rows(s)
                dve.tensor_copy(proj2[:, :, 1024 + 256 * s:1024 + 256 * s + w],
                                PS[:, 2 * s, :].rearrange("p (t n) -> p t n", t=TT)[:, :, 0:w]
                                ).then_inc(slot_free[s], 1)
            own(dve.engine_nop())
            dve.sem_inc(src_ready, 1)
            own(dve.tensor_copy(gate[:, :, :], proj2[:, :, 1280:1304]))
            dve.sem_inc(gate_arg, 1)
            dve.wait_ge(gate_exp, 1)
            dve.sem_inc(gate_exp, -1)
            own(dve.tensor_scalar(gate[:, :, :], gate[:, :, :], 1.0, None, ADD))
            own(dve.reciprocal(gate[:, :, :], gate[:, :, :]))
            dve.memset(kcT[:, :], 0.0)
            own(dve.memset(kblk[:, :, :, :], 0.0))
            dve.wait_ge(evac_done, 1)
            dve.sem_inc(evac_done, -1)
            for kv in range(2):
                for g in range(2):
                    rows = slice(HD * g, HD * g + HD)
                    v = kcvT[rows, kv, :].rearrange("p (m j) -> p j m", j=16)
                    for jh in range(2):
                        dve.tensor_tensor(
                            kblk[rows, kv, 16 * jh:16 * jh + 16, NCMP * g:NCMP * g + NCMP], v[:, :, jh:jh + NCMP],
                            peT[rows, kv, 16 * jh:16 * jh + 16].unsqueeze(2).to_broadcast([HD, 16, NCMP]), ADD)
                own(dve.engine_nop())
                dve.sem_inc(kb_ready, 1)
            for t in range(TT):
                for at, to, nh in ((0, 0, 8), (768, 512, 2), (1024, 640, 2)):
                    rope(proj2[:, t, at:at + HD * nh].rearrange("p (h d) -> p h d", d=HD),
                         qkr2[:, t, to:to + HD * nh].rearrange("p (h d) -> p h d", d=HD),
                         rope2[:, 0, t, :], rope2[:, 1, t, :], 1, 32,
                         tmp1[:, t, to:to + HD * nh].rearrange("p (h d) -> p h d", d=HD),
                         tmp2[:, t, to:to + HD * nh].rearrange("p (h d) -> p h d", d=HD))
            own(dve.engine_nop())
            dve.sem_inc(src_ready, 1)
            for w, at in ((0, 896), (1, 1152)):
                dve.tensor_copy(vaug[:, :, 2 * w:2 * w + 2, 0:HD],
                                proj2[:, :, at:at + 128].rearrange("p t (g d) -> p t g d", g=2))
            own(dve.memset(vaug[:, :, :, HD:HD + 1], 1.0))
            dve.sem_inc(vals_ready, 1)
            own(dve.tensor_tensor(zT[:, :, :], convT[:, 4:8, :], convT[:, 8:12, :], MUL))
            for b in range(4):
                dve.tensor_scalar(convT[:, 4 + b, :], zT[:, b, :], convw[:, b, 2:3], None, MUL)
            own(dve.engine_nop())
            for lag in (1, 2):
                for b in range(4):
                    c = convT[:, 4 + b, lag:S]
                    dve.scalar_tensor_tensor(c, zT[:, b, 0:S - lag], convw[:, b, 2 - lag:3 - lag], c, MUL, ADD)
                own(dve.engine_nop())
            own(dve.tensor_tensor(zT[:, :, :], convT[:, 0:4, :], convT[:, 4:8, :], MUL))
            own(dve.tensor_tensor(convT[:, 0:4, :], zT[:, :, :], zT[:, :, :], MUL))
            dve.wait_ge(evac_done, 1)
            dve.sem_inc(evac_done, -1)
            for hb in range(2):
                dve.tensor_copy(hidx[:, hb, :].rearrange("p (g r n) -> p g r n", g=2, r=4),
                                hidT[:, 1, hb, :].rearrange("p (g n) -> p g n", g=2).unsqueeze(2)
                                .to_broadcast([P, 2, 4, NCMP]))
            own(dve.engine_nop())
            dve.sem_inc(kb_ready, 1)
            dve.wait_ge(dve_full[0], 1)
            dve.sem_inc(dve_full[0], -1)
            own(dve.tensor_copy(krow[0:NCMP, :], PS[0:NCMP, 0, 0:2 * HD]))
            dve.sem_inc(slot_free[0], 1)
            hv = lambda x: x[0:NCMP, 0:2 * HD].rearrange("p (h d) -> p h d", d=HD)
            rope(hv(krow), hv(kcmp), rope2[0:NCMP, 0, 2, :], rope2[0:NCMP, 1, 2, :], 1, 32,
                 hv(tmp1[:, 0, :]), hv(tmp2[:, 0, :]))
            own(dve.engine_nop())
            dve.sem_inc(src_ready, 1)
            dve.wait_ge(dve_full[1], 1)
            dve.sem_inc(dve_full[1], -1)
            own(dve.tensor_copy(v120[0:120, :], PS[0:120, 2, 0:HD]))
            dve.sem_inc(slot_free[1], 1)
            own(dve.tensor_tensor(bd[0:120, :].rearrange("p (h d) -> p h d", d=HD),
                                  v120[0:120, :].unsqueeze(1).to_broadcast([120, 8, HD]),
                                  hmask[0:120, :].unsqueeze(2).to_broadcast([120, 8, HD]), MUL))
            dve.wait_ge(dve_full[1], 1)
            dve.sem_inc(dve_full[1], -1)
            own(dve.tensor_scalar(sc_c[:, :, :], PS[:, 2, 0:240].rearrange("p (t n) -> p t n", t=TT), SQ, None, MUL))
            dve.sem_inc(slot_free[1], 1)
            for t in range(TT):
                x = sc_c[:, t, :].rearrange("p (h n) -> p h n", n=NCMP)
                own(dve.tensor_tensor(x, x, bc(cmpbias[:, t, :].unsqueeze(1), 8, NCMP), ADD))
                own(dve.tensor_reduce(mx_c[:, t, :], x, AX.X, MAX))
                own(dve.tensor_tensor(x, x, bc(mx_c[:, t, :].unsqueeze(2), 8, NCMP), SUB))
            dve.sem_inc(shifted_ready, 1)
            dve.wait_ge(cmp_exp, 1)
            dve.sem_inc(cmp_exp, -1)
            for t in range(TT):
                x = pr_c[:, t, :].rearrange("p (h n) -> p h n", n=NCMP)
                dve.tensor_tensor(x, x, bc(cmpmask[:, t, :].unsqueeze(1), 8, NCMP), MUL)
            own(dve.engine_nop())
            dve.sem_inc(pcT_ready, 1)
            gh = gate[:, :, :].rearrange("p t (h c) -> p t h c", c=3)
            for t, s in ((0, 1), (1, 0)):
                dve.wait_ge(dve_full[s], 1)
                dve.sem_inc(dve_full[s], -1)
                own(dve.tensor_scalar(dn_c[:, t, :], PS[:, 2 * s + 1, 0:8], 1e-30, None, MAX))
                own(dve.reciprocal(dn_c[:, t, :], dn_c[:, t, :]))
                own(dve.tensor_tensor(dn_c[:, t, :], dn_c[:, t, :], gh[:, t, :, 0], MUL))
                dve.tensor_tensor(o_all[:, t, 0:512].rearrange("p (h d) -> p h d", d=HD),
                                  PS[:, 2 * s, :].rearrange("p (h d) -> p h d", d=HD),
                                  bc(dn_c[:, t, :].unsqueeze(2), 8, HD), MUL).then_inc(slot_free[s], 1)
            own(dve.engine_nop())
            dve.sem_inc(src_ready, 1)
            dve.wait_ge(dve_full[1], 1)
            dve.sem_inc(dve_full[1], -1)
            own(dve.tensor_scalar(ss[:, :], PS[:, 2, 0:S], 1 / 512, 1e-6, MUL, ADD))
            dve.sem_inc(slot_free[1], 1)
            dve.sem_inc(var2_ready, 1)
            dve.wait_ge(std2_ready, 1)
            dve.sem_inc(std2_ready, -1)
            own(dve.reciprocal(ss[:, :], ss[:, :]))
            for b in range(4):
                dve.scalar_tensor_tensor(xT[:, b, :], zT[:, b, :], convw[:, b, 3:4], ss[:, :], MUL, MUL)
            own(dve.engine_nop())

            def finish2(u, s):
                w, g, t = u // 4, u // 2 % 2, u % 2
                v = ps2(s)[:, 0:260].rearrange("p (r n) -> p r n", r=4)
                own(dve.reciprocal(den[:, u % 2, :], v[:, :, HD]))
                own(dve.tensor_tensor(den[:, u % 2, :], den[:, u % 2, :], gh[:, t, 4 * g:4 * g + 4, 1 + w], MUL))
                x = tmp1[:, u % 2, 0:256].rearrange("p (r d) -> p r d", r=4)
                own(dve.tensor_tensor(x, v[:, :, 0:HD], bc(den[:, u % 2, :].unsqueeze(2), 4, HD), MUL))
                dve.sem_inc(slot_free[s], 1)
                o = o_all[:, t, 256 * g:256 * g + 256].rearrange("p (r d) -> p r d", r=4)
                own(dve.tensor_tensor(o, o, x, ADD))

            attention(8, lambda u, s: shift(u, s, bc(causal[:, u % 2, :].unsqueeze(1), 4, S), SQ), finish2)
            rms_norm(o_all, o_all, 0, 512)
            dve.sem_inc(src_ready, 1)

            def rows_to(dst):
                with dve.Fori(0, 2) as i:
                    for s in (0, 1):
                        take_rows(s)
                        dve.tensor_copy(dst[:, :, bass.ds(512 * i + 256 * s, 256)],
                                        PS[:, 2 * s, :].rearrange("p (t n) -> p t n", t=TT)
                                        ).then_inc(slot_free[s], 1)
                own(dve.engine_nop())

            rows_to(o_all)
            residual_rms(o_all, 1)
            dve.sem_inc(arena_free2, 1)
            rms_norm(h, tmp1, 0)
            dve.sem_inc(src_ready, 1)
            dve.wait_ge(mem_in, 16)
            rms_norm(memr, o_all, 1)
            dve.sem_inc(src_ready, 1)

            def finish3(t, s):
                own(dve.reciprocal(den[:, t, :], PS[:, 4 + t, 0:4]))
                dve.tensor_tensor(o_all[:, t, :].rearrange("p (r d) -> p r d", r=4),
                                  ps2(s).rearrange("p (r d) -> p r d", r=4),
                                  bc(den[:, t, :].unsqueeze(2), 4, S), MUL).then_inc(slot_free[s], 1)

            attention(TT, shift, finish3)
            own(dve.engine_nop())
            dve.sem_inc(src_ready, 1)
            rows_to(o_all)
            residual_rms(o_all, 0)
            rms_norm(h, tmp1, 1)
            dve.sem_inc(src_ready, 1)
            dve.sem_inc(act_used, 2)
            with dve.Fori(0, NFB // 2) as i:
                for s in (0, 1):
                    dve.wait_ge(silu_done, 1)
                    dve.sem_inc(silu_done, -1)
                    dve.tensor_tensor(ffT[:, 2 * i + s, :], sil[:, s, :], PS[:, 2 * s, S:2 * S],
                                      MUL).then_inc(slot_free[s], 1)
                    own(dve.engine_nop())
                    dve.sem_inc(act_used, 1)
            dve.sem_inc(ffn_ready, 1)
            dve.wait_ge(acc_ready, 1)
            dve.sem_inc(acc_ready, -1)
            own(dve.tensor_copy(o_all[:, :, :], acc[:, :, :]))
            residual_rms(o_all, 0)
            dve.sem_inc(out_ready, 1)


def by_chunk(w):
    n = w.shape[-1]
    return w.reshape(KB, P, n // CW, CW).transpose(2, 1, 0, 3).reshape(n // CW, P, CHUNK)


def rows_of_tiles(a):
    return np.ascontiguousarray(a.reshape(TT, P, *a.shape[1:]).swapaxes(0, 1))


def shape_constants():
    f = np.float32
    t = np.arange(S)
    dist = np.abs(t[:, None] - t[None, :])
    slopes = (2.0 ** (-(np.arange(1, 9, dtype=f) * 8.0 / 8))).astype(f)
    bias = np.where(dist[:, None, :] <= 128, -(slopes[None, :, None] * dist[:, None, :].astype(f)), f(NEG))
    inv = (f(10000.0) ** (-np.arange(16, dtype=f) / f(16))).astype(f)
    pos = np.stack([t // 64, t % 64], -1).astype(f)
    ang = (pos[:, :, None] * inv).astype(f)
    cos = np.stack([np.cos(ang)] * 2, 2).reshape(S, HD)
    sin = np.stack([-np.sin(ang), np.sin(ang)], 2).reshape(S, HD)
    valid = (np.arange(NCMP)[None, :] * 16 + CMPJ - 1) <= t[:, None]
    head = np.zeros((P, 8), f)
    head[np.arange(120), np.arange(120) // NCMP] = 1.0
    return {
        "c_biasB": rows_of_tiles(bias.astype(f)),
        "c_ropeA": np.ascontiguousarray(
            np.stack([rows_of_tiles(cos), rows_of_tiles(sin)], 1).astype(f)),
        "c_causal": rows_of_tiles(np.where(t[None, :] <= t[:, None], f(0), f(NEG))),
        "c_cmpbias": rows_of_tiles(np.where(valid, f(0), f(NEG))),
        "c_cmpmask": rows_of_tiles(valid.astype(f)),
        "c_hmask": head,
        "c_invf": (f(10000.0) ** (-np.arange(32, dtype=f) / f(32))).astype(f),
    }


def layout(x):
    a = dict(shape_constants())
    heads = lambda at: [at + HD * i + j for i in PERM for j in range(HD)]
    cols = heads(0) + list(range(512, 768)) + heads(768) + list(range(1280, 1536))
    w = x["w_in"][:, :, cols]
    a["w_in"] = np.stack([by_chunk(m) for m in w])
    a["w_o"] = np.stack([by_chunk(m) for m in x["w_o"]])
    a["peer_wq"] = np.stack([by_chunk(m) for m in x["peer_wq"]])
    a["peer_keys"] = x["peer_keys"].transpose(0, 4, 1, 2, 3).reshape(DEPTH, P, PH, 2 * NK)
    a["peer_u"] = x["peer_u"].reshape(DEPTH, NK, NPAIR, 2, KB, P).transpose(0, 2, 5, 3, 4, 1).reshape(
        DEPTH, NPAIR, P, CHUNK)
    a["peer_v"] = x["peer_v"].reshape(DEPTH, NK, NPAIR, CHUNK).transpose(0, 2, 1, 3)
    a["gn_g"] = np.concatenate([x["gn_a_g"], x["gn_b_g"]], 1)
    a["qk_g"] = np.concatenate([x["qn_g"], x["kn_g"]], 1)
    for n in ("x", "ln_in_g", "ln_in_b", "sink", "ln1_g", "ln1_b", "ln2_g", "ln2_b", "mem_2",
              "norm_mix_pre_2", "norm_attn_out_2", "norm_mix_post_2", "norm_x_pre_2", "norm_mem_2",
              "norm_x_post_2", "norm_ffn_pre_2", "norm_ffn_post_2"):
        a[n] = x[n]
    p = np.arange(P)
    a["pos_2"] = x["positions_2"][0][np.stack([p, P + p, CMPJ - 1 + 16 * np.minimum(p, NCMP - 1)], 1)]
    w = x["w_in_2"]
    cols = list(range(1536)) + heads(1536) + list(range(2048, w.shape[1]))
    wide = np.zeros((D, (N_CONV + N_PROJ2) * CW), w.dtype)
    wide[:, :len(cols)] = w[:, cols]
    a["w_in_2"] = by_chunk(wide)
    w1 = np.stack([x["w1_kc_2"], x["w1_vc_2"]]).reshape(2, 4, 8, HD, CW).transpose(0, 1, 3, 2, 4)
    a["w1_2"] = np.concatenate([w1, w1], 2).reshape(8, P, CHUNK)
    a["w2_2"] = np.stack([x["w2_kc_2"], x["w2_vc_2"]]).reshape(2, 2, P, HD).transpose(2, 0, 1, 3)
    pe = np.stack([x["pe_kc_2"], x["pe_vc_2"]]).transpose(2, 0, 1)
    a["pe_2"] = np.concatenate([pe, pe], 0)
    a["conv_2"] = np.concatenate([x["conv_w_2"], x["norm_conv_out_2"][None]], 0).reshape(4, 4, P).transpose(2, 1, 0)
    for n in ("w_out_2", "w_q_x_2", "w_kv_x_2", "w_o_x_2"):
        a[n] = by_chunk(x[n])
    w = x["w_gate_up_2"]
    a["w_gate_up_2"] = by_chunk(w.reshape(D, 2, NFB, P).transpose(0, 2, 1, 3).reshape(D, 2 * FF))
    a["w_down_2"] = x["w_down_2"].reshape(NFB // 2, 2, P, D).transpose(0, 2, 1, 3).reshape(NFB // 2, P, CHUNK)
    return {k: np.ascontiguousarray(v) for k, v in a.items()}


def kernel(**inputs):
    import concourse.bacc as bacc
    from concourse.bass_utils import run_bass_kernel_spmd

    arrays = layout({k: np.asarray(v) for k, v in inputs.items()})
    nc = bacc.Bacc("TRN2", target_bir_lowering=False, num_devices=1)
    aps = {k: nc.dram_tensor(f"in_{k}", v.shape, mybir.dt.from_np(v.dtype), kind="ExternalInput").ap()
           for k, v in arrays.items()}
    out = nc.dram_tensor("out", (1, S, D), mybir.dt.float32, kind="ExternalOutput").ap()
    build(nc, aps, out)
    r = run_bass_kernel_spmd(nc, [{f"in_{k}": v for k, v in arrays.items()}], core_ids=[0])
    return r.results[0]["out"]
```

```python
import math

import numpy as np
import concourse.bass as bass
from concourse import mybir
from contextlib import ExitStack

P = 128
D = 1024
S = 256
DEPTH = 2
KB = D // P
TT = S // P
HD = 64
CW = 256
CHUNK = KB * CW
N_IN, N_O, N_WQ = 6, 4, 8
NK = 128
QW = CHUNK // 4
NPAIR = NK // 2
PH, TOPK = 8, 16
N_CONV, N_PROJ2 = 6, 6
P2W = 1304
NCMP = 15
CMPJ = 32
FF = 2816
NFB = FF // P
XH = 4
ALPHA = (2.0 * DEPTH) ** 0.25
NEG = -1e30
ARENA = NK * S
TAIL = 26624
SQ = 0.125
PERM = [0, 4, 1, 5, 2, 6, 3, 7]


def build(nc, A, out):
    F32, U32, I32, F32R = mybir.dt.float32, mybir.dt.uint32, mybir.dt.int32, mybir.dt.float32r
    ALU, ACT, AX = mybir.AluOpType, mybir.ActivationFunctionType, mybir.AxisListType
    MUL, ADD, SUB, MAX = ALU.mult, ALU.add, ALU.subtract, ALU.max
    ctx = ExitStack()
    with ctx:
        def sb(name, shape, dt=F32):
            return ctx.enter_context(nc.sbuf_tensor(name, shape, dt))

        def sem(name):
            return ctx.enter_context(nc.semaphore(name))

        arena = sb("arena", [P, ARENA])

        def region(off, *shape):
            n = int(np.prod(shape))
            assert off + n <= ARENA
            v = arena[:, off:off + n]
            if len(shape) == 2:
                v = v.rearrange("p (a b) -> p a b", a=shape[0])
            if len(shape) == 3:
                v = v.rearrange("p (a b c) -> p a b c", a=shape[0], b=shape[1])
            if len(shape) == 4:
                v = v.rearrange("p (a b c d) -> p a b c d", a=shape[0], b=shape[1], c=shape[2])
            return v

        ring = sb("ring", [P, 2, CHUNK])
        h = sb("h", [P, TT, D])
        wh = sb("wh", [P, 4, QW], F32R)
        wl = sb("wl", [P, 4, QW], F32R)
        xh = sb("xh", [P, KB, S], F32R)
        xl = sb("xl", [P, KB, S], F32R)
        gains0 = sb("gains0", [P, 2, D])
        gains1 = region(4352, 2, D)
        gains2 = region(10240, 1, D)
        ident = sb("ident", [P, P])
        identa = sb("identa", [P, P])
        iota = sb("iota", [P, P])
        iota16 = sb("iota16", [P, TOPK])
        mhalf = sb("mhalf", [P, 1])
        ones = sb("ones", [P, P])
        qkg = sb("qkg", [P, DEPTH, 2 * HD])
        sinks = sb("sinks", [P, DEPTH, 8])
        ropeA = region(6400, 2, TT, HD)
        stats = sb("stats", [P, TT, 2, 6])
        mv = sb("mv", [P, TT, 2])
        ve = sb("ve", [P, 20])
        rstd = sb("rstd", [P, 20])
        peer_k = region(TAIL, PH, 2 * NK)
        qTc = region(28672, 2, S)
        scc = region(29184, 4, NK)
        scr = region(29696, 4, NK)
        s16 = region(30208, PH, 4 * TOPK)
        i16 = region(30720, PH, 4 * TOPK)
        s16c = sb("s16c", [P, 4, TOPK])
        i16c = sb("i16c", [P, 4, TOPK], U32)
        qsc = sb("qsc", [P, 2 * HD + 8])
        cand = peer_k[:, 0:2, :].rearrange("p t (i k) -> p t i k", i=1)[:, :, 0, :]
        candr = peer_k[:, 2:4, :].rearrange("p t (i k) -> p t i k", i=1)[:, :, 0, :]
        oneh = peer_k[:, 4:6, :].rearrange("p a b -> p (a b)").rearrange("p (a b) -> p a b", b=TOPK)
        t16 = sb("t16", [P, TT * TOPK])
        p16 = sb("p16", [P, TT * TOPK], U32)
        pj = sb("pj", [P, 2, TT * TOPK], U32)
        pf = sb("pf", [P, 2, TT * TOPK])
        sel = sb("sel", [P, 3, TT, PH * TOPK])
        selT = sb("selT", [P, 3, S])
        gsm = sb("gsm", [P, TT * PH])
        ohA = gains0[:, 0, :].rearrange("p (s n k) -> p s n k", s=2, n=4)
        ohB = gains0[:, 1, :].rearrange("p (s n k) -> p s n k", s=2, n=4)
        gst = sb("gst", [P, 2, 4 * NK])
        wst = [m[:, 0:2, :] for m in (xh, xl)]
        PS = ctx.enter_context(nc.psum_tensor("PS", [P, 8, 512], F32))

        def ps2(s):
            return PS[:, 2 * s:2 * s + 2, :].rearrange("p a b -> p (a b)")

        acc = PS[:, 4:8, :].rearrange("p (t c) n -> p t (c n)", t=TT)

        chunk_in = [sem(f"chunk_in{s}") for s in (0, 1)]
        high_ready = [sem(f"high_ready{q}") for q in range(4)]
        parts_ready = [sem(f"parts_ready{q}") for q in range(4)]
        parts_free = [sem(f"parts_free{q}") for q in range(4)]
        xh_ready = [sem(f"xh_ready{s}") for s in (0, 1)]
        chunk_free = [sem(f"chunk_free{s}") for s in (0, 1)]
        act_full = [sem(f"act_full{s}") for s in (0, 1)]
        dve_full = [sem(f"dve_full{s}") for s in (0, 1)]
        slot_free = [sem(f"slot_free{s}") for s in (0, 1)]
        src_ready = sem("src_ready")
        var_ready = sem("var_ready")
        rstd_ready = sem("rstd_ready")
        gain_in = [sem(f"gain_in{s}") for s in range(4)]
        gain_free = [sem(f"gain_free{s}") for s in (0, 1)]
        consts_in = [sem(f"consts_in{i}") for i in range(24)]
        consts_dve, consts_pe = sem("consts_dve"), sem("consts_pe")
        keys_in, keys_free = sem("keys_in"), sem("keys_free")
        rope_in = sem("rope_in")
        bias_in, arena_free, arena_free2 = sem("bias_in"), sem("arena_free"), sem("arena_free2")
        shifted_ready = sem("shifted_ready")
        probs_ready = sem("probs_ready")
        sinkarg_ready, sinkexp_ready = sem("sinkarg_ready"), sem("sinkexp_ready")
        vals_ready = sem("vals_ready")
        evac_done = sem("evac_done")
        oneh_ready = sem("oneh_ready")
        choices_ready = sem("choices_ready")
        gates_ready = [sem(f"gates_ready{s}") for s in (0, 1)]
        gates_used = [sem(f"gates_used{s}") for s in (0, 1)]
        oneh_used = [sem(f"oneh_used{s}") for s in (0, 1)]
        gates_done = sem("gates_done")
        routing_done = sem("routing_done")
        wst_ready = [sem(f"wst_ready{s}") for s in (0, 1)]
        wst_used = [sem(f"wst_used{s}") for s in (0, 1)]
        acc_ready = sem("acc_ready")
        h_ready = sem("h_ready")
        gelu_done = sem("gelu_done")
        smarg_ready, smexp_ready = sem("smarg_ready"), sem("smexp_ready")
        mem_in, pos_in = sem("mem_in"), sem("pos_in")
        ang_ready, trig_ready = sem("ang_ready"), sem("trig_ready")
        gate_arg, gate_exp = sem("gate_arg"), sem("gate_exp")
        kb_ready = sem("kb_ready")
        pcT_ready, cmp_exp = sem("pcT_ready"), sem("cmp_exp")
        var2_ready, std2_ready = sem("var2_ready"), sem("std2_ready")
        silu_done, act_used = sem("silu_done"), sem("act_used")
        ffn_ready = sem("ffn_ready")
        out_ready, out_done = sem("out_ready"), sem("out_done")
        x_in = sem("x_in")
        dve_own, act_own, pool_own = sem("dve_own"), sem("act_own"), sem("pool_own")

        proj = region(0, TT, 1536)
        qkr = region(3072, TT, 640)
        tmp1 = region(28672, TT, D)
        tmp2 = region(30720, TT, D)
        qkT = region(8448, 2, 6, S)
        vaug = region(11520, TT, 4, 65)
        biasB = region(12288, TT, 8, S)
        o_all = region(16384, TT, D)
        shf = region(18432, 2, 4, S)
        prb = region(20480, 2, 4, S)
        prT = region(22528, 2, 8, P)
        mx = region(24576, 2, 4)
        den = region(24592, 2, 4)
        snk = region(24608, 2, 4)
        esk = region(24624, 2, 4)
        zT = region(0, 4, S)
        convT = region(1024, 12, S)
        proj2 = region(4096, TT, P2W)
        qkr2 = region(6704, TT, 768)
        kcvT = region(8240, 2, S)
        w2k = region(8752, 2, 2, HD)
        qk2T = region(26560, 6, S)
        causal = region(12288, TT, S)
        cmpbias = region(12800, TT, NCMP)
        cmpmask = region(12830, TT, NCMP)
        hmask = region(12860, 8)
        peT = region(12868, 2, CMPJ)
        convw = region(12932, 4, 4)
        rope2 = region(12948, 2, 3, HD)
        angs = region(13332, 8, 96)
        pos_f = region(14100, 3)
        invf = region(14103, 32)
        gate = region(14135, TT, 24)
        hidT = region(14183, 2, 2, 2 * NCMP)
        hidx = region(14303, 2, 120)
        kcmp = region(14543, 2 * HD)
        kcT = region(9144, 2 * NCMP)
        sc_c = region(14686, TT, 120)
        pr_c = region(14926, TT, 120)
        prT_c = region(15166, TT, P)
        mx_c = region(15422, TT, 8)
        dn_c = region(15438, TT, 8)
        bd = region(15454, 512)
        v120 = region(15966, HD)
        ss = region(16030, S)
        posv = region(16290, 3)
        krow = region(9008, 2 * HD)
        coef = region(9136, 8)
        kblk = region(24640, 2, CMPJ, 2 * NCMP)
        memr = region(0, TT, D)
        qxT = region(4096, KB, S)
        kxT = region(6144, KB, S)
        vx = region(8192, TT, D)
        ffT = region(0, NFB, S)
        sil = region(6144, 2, S)

        block = ctx.enter_context(nc.Block())

        @block.sync
        def _(sp):
            def stream(src, n):
                with sp.Fori(0, n // 2) as i:
                    for s in (0, 1):
                        sp.wait_ge(chunk_free[s], 2)
                        sp.sem_inc(chunk_free[s], -2)
                        sp.dma_start(ring[:, s, :], src(2 * i + s)).then_inc(chunk_in[s], 16)

            def gain(at, *rows, block2=False):
                sp.wait_ge(gain_free[at], 1)
                sp.sem_inc(gain_free[at], -1)
                dst = (gains0, gains1, gains2)[at + block2 * at]
                for i, g in enumerate(rows):
                    sp.dma_start(dst[:, i, 0:g.shape[-1]],
                                 g.partition_broadcast(P)).then_inc(gain_in[2 * at + i], 16)

            for s in (0, 1):
                sp.sem_inc(chunk_free[s], 2)
            gain(0, A["ln_in_g"], A["ln_in_b"])
            with sp.Fori(0, DEPTH) as l:
                stream(lambda c: A["w_in"][l, c], N_IN)
                sp.wait_ge(arena_free, 1)
                sp.sem_inc(arena_free, -1)
                sp.dma_start(ropeA[:, :, :, :], A["c_ropeA"]).then_inc(rope_in, 16)
                gain(1, A["gn_g"][l])
                sp.dma_start(biasB[:, :, :, :], A["c_biasB"]).then_inc(bias_in, 16)
                sp.wait_ge(keys_free, 1)
                sp.sem_inc(keys_free, -1)
                sp.dma_start(peer_k[:, :, :], A["peer_keys"][l]).then_inc(keys_in, 16)
                stream(lambda c: A["w_o"][l, c], N_O)
                gain(1, A["ln1_g"][l], A["ln1_b"][l])
                stream(lambda c: A["peer_wq"][l, c], N_WQ)
                stream(lambda c: A["peer_u"][l, c], NPAIR)
                stream(lambda c: A["peer_v"][l, c], NPAIR)
                gain(0, A["ln2_g"][l], A["ln2_b"][l])
            sp.wait_ge(arena_free, 1)
            sp.sem_inc(arena_free, -1)
            gain(1, A["norm_mix_pre_2"], block2=True)
            stream(lambda c: A["w_in_2"][c], N_CONV + N_PROJ2)
            gain(0, A["norm_attn_out_2"])
            stream(lambda c: A["w1_2"][c], 8)
            gain(1, A["norm_mix_post_2"], block2=True)
            stream(lambda c: A["w_out_2"][c], 4)
            gain(0, A["norm_x_pre_2"])
            stream(lambda c: A["w_q_x_2"][c], 2)
            gain(1, A["norm_mem_2"], block2=True)
            stream(lambda c: A["w_q_x_2"][2 + c], 2)
            stream(lambda c: A["w_kv_x_2"][c], 8)
            gain(0, A["norm_x_post_2"])
            stream(lambda c: A["w_o_x_2"][c], 4)
            gain(1, A["norm_ffn_pre_2"], block2=True)
            stream(lambda c: A["w_gate_up_2"][c], NFB)
            gain(0, A["norm_ffn_post_2"])
            stream(lambda c: A["w_down_2"][c], NFB // 2 - 1)
            sp.wait_ge(chunk_free[0], 2)
            sp.sem_inc(chunk_free[0], -2)
            sp.dma_start(ring[:, 0, :], A["w_down_2"][NFB // 2 - 1]).then_inc(chunk_in[0], 16)
            sp.wait_ge(out_ready, 1)
            sp.sem_inc(out_ready, -1)
            sp.dma_start(out.rearrange("b (t p) d -> p (b t) d", p=P), h[:, :, :]).then_inc(out_done, 16)
            sp.wait_ge(out_done, 16)

        @block.gpsimd
        def _(pool):
            def own(ins):
                ins.then_inc(pool_own, 1)
                pool.wait_ge(pool_own, 1)
                pool.sem_inc(pool_own, -1)

            own(pool.memset(mhalf[:, :], -0.5))
            own(pool.memset(ones[:, :], 1.0))
            own(pool.memset(ident[:, :], 0.0))
            own(pool.memset(identa[:, :], 0.0))
            for m, v in ((ident, 1.0), (identa, ALPHA)):
                own(pool.affine_select(out=m[:, :], in_=m[:, :], compare_op=ALU.not_equal, fill=v,
                                       base=0, pattern=[[-1, P]], channel_multiplier=1))
            own(pool.iota(iota[:, :], pattern=[[1, P]], base=0, channel_multiplier=0,
                          allow_small_or_imprecise_dtypes=True))
            own(pool.iota(iota16[:, :], pattern=[[1, TOPK]], base=0, channel_multiplier=0,
                          allow_small_or_imprecise_dtypes=True))
            pool.sem_inc(consts_dve, 1)
            pool.sem_inc(consts_pe, 1)

            def power(n):
                pool.wait_ge(var_ready, 1)
                pool.sem_inc(var_ready, -1)
                pool.tensor_tensor(rstd[:, 0:n], ve[:, 0:n], mhalf[:, :].to_broadcast([P, n]),
                                   ALU.pow).then_inc(rstd_ready, 1)

            power(TT)
            def low_parts(n):
                with pool.Fori(0, n // 2):
                    for s in (0, 1):
                        for q in range(3):
                            pool.wait_ge(high_ready[q], 1)
                            pool.sem_inc(high_ready[q], -1)
                            pool.tensor_tensor(wl[:, q, :], ring[:, s, q * QW:(q + 1) * QW],
                                               wh[:, q, :].bitcast(F32), SUB).then_inc(
                                                   parts_ready[q] if q < 2 else pool_own, 1)
                        pool.wait_ge(pool_own, 1)
                        pool.sem_inc(pool_own, -1)
                        pool.sem_inc(parts_ready[2], 1)
                        pool.sem_inc(chunk_free[s], 1)

            with pool.Fori(0, DEPTH):
                low_parts(N_IN)
                power(20)
                power(16)
                power(16)
                low_parts(N_O)
                power(TT)
                low_parts(N_WQ)
                low_parts(NPAIR)
                pool.wait_ge(choices_ready, 1)
                pool.sem_inc(choices_ready, -1)
                av = arena[:, :].rearrange("p (e n) -> p n e", n=S)
                with pool.Fori(0, S // 8) as i:
                    for s in (0, 1):
                        pool.wait_ge(gates_ready[s], 1)
                        pool.sem_inc(gates_ready[s], -1)
                        a = av[:, bass.ds(8 * i + 4 * s, 4), :]
                        pool.tensor_tensor(a, a, gst[:, s, :].rearrange("p (n e) -> p n e", n=4),
                                           MUL).then_inc(gates_used[s], 1)
                power(TT)
            pool.wait_ge(arena_free2, 1)
            pool.sem_inc(arena_free2, -1)
            for i, (dst, src) in enumerate((
                    (causal[:, :, :], A["c_causal"]), (cmpbias[:, :, :], A["c_cmpbias"]),
                    (cmpmask[:, :, :], A["c_cmpmask"]), (hmask[:, :], A["c_hmask"]),
                    (peT[:, :, :], A["pe_2"]), (convw[:, :, :], A["conv_2"]),
                    (w2k[:, :, :, :], A["w2_2"]), (invf[:, :], A["c_invf"].partition_broadcast(P)))):
                pool.dma_start(dst, src).then_inc(consts_in[i], 16)
            pool.dma_start(pos_f[:, :].bitcast(I32), A["pos_2"]).then_inc(consts_in[8], 16)
            power(TT)
            low_parts(N_CONV + N_PROJ2)
            power(TT)
            low_parts(4)
            power(TT)
            pool.wait_ge(arena_free2, 1)
            pool.sem_inc(arena_free2, -1)
            pool.dma_start(memr[:, :, :], A["mem_2"][0].rearrange("(t p) d -> p t d", p=P)).then_inc(mem_in, 16)
            power(TT)
            power(TT)
            low_parts(4)
            low_parts(8)
            low_parts(4)
            power(TT)
            power(TT)
            low_parts(NFB)
            power(TT)

        @block.tensor
        def _(pe):
            def evacuated():
                for s in (0, 1):
                    pe.wait_ge(slot_free[s], 1)

            def transposes(s, full, pairs):
                pe.wait_ge(slot_free[s], 1)
                pe.sem_inc(slot_free[s], -1)
                for dst, src in pairs:
                    n = src.shape[0]
                    last = pe.transpose(dst, src, ident[0:n, 0:n])
                last.then_inc(full[s], 1)

            def to_xT(src):
                pe.wait_ge(src_ready, 1)
                pe.sem_inc(src_ready, -1)
                for t in range(TT):
                    transposes(t, act_full, [(ps2(t)[:, k * P:(k + 1) * P], src[:, t, k * P:(k + 1) * P])
                                             for k in range(KB)])
                evacuated()

            def rows_by_chunk(s, full, width=CW):
                pe.wait_ge(slot_free[s], 1)
                pe.sem_inc(slot_free[s], -1)
                for q in range(4):
                    pe.wait_ge(parts_ready[q], 1)
                    pe.sem_inc(parts_ready[q], -1)
                    for t in range(TT):
                        for k in range(2):
                            for i, (x, w) in enumerate(((xh, wh), (xh, wl), (xl, wh))):
                                last = pe.matmul(PS[:, 2 * s + t, 0:width], x[:, 2 * q + k, t * P:(t + 1) * P],
                                                 w[:, q, k * CW:k * CW + width], start=q + k + i == 0,
                                                 stop=q + k + i == 6)
                    if q < 3:
                        last.then_inc(parts_free[q], 1)
                last.then_inc(full[s], 1)

            def chunk_by_cols(s, full):
                pe.wait_ge(slot_free[s], 1)
                pe.sem_inc(slot_free[s], -1)
                for q in range(4):
                    pe.wait_ge(parts_ready[q], 1)
                    pe.sem_inc(parts_ready[q], -1)
                    for b in range(2):
                        for k in range(2):
                            for i, (w, x) in enumerate(((wh, xh), (wh, xl), (wl, xh))):
                                last = pe.matmul(PS[:, 2 * s + b, 0:S],
                                                 w[:, q, k * CW + b * P:k * CW + (b + 1) * P],
                                                 x[:, 2 * q + k, :], start=q + k + i == 0, stop=q + k + i == 6)
                    if q < 3:
                        last.then_inc(parts_free[q], 1)
                last.then_inc(full[s], 1)

            def loop2(n, f, *a):
                with pe.Fori(0, n // 2):
                    for s in (0, 1):
                        f(s, *a)

            def attention(units, score, sums=None, value=None):
                n = [0]

                def slot():
                    n[0] += 1
                    return (n[0] - 1) % 2

                def scores(u):
                    s = slot()
                    pe.wait_ge(slot_free[s], 1)
                    pe.sem_inc(slot_free[s], -1)
                    for r in range(4):
                        prods = score(u, r)
                        for i, (a, b) in enumerate(prods):
                            last = pe.matmul(ps2(s)[:, r * S:(r + 1) * S], a, b, start=i == 0,
                                             stop=i == len(prods) - 1)
                    last.then_inc(dve_full[s], 1)

                scores(0)
                for u in range(units):
                    if u + 1 < units:
                        scores(u + 1)
                    pe.wait_ge(probs_ready, 1)
                    pe.sem_inc(probs_ready, -1)
                    s = slot()
                    transposes(s, act_full, [(ps2(s)[:, i * P:(i + 1) * P],
                                              prb[:, u % 2, i // 2, (i % 2) * P:(i % 2 + 1) * P])
                                             for i in range(8)])
                    pe.wait_ge(slot_free[s], 1)
                    s = slot()
                    pe.wait_ge(slot_free[s], 1)
                    pe.sem_inc(slot_free[s], -1)
                    for r in range(4):
                        for o, v in value(u, s, r):
                            for st in range(TT):
                                last = pe.matmul(o, prT[:, u % 2, 2 * r + st, :], v(st), start=st == 0,
                                                 stop=st == TT - 1)
                    last.then_inc(dve_full[s], 1)

            pe.wait_ge(consts_pe, 1)
            pe.sem_inc(consts_pe, -1)
            with pe.Fori(0, DEPTH):
                to_xT(h)
                loop2(N_IN, rows_by_chunk, dve_full)
                for ab in (1, 0):
                    pe.wait_ge(src_ready, 1)
                    pe.sem_inc(src_ready, -1)
                    for t in range(TT):
                        src = proj[:, t, 768:1408] if ab else qkr[:, t, :]
                        transposes(t, act_full, [(ps2(t)[:, j * P:(j + 1) * P], src[:, j * P:(j + 1) * P])
                                                 for j in range(5)])
                evacuated()
                pe.wait_ge(vals_ready, 1)
                pe.sem_inc(vals_ready, -1)

                def score(u, r):
                    ab, g, t = u // 4, u // 2 % 2, u % 2
                    rows = slice(HD * g, HD * g + HD)
                    return [(qkT[rows, ab, r, t * P:(t + 1) * P], qkT[rows, ab, 4, :])]

                def value(u, s, r):
                    return [(ps2(s)[:, r * 65:(r + 1) * 65], lambda st: vaug[:, st, u // 2, :])]

                attention(8, score, value=value)
                to_xT(o_all)
                loop2(N_O, rows_by_chunk, dve_full)
                to_xT(h)
                pe.wait_ge(keys_in, 16)
                with pe.Fori(0, N_WQ // 2) as i:
                    for s in (0, 1):
                        chunk_by_cols(0, act_full)
                        pe.wait_ge(slot_free[0], 1)
                        pe.wait_ge(slot_free[1], 1)
                        pe.sem_inc(slot_free[1], -1)
                        for t in range(TT):
                            for p in range(2):
                                last = pe.matmul(PS[:, 2, (2 * t + p) * NK:(2 * t + p + 1) * NK],
                                                 qTc[:, p, t * P:(t + 1) * P],
                                                 peer_k[:, 2 * i + s, p * NK:(p + 1) * NK], start=True, stop=True)
                        last.then_inc(dve_full[1], 1)
                pe.wait_ge(keys_in, 16)
                pe.sem_inc(keys_in, -16)
                def experts():
                    for j in range(2):
                        pe.wait_ge(slot_free[j], 1)
                        pe.sem_inc(slot_free[j], -1)
                        for q in (2 * j, 2 * j + 1):
                            pe.wait_ge(parts_ready[q], 1)
                            pe.sem_inc(parts_ready[q], -1)
                            for k in range(4):
                                at = 4 * (q % 2) + k
                                for i, (w, x) in enumerate(((wh, xh), (wh, xl), (wl, xh))):
                                    last = pe.matmul(PS[:, 2 * j, 0:S], w[:, q, k * P:(k + 1) * P], x[:, at, :],
                                                     start=at + i == 0, stop=at + i == 9)
                            if q % 2 == 0:
                                last.then_inc(parts_free[q], 1)
                        last.then_inc(act_full[j], 1)

                with pe.Fori(0, NPAIR):
                    experts()
                pe.wait_ge(src_ready, 1)
                pe.sem_inc(src_ready, -1)
                for t in range(TT):
                    transposes(t, dve_full, [(ps2(t)[:, i * P:(i + 1) * P], sel[:, i, t, :]) for i in range(3)])
                with pe.Fori(0, S // 8):
                    for s in (0, 1):
                        pe.wait_ge(oneh_ready, 1)
                        pe.sem_inc(oneh_ready, -1)
                        pe.wait_ge(slot_free[s], 1)
                        pe.sem_inc(slot_free[s], -1)
                        for n in range(4):
                            last = pe.matmul(PS[:, 2 * s, n * P:(n + 1) * P], ohA[:, s, n, :], ohB[:, s, n, :],
                                             start=True, stop=True)
                        last.then_inc(act_full[s], 1)
                for t in range(TT):
                    for c in range(2):
                        pe.matmul(acc[:, t, c * 512:(c + 1) * 512], identa[:, :], h[:, t, c * 512:(c + 1) * 512],
                                  start=True, stop=False)
                def weigh(end=False):
                    for j in range(2):
                        pe.wait_ge(wst_ready[j], 1)
                        pe.sem_inc(wst_ready[j], -1)
                        for c in range(2):
                            q = 2 * j + c
                            pe.wait_ge(parts_ready[q], 1)
                            pe.sem_inc(parts_ready[q], -1)
                            for t in range(TT):
                                for i, (x, w) in enumerate(((0, wh), (0, wl), (1, wh))):
                                    last = pe.matmul(acc[:, t, c * 512:(c + 1) * 512],
                                                     wst[x][:, j, t * P:(t + 1) * P], w[:, q, :],
                                                     start=False, stop=end and j == 1 and i == 2)
                            if c == 0:
                                last.then_inc(parts_free[q], 1)
                        last.then_inc(wst_used[j], 1)

                with pe.Fori(0, NPAIR - 1):
                    weigh()
                weigh(True)
                pe.drain().then_inc(acc_ready, 1)

            to_xT(tmp1)
            loop2(N_CONV, chunk_by_cols, dve_full)
            loop2(N_PROJ2 - 2, rows_by_chunk, dve_full)
            rows_by_chunk(0, dve_full)
            rows_by_chunk(1, dve_full, 24)
            pe.wait_ge(src_ready, 1)
            pe.sem_inc(src_ready, -1)
            for t in range(TT):
                transposes(t, act_full, [(ps2(t)[:, i * P:(i + 1) * P], proj2[:, t, 512 + i * P:512 + (i + 1) * P])
                                         for i in range(2)])
            for kv in range(2):
                pe.wait_ge(kb_ready, 1)
                pe.sem_inc(kb_ready, -1)
                pe.wait_ge(slot_free[kv], 1)
                pe.sem_inc(slot_free[kv], -1)
                for c in range(4):
                    s = c % 2
                    pe.wait_ge(chunk_in[s], 16)
                    pe.sem_inc(chunk_in[s], -16)
                    for hb in range(2):
                        for j in range(8):
                            last = pe.matmul(PS[:, 2 * kv + hb, 0:2 * NCMP],
                                             ring[:, s, j * CW + hb * P:j * CW + (hb + 1) * P],
                                             kblk[:, kv, 8 * c + j, :], start=c + j == 0, stop=c + j == 10)
                    if c < 3:
                        last.then_inc(chunk_free[s], 2)
                last.then_inc(act_full[kv], 1)
            pe.wait_ge(src_ready, 1)
            pe.sem_inc(src_ready, -1)
            evacuated()
            for t in range(TT):
                transposes(t, act_full, [(ps2(t)[:, j * P:(j + 1) * P], qkr2[:, t, j * P:(j + 1) * P])
                                         for j in range(6)])
            pe.wait_ge(kb_ready, 1)
            pe.sem_inc(kb_ready, -1)
            pe.wait_ge(slot_free[0], 1)
            pe.sem_inc(slot_free[0], -1)
            for g in range(2):
                for hb in range(2):
                    last = pe.matmul(PS[0:NCMP, 0, g * HD:(g + 1) * HD], hidT[:, 0, hb, g * NCMP:(g + 1) * NCMP],
                                     w2k[:, 0, hb, :], start=hb == 0, stop=hb == 1)
            last.then_inc(dve_full[0], 1)
            pe.wait_ge(slot_free[1], 1)
            pe.sem_inc(slot_free[1], -1)
            for hb in range(2):
                last = pe.matmul(PS[0:120, 2, 0:HD], hidx[:, hb, :], w2k[:, 1, hb, :], start=hb == 0, stop=hb == 1)
            last.then_inc(dve_full[1], 1)
            pe.wait_ge(src_ready, 1)
            pe.sem_inc(src_ready, -1)
            transposes(0, act_full, [(PS[:, 0, 0:NCMP], kcmp[0:NCMP, :])])
            pe.wait_ge(slot_free[1], 1)
            pe.sem_inc(slot_free[1], -1)
            pe.wait_ge(slot_free[0], 1)
            for t in range(TT):
                o = PS[:, 2, t * 120:(t + 1) * 120].rearrange("p (g r n) -> p g r n", g=2, r=4)
                for r in range(4):
                    last = pe.matmul(o[:, :, r, :], qk2T[:, r, t * P:(t + 1) * P], kcT[:, :],
                                     start=True, stop=True)
            last.then_inc(dve_full[1], 1)
            pe.wait_ge(pcT_ready, 1)
            pe.sem_inc(pcT_ready, -1)
            transposes(0, act_full, [(PS[0:120, 0, t * P:(t + 1) * P], pr_c[:, t, :]) for t in range(TT)])
            pe.wait_ge(slot_free[0], 1)
            for t, s in ((0, 1), (1, 0)):
                pe.wait_ge(slot_free[s], 1)
                pe.sem_inc(slot_free[s], -1)
                pe.matmul(PS[:, 2 * s, :], prT_c[0:120, t, :], bd[0:120, :], start=True, stop=True)
                pe.matmul(PS[:, 2 * s + 1, 0:8], prT_c[0:120, t, :], hmask[0:120, :], start=True,
                          stop=True).then_inc(dve_full[s], 1)
            pe.wait_ge(src_ready, 1)
            pe.sem_inc(src_ready, -1)
            pe.wait_ge(slot_free[1], 1)
            pe.sem_inc(slot_free[1], -1)
            for b in range(4):
                last = pe.matmul(PS[:, 2, 0:S], ones[:, :], convT[:, b, :], start=b == 0, stop=b == 3)
            last.then_inc(dve_full[1], 1)

            def score2(u, r):
                w, g, t = u // 4, u // 2 % 2, u % 2
                rows = slice(HD * g, HD * g + HD)
                return [(qk2T[rows, r, t * P:(t + 1) * P], qk2T[rows, 4 + w, :])]

            pe.wait_ge(vals_ready, 1)
            pe.sem_inc(vals_ready, -1)
            attention(8, score2, value=lambda u, s, r: [(ps2(s)[:, r * 65:(r + 1) * 65],
                                                         lambda st: vaug[:, st, u // 2, :])])
            pe.wait_ge(src_ready, 1)
            pe.sem_inc(src_ready, -1)
            for t in range(TT):
                transposes(t, act_full, [(ps2(t)[:, k * P:(k + 1) * P], o_all[:, t, k * P:(k + 1) * P])
                                         for k in range(4)])
            evacuated()
            loop2(4, rows_by_chunk, dve_full)
            to_xT(tmp1)
            loop2(4, chunk_by_cols, act_full)
            to_xT(o_all)
            loop2(4, chunk_by_cols, act_full)
            loop2(4, rows_by_chunk, act_full)
            evacuated()

            def score3(t, r):
                return [(qxT[:, 2 * r + b, t * P:(t + 1) * P], kxT[:, 2 * r + b, :]) for b in range(2)]

            def value3(t, s, r):
                return [(PS[:, 4 + t, r:r + 1], lambda st: ones[:, 0:1]),
                        (ps2(s)[:, r * S:(r + 1) * S], lambda st: vx[:, st, r * S:(r + 1) * S])]

            attention(TT, score3, value=value3)
            to_xT(o_all)
            loop2(4, rows_by_chunk, dve_full)
            to_xT(tmp1)
            loop2(NFB, chunk_by_cols, act_full)
            pe.wait_ge(ffn_ready, 1)
            pe.sem_inc(ffn_ready, -1)
            for c in range(NFB // 2):
                s = c % 2
                pe.wait_ge(chunk_in[s], 16)
                pe.sem_inc(chunk_in[s], -16)
                for b in range(2):
                    for t in range(TT):
                        for q in range(2):
                            last = pe.matmul(acc[:, t, q * 512:(q + 1) * 512], ffT[:, 2 * c + b, t * P:(t + 1) * P],
                                             ring[:, s, b * D + q * 512:b * D + (q + 1) * 512],
                                             start=c + b == 0, stop=c + b == NFB // 2, skip_group_check=True)
                if c == NFB // 2 - 1:
                    last.then_inc(acc_ready, 1)
                else:
                    last.then_inc(chunk_free[s], 2)

        @block.scalar
        def _(act):
            def high(s, q):
                if q == 0:
                    act.wait_ge(chunk_in[s], 16)
                    act.sem_inc(chunk_in[s], -16)
                act.wait_ge(parts_free[q], 1)
                act.sem_inc(parts_free[q], -1)
                act.activation(wh[:, q, :], ring[:, s, q * QW:(q + 1) * QW], ACT.Copy).then_inc(high_ready[q], 1)

            def high_parts(n, between=None, result=None, peel=0):
                for q in range(4):
                    high(0, q)
                if between:
                    between()

                def chunk(c, s):
                    for q in range(3):
                        high(s, q)
                    if result:
                        result(c - 1, 1 - s)
                    high(s, 3)

                if peel:
                    chunk(1, 1)
                    chunk(2, 0)
                with act.Fori(peel, n // 2 - 1) as i:
                    chunk(2 * i + 1, 1)
                    chunk(2 * i + 2, 0)
                chunk(n - 1, 1)
                if result:
                    result(n - 1, 1)

            def evac(s, dst, src, parts=None):
                act.wait_ge(act_full[s], 1)
                act.sem_inc(act_full[s], -1)
                if parts is not None:
                    act.sem_inc(parts_free[3], 1)
                act.activation(dst, src, ACT.Copy).then_inc(slot_free[s], 1)

            def to_xT(nk=KB, k0=0):
                for t in range(TT):
                    act.wait_ge(act_full[t], 1)
                    act.sem_inc(act_full[t], -1)
                    act.activation(xh[:, k0:k0 + nk, t * P:(t + 1) * P],
                                   ps2(t)[:, 0:nk * P].rearrange("p (k n) -> p k n", k=nk),
                                   ACT.Copy).then_inc(xh_ready[t], 1)

            def halves(s):
                return PS[:, 2 * s:2 * s + 2, 0:CW]

            def attention(units, scale, sink=lambda u: False):
                n = [0]

                def slot():
                    n[0] += 1
                    return (n[0] - 1) % 2

                slot()
                for u in range(units):
                    if u + 1 < units:
                        slot()
                    act.wait_ge(shifted_ready, 1)
                    act.sem_inc(shifted_ready, -1)
                    act.activation(prb[:, u % 2, :, :], shf[:, u % 2, :, :], ACT.Exp,
                                   scale=scale(u)).then_inc(probs_ready, 1)
                    if sink(u):
                        act.wait_ge(sinkarg_ready, 1)
                        act.sem_inc(sinkarg_ready, -1)
                        act.activation(esk[:, u % 2, :], snk[:, u % 2, :], ACT.Exp).then_inc(sinkexp_ready, 1)
                    s = slot()
                    evac(s, prT[:, u % 2, :, :], ps2(s).rearrange("p (a b) -> p a b", a=8))
                    slot()

            act.dma_start(h[:, :, :], A["x"][0].rearrange("(t p) d -> p t d", p=P)).then_inc(x_in, 16)
            act.dma_start(qkg[:, :, :], A["qk_g"].partition_broadcast(P)).then_inc(consts_in[20], 16)
            act.dma_start(sinks[:, :, :], A["sink"].partition_broadcast(P)).then_inc(consts_in[21], 16)
            for q in range(4):
                act.sem_inc(parts_free[q], 1)
            with act.Fori(0, DEPTH):
                high_parts(N_IN, to_xT)
                for ab in (1, 0):
                    for t in range(TT):
                        evac(t, qkT[:, ab, 0:5, t * P:(t + 1) * P],
                             ps2(t)[:, 0:640].rearrange("p (k n) -> p k n", k=5))
                attention(8, lambda u: SQ if u < 4 else 1.0, lambda u: u >= 4)
                high_parts(N_O, to_xT)
                high_parts(N_WQ, to_xT, lambda c, s: evac(0, qTc[:, :, :], halves(0), s))

                def expert(c, s, j):
                    act.wait_ge(act_full[j], 1)
                    act.sem_inc(act_full[j], -1)
                    act.sem_inc(parts_free[2 * j + 1], 1)
                    act.activation(arena[:, bass.ts(2 * c + j, S)], PS[:, 2 * j, 0:S],
                                   ACT.Gelu).then_inc(slot_free[j], 1)

                def experts(c, s):
                    high(s, 0)
                    expert(c - 1, 1 - s, 0)
                    high(s, 1)
                    high(s, 2)
                    expert(c - 1, 1 - s, 1)
                    high(s, 3)

                for q in range(4):
                    high(0, q)
                early = TAIL // (4 * S)
                experts(1, 1)
                experts(2, 0)
                with act.Fori(1, early) as i:
                    experts(2 * i + 1, 1)
                    experts(2 * i + 2, 0)
                act.wait_ge(routing_done, 1)
                act.sem_inc(routing_done, -1)
                with act.Fori(early, NPAIR // 2 - 1) as i:
                    experts(2 * i + 1, 1)
                    experts(2 * i + 2, 0)
                experts(NPAIR - 1, 1)
                expert(NPAIR - 1, 1, 0)
                expert(NPAIR - 1, 1, 1)
                act.drain().then_inc(gelu_done, 1)
                act.wait_ge(smarg_ready, 1)
                act.sem_inc(smarg_ready, -1)
                act.activation(sel[:, 2, :, :], sel[:, 2, :, :], ACT.Exp).then_inc(smexp_ready, 1)
                for s in (0, 1):
                    act.sem_inc(gates_used[s], 1)
                with act.Fori(0, S // 8):
                    for s in (0, 1):
                        act.wait_ge(act_full[s], 1)
                        act.sem_inc(act_full[s], -1)
                        act.sem_inc(oneh_used[s], 1)
                        act.wait_ge(gates_used[s], 1)
                        act.sem_inc(gates_used[s], -1)
                        act.activation(gst[:, s, :], PS[:, 2 * s, :], ACT.Copy).then_inc(act_own, 1)
                        act.wait_ge(act_own, 1)
                        act.sem_inc(act_own, -1)
                        act.sem_inc(gates_ready[s], 1)
                        act.sem_inc(slot_free[s], 1)
                for s in (0, 1):
                    act.wait_ge(gates_used[s], 1)
                    act.sem_inc(gates_used[s], -1)
                act.sem_inc(gates_done, 1)
                high_parts(NPAIR)
            def to_xT_and_trig():
                to_xT()
                act.wait_ge(ang_ready, 1)
                act.sem_inc(ang_ready, -1)
                act.activation(angs[:, 6, :], angs[:, 2, :], ACT.Sin)
                act.activation(angs[:, 7, :], angs[:, 3, :], ACT.Sin).then_inc(trig_ready, 1)

            high_parts(N_CONV + N_PROJ2, to_xT_and_trig)
            act.wait_ge(gate_arg, 1)
            act.sem_inc(gate_arg, -1)
            act.activation(gate[:, :, :], gate[:, :, :], ACT.Exp, scale=-1.0).then_inc(gate_exp, 1)
            for t in range(TT):
                evac(t, kcvT[:, :, t * P:(t + 1) * P], ps2(t)[:, 0:2 * P].rearrange("p (k n) -> p k n", k=2))
            act.drain().then_inc(evac_done, 1)
            for kv in range(2):
                act.wait_ge(act_full[kv], 1)
                act.sem_inc(act_full[kv], -1)
                act.sem_inc(chunk_free[1], 2)
                act.activation(hidT[:, kv, :, :], PS[:, 2 * kv:2 * kv + 2, 0:2 * NCMP],
                               ACT.Silu).then_inc(slot_free[kv], 1)
            act.drain().then_inc(evac_done, 1)
            for t in range(TT):
                evac(t, qk2T[:, :, t * P:(t + 1) * P], ps2(t)[:, 0:768].rearrange("p (k n) -> p k n", k=6))
            act.wait_ge(act_full[0], 1)
            act.sem_inc(act_full[0], -1)
            act.activation(kcT[0:HD, 0:NCMP], PS[0:HD, 0, 0:NCMP], ACT.Copy)
            act.activation(kcT[HD:P, NCMP:2 * NCMP], PS[HD:P, 0, 0:NCMP], ACT.Copy).then_inc(slot_free[0], 1)
            act.wait_ge(shifted_ready, 1)
            act.sem_inc(shifted_ready, -1)
            act.activation(pr_c[:, :, :], sc_c[:, :, :], ACT.Exp).then_inc(cmp_exp, 1)
            evac(0, prT_c[0:120, :, :], PS[0:120, 0, 0:2 * P].rearrange("p (t n) -> p t n", t=TT))
            act.wait_ge(var2_ready, 1)
            act.sem_inc(var2_ready, -1)
            act.activation(ss[:, :], ss[:, :], ACT.Sqrt).then_inc(std2_ready, 1)
            attention(8, lambda u: 1.0)
            high_parts(4, lambda: to_xT(nk=4, k0=4))
            high_parts(4, to_xT, lambda c, s: evac(s, qxT[:, bass.ds(2 * c, 2), :], halves(s), s))
            high_parts(4, to_xT, lambda c, s: evac(s, kxT[:, bass.ds(2 * c, 2), :], halves(s), s))
            high_parts(4, None, lambda c, s: evac(s, vx[:, :, bass.ds(CW * c, CW)], halves(s), s))
            attention(TT, lambda u: 1.0 / 16)
            high_parts(4, to_xT)

            def silu(c, s):
                act.wait_ge(act_full[s], 1)
                act.sem_inc(act_full[s], -1)
                act.sem_inc(parts_free[3], 1)
                act.wait_ge(act_used, 1)
                act.sem_inc(act_used, -1)
                act.activation(sil[:, s, :], PS[:, 2 * s, 0:S], ACT.Silu).then_inc(silu_done, 1)

            high_parts(NFB, to_xT, silu, peel=1)

        @block.vector
        def _(dve):
            def own(ins):
                ins.then_inc(dve_own, 1)
                dve.wait_ge(dve_own, 1)
                dve.sem_inc(dve_own, -1)

            def bc(ap, *shape):
                return ap.to_broadcast([P, *shape])

            def power(n, scale, eps, sums):
                dve.tensor_scalar(ve[:, 0:n], sums, scale, eps, MUL, ADD).then_inc(var_ready, 1)
                dve.wait_ge(rstd_ready, 1)
                dve.sem_inc(rstd_ready, -1)

            def layer_norm(src, dst, at):
                for t in range(TT):
                    for c in range(2):
                        dve.bn_stats(stats[:, t, c, :], src[:, t, c * 512:(c + 1) * 512])
                own(dve.engine_nop())
                for t in range(TT):
                    dve.bn_aggr(mv[:, t, :], stats[:, t, :, :])
                own(dve.engine_nop())
                power(TT, 1.0, 1e-5, mv[:, :, 1])
                for t in range(TT):
                    dve.tensor_scalar(tmp2[:, t, :], src[:, t, :], mv[:, t, 0:1], rstd[:, t:t + 1], SUB, MUL)
                dve.wait_ge(gain_in[2 * at], 16)
                dve.sem_inc(gain_in[2 * at], -16)
                dve.wait_ge(gain_in[2 * at + 1], 16)
                dve.sem_inc(gain_in[2 * at + 1], -16)
                own(dve.engine_nop())
                own(dve.tensor_tensor(tmp2[:, :, :], tmp2[:, :, :], bc((gains0, gains1)[at][:, 0, :].unsqueeze(1), TT, D),
                                      MUL))
                own(dve.tensor_tensor(dst[:, :, :], tmp2[:, :, :], bc((gains0, gains1)[at][:, 1, :].unsqueeze(1), TT, D),
                                      ADD))
                dve.sem_inc(gain_free[at], 1)

            def rms_norm(src, dst, at, width=D):
                for t in range(TT):
                    dve.tensor_tensor_reduce(out=tmp2[:, t, 0:width], in0=src[:, t, 0:width], in1=src[:, t, 0:width],
                                             scale=1.0, scalar=0.0, op0=MUL, op1=ADD, accum_out=mv[:, t, 0:1])
                own(dve.engine_nop())
                power(TT, 1.0 / width, 1e-6, mv[:, :, 0])
                dve.wait_ge(gain_in[2 * at], 16)
                dve.sem_inc(gain_in[2 * at], -16)
                for t in range(TT):
                    dve.scalar_tensor_tensor(dst[:, t, 0:width], src[:, t, 0:width], rstd[:, t:t + 1],
                                             (gains0, gains2)[at][:, 0, 0:width], MUL, MUL)
                own(dve.engine_nop())
                dve.sem_inc(gain_free[at], 1)

            def residual_rms(src, at):
                rms_norm(src, tmp1, at)
                own(dve.tensor_tensor(h[:, :, :], h[:, :, :], tmp1[:, :, :], ADD))

            def take_rows(s):
                dve.wait_ge(dve_full[s], 1)
                dve.sem_inc(dve_full[s], -1)
                dve.sem_inc(parts_free[3], 1)

            def low(s, q, freed=1):
                dve.wait_ge(high_ready[q], 1)
                dve.sem_inc(high_ready[q], -1)
                part = dve.tensor_tensor(wl[:, q, :], ring[:, s, q * QW:(q + 1) * QW],
                                         wh[:, q, :].bitcast(F32), SUB)
                if q < 3:
                    part.then_inc(parts_ready[q], 1)
                else:
                    own(part)
                    dve.sem_inc(parts_ready[3], 1)
                    dve.sem_inc(chunk_free[s], freed)

            def low_parts(n):
                with dve.Fori(0, n // 2):
                    for s in (0, 1):
                        low(s, 3)

            def low_xT(nk=KB, k0=0):
                for t in range(TT):
                    dve.wait_ge(xh_ready[t], 1)
                    dve.sem_inc(xh_ready[t], -1)
                    dve.tensor_tensor(xl[:, k0:k0 + nk, t * P:(t + 1) * P],
                                      ps2(t)[:, 0:nk * P].rearrange("p (k n) -> p k n", k=nk),
                                      xh[:, k0:k0 + nk, t * P:(t + 1) * P].bitcast(F32), SUB
                                      ).then_inc(slot_free[t], 1)

            def rope(x, y, cos, sin, a, f, t1, t2):
                n, nh = x.shape[0], x.shape[1]
                dve.tensor_tensor(t1, x, cos.unsqueeze(1).to_broadcast([n, nh, HD]), MUL)
                xs = x.rearrange("p h (a b f) -> p h a b f", a=a, b=2)
                ys = t2.rearrange("p h (a b f) -> p h a b f", a=a, b=2)
                sn = sin.rearrange("p (a b f) -> p a b f", a=a, b=2)
                for b in range(2):
                    dve.tensor_tensor(ys[:, :, :, b, :], xs[:, :, :, 1 - b, :],
                                      sn[:, :, b, :].unsqueeze(1).to_broadcast([n, nh, a, f]), MUL)
                own(dve.engine_nop())
                dve.tensor_tensor(y, t1, t2, ADD)

            def attention(units, first, finish):
                n = [0]

                def slot():
                    n[0] += 1
                    return (n[0] - 1) % 2

                def scores(u):
                    s = slot()
                    dve.wait_ge(dve_full[s], 1)
                    dve.sem_inc(dve_full[s], -1)
                    first(u, s)

                scores(0)
                for u in range(units):
                    if u + 1 < units:
                        scores(u + 1)
                    slot()
                    s = slot()
                    dve.wait_ge(dve_full[s], 1)
                    dve.sem_inc(dve_full[s], -1)
                    finish(u, s)

            def shift(u, s, biased=None, scale=1.0, sink=None):
                b = u % 2
                sc = ps2(s).rearrange("p (r n) -> p r n", r=4)
                if biased is None:
                    own(dve.tensor_reduce(mx[:, b, :], sc, AX.X, MAX))
                    own(dve.tensor_tensor(shf[:, b, :, :], sc, bc(mx[:, b, :].unsqueeze(2), 4, S), SUB))
                    dve.sem_inc(slot_free[s], 1)
                    dve.sem_inc(shifted_ready, 1)
                    return
                own(dve.scalar_tensor_tensor(shf[:, b, :, :], sc, scale, biased, MUL, ADD))
                dve.sem_inc(slot_free[s], 1)
                own(dve.tensor_reduce(mx[:, b, :], shf[:, b, :, :], AX.X, MAX))
                if sink is not None:
                    own(dve.tensor_tensor(mx[:, b, :], mx[:, b, :], sink, MAX))
                dve.tensor_tensor(shf[:, b, :, :], shf[:, b, :, :], bc(mx[:, b, :].unsqueeze(2), 4, S),
                                  SUB).then_inc(shifted_ready, 1)
                if sink is not None:
                    dve.tensor_tensor(snk[:, b, :], sink, mx[:, b, :], SUB).then_inc(sinkarg_ready, 1)

            dve.wait_ge(consts_dve, 1)
            dve.sem_inc(consts_dve, -1)
            for s in (0, 1):
                dve.sem_inc(slot_free[s], 1)
            for s in (0, 1):
                dve.sem_inc(gain_free[s], 1)
            dve.sem_inc(keys_free, 1)
            dve.wait_ge(x_in, 16)
            dve.sem_inc(x_in, -16)
            layer_norm(h, h, 0)
            for i in (20, 21):
                dve.wait_ge(consts_in[i], 16)
                dve.sem_inc(consts_in[i], -16)
            with dve.Fori(0, DEPTH) as l:
                dve.sem_inc(src_ready, 1)
                dve.sem_inc(arena_free, 1)
                low_xT()
                with dve.Fori(0, N_IN // 2) as i:
                    for s in (0, 1):
                        low(s, 3)
                        take_rows(s)
                        dve.tensor_copy(proj[:, :, bass.ds(512 * i + 256 * s, 256)],
                                        PS[:, 2 * s:2 * s + 2, 0:CW]
                                        ).then_inc(slot_free[s], 1)
                own(dve.engine_nop())
                dve.sem_inc(src_ready, 1)
                dve.wait_ge(rope_in, 16)
                dve.sem_inc(rope_in, -16)
                qk = proj[:, :, 0:640]
                sq = tmp1[:, :, 0:640]
                own(dve.tensor_tensor(sq, qk, qk, MUL))
                own(dve.tensor_reduce(ve[:, 0:20].rearrange("p (t h) -> p t h", t=TT),
                                      sq.rearrange("p t (h d) -> p t h d", d=HD), AX.X, ADD))
                power(20, 1.0 / HD, 1e-6, ve[:, 0:20])
                own(dve.tensor_copy(qsc[:, 0:2 * HD], qkg[:, l, :]))
                own(dve.tensor_copy(qsc[:, 2 * HD:2 * HD + 8], sinks[:, l, :]))
                for t in range(TT):
                    x = qk[:, t, :].rearrange("p (h d) -> p h d", d=HD)
                    own(dve.tensor_tensor(x, x, bc(rstd[:, 10 * t:10 * t + 10].unsqueeze(2), 10, HD), MUL))
                    dve.tensor_tensor(x[:, 0:8, :], x[:, 0:8, :], bc(qsc[:, 0:HD].unsqueeze(1), 8, HD), MUL)
                    own(dve.tensor_tensor(x[:, 8:10, :], x[:, 8:10, :],
                                          bc(qsc[:, HD:2 * HD].unsqueeze(1), 2, HD), MUL))
                    rope(x, qkr[:, t, :].rearrange("p (h d) -> p h d", d=HD), ropeA[:, 0, t, :], ropeA[:, 1, t, :],
                         2, 16, tmp1[:, t, 0:640].rearrange("p (h d) -> p h d", d=HD),
                         tmp2[:, t, 0:640].rearrange("p (h d) -> p h d", d=HD))
                own(dve.engine_nop())
                dve.sem_inc(src_ready, 1)
                for ab in range(2):
                    at = 640 if ab == 0 else 1408
                    dve.tensor_copy(vaug[:, :, 2 * ab:2 * ab + 2, 0:HD],
                                    proj[:, :, at:at + 128].rearrange("p t (g d) -> p t g d", g=2))
                own(dve.memset(vaug[:, :, :, HD:HD + 1], 1.0))
                dve.sem_inc(vals_ready, 1)
                dve.wait_ge(bias_in, 16)
                dve.sem_inc(bias_in, -16)

                def first(u, s):
                    ab, g, t = u // 4, u // 2 % 2, u % 2
                    if ab == 0:
                        shift(u, s)
                    else:
                        shift(u, s, biasB[:, t, 4 * g:4 * g + 4, :], SQ, qsc[:, 2 * HD + 4 * g:2 * HD + 4 * g + 4])

                def finish(u, s):
                    ab, g, t = u // 4, u // 2 % 2, u % 2
                    v = ps2(s)[:, 0:260].rearrange("p (r n) -> p r n", r=4)
                    if ab:
                        dve.wait_ge(sinkexp_ready, 1)
                        dve.sem_inc(sinkexp_ready, -1)
                        own(dve.tensor_tensor(den[:, u % 2, :], v[:, :, HD], esk[:, u % 2, :], ADD))
                        own(dve.reciprocal(den[:, u % 2, :], den[:, u % 2, :]))
                    else:
                        own(dve.reciprocal(den[:, u % 2, :], v[:, :, HD]))
                    o = o_all[:, t, 512 * ab + 256 * g:512 * ab + 256 * g + 256].rearrange("p (r d) -> p r d", r=4)
                    dve.tensor_tensor(o, v[:, :, 0:HD], bc(den[:, u % 2, :].unsqueeze(2), 4, HD),
                                      MUL).then_inc(slot_free[s], 1)

                attention(8, first, finish)
                own(dve.engine_nop())
                for ab in range(2):
                    o = o_all[:, :, 512 * ab:512 * ab + 512]
                    own(dve.tensor_tensor(tmp1[:, :, 0:512], o, o, MUL))
                    own(dve.tensor_reduce(ve[:, 0:16].rearrange("p (t h) -> p t h", t=TT),
                                          tmp1[:, :, 0:512].rearrange("p t (h d) -> p t h d", d=HD), AX.X, ADD))
                    power(16, 1.0 / HD, 1e-6, ve[:, 0:16])
                    for t in range(TT):
                        x = o[:, t, :].rearrange("p (h d) -> p h d", d=HD)
                        dve.tensor_tensor(x, x, bc(rstd[:, 8 * t:8 * t + 8].unsqueeze(2), 8, HD), MUL)
                    own(dve.engine_nop())
                dve.wait_ge(gain_in[2], 16)
                dve.sem_inc(gain_in[2], -16)
                own(dve.tensor_tensor(o_all[:, :, :], o_all[:, :, :], bc(gains1[:, 0, :].unsqueeze(1), TT, D), MUL))
                dve.sem_inc(gain_free[1], 1)
                dve.sem_inc(src_ready, 1)
                low_xT()
                with dve.Fori(0, N_O // 2) as i:
                    for s in (0, 1):
                        low(s, 3)
                        take_rows(s)
                        c = bass.ds(512 * i + 256 * s, 256)
                        dve.scalar_tensor_tensor(h[:, :, c], h[:, :, c], ALPHA,
                                                 PS[:, 2 * s:2 * s + 2, 0:CW], MUL,
                                                 ADD).then_inc(slot_free[s], 1)
                own(dve.engine_nop())
                layer_norm(h, h, 1)
                dve.sem_inc(src_ready, 1)
                low_xT()
                with dve.Fori(0, N_WQ // 2) as i:
                    for s in (0, 1):
                        low(s, 3)
                        dve.wait_ge(dve_full[1], 1)
                        dve.sem_inc(dve_full[1], -1)
                        own(dve.tensor_copy(scc[:, :, :], PS[:, 2, :].rearrange("p (a n) -> p a n", a=4)))
                        dve.sem_inc(slot_free[1], 1)
                        for a in range(4):
                            dve.max(s16c[:, a, 0:8], scc[:, a, :])
                        own(dve.engine_nop())
                        for a in range(4):
                            dve.max_index(i16c[:, a, 0:8], s16c[:, a, 0:8], scc[:, a, :])
                            dve.match_replace(scr[:, a, :], s16c[:, a, 0:8], scc[:, a, :], -3e38)
                        own(dve.engine_nop())
                        for a in range(4):
                            dve.max(s16c[:, a, 8:16], scr[:, a, :])
                        own(dve.engine_nop())
                        for a in range(4):
                            dve.max_index(i16c[:, a, 8:16], s16c[:, a, 8:16], scr[:, a, :])
                        own(dve.engine_nop())
                        c = 2 * i + s
                        dve.tensor_copy(s16[:, c, :], s16c[:, :, :].rearrange("p a k -> p (a k)"))
                        own(dve.tensor_copy(i16[:, c, :], i16c[:, :, :].rearrange("p a k -> p (a k)")))
                with dve.Fori(0, PH // 2) as cc:
                    for u in (0, 3):
                        c = 2 * cc + u // 3
                        sv = s16[:, c, :].rearrange("p (t a k) -> p t a k", t=TT, a=2)
                        iv = i16[:, c, :].rearrange("p (t a k) -> p t a k", t=TT, a=2)
                        for t in range(TT):
                            dve.tensor_tensor(cand[:, t, :].rearrange("p (i j) -> p i j", i=TOPK),
                                              bc(sv[:, t, 0, :].unsqueeze(2), TOPK, TOPK),
                                              bc(sv[:, t, 1, :].unsqueeze(1), TOPK, TOPK), ADD)
                        own(dve.engine_nop())
                        low(u % 2, 3)
                        for t in range(TT):
                            k = TOPK * t
                            own(dve.max(t16[:, k:k + 8], cand[:, t, :]))
                            dve.max_index(p16[:, k:k + 8], t16[:, k:k + 8], cand[:, t, :])
                            own(dve.match_replace(candr[:, t, :], t16[:, k:k + 8], cand[:, t, :], -3e38))
                            own(dve.max(t16[:, k + 8:k + 16], candr[:, t, :]))
                            own(dve.max_index(p16[:, k + 8:k + 16], t16[:, k + 8:k + 16], candr[:, t, :]))
                        low((u + 1) % 2, 3)
                        dve.tensor_scalar(pj[:, 0, :], p16[:, :], 4, None, ALU.logical_shift_right)
                        own(dve.tensor_scalar(pj[:, 1, :], p16[:, :], 15, None, ALU.bitwise_and))
                        own(dve.tensor_copy(pf[:, :, :], pj[:, :, :]))
                        for a in range(2):
                            own(dve.tensor_tensor(oneh[:, :, :], bc(iota16[:, :].unsqueeze(1), TT * TOPK, TOPK),
                                                  bc(pf[:, a, :].unsqueeze(2), TT * TOPK, TOPK), ALU.is_equal))
                            for t in range(TT):
                                x = oneh[:, TOPK * t:TOPK * t + TOPK, :]
                                dve.tensor_tensor(x, x, bc(iv[:, t, a, :].unsqueeze(1), TOPK, TOPK), MUL)
                            own(dve.engine_nop())
                            own(dve.tensor_reduce(sel[:, a, :, bass.ts(c, TOPK)],
                                                  oneh[:, :, :].rearrange("p (t k) j -> p t k j", t=TT), AX.X, ADD))
                        low((u + 2) % 2, 3)
                        for t in range(TT):
                            dve.tensor_scalar(sel[:, 2, t, bass.ts(c, TOPK)], t16[:, TOPK * t:TOPK * t + TOPK],
                                              t16[:, TOPK * t:TOPK * t + 1], None, SUB)
                        own(dve.engine_nop())
                dve.sem_inc(keys_free, 1)
                dve.sem_inc(routing_done, 1)
                dve.sem_inc(smarg_ready, 1)
                low_parts(NPAIR - 3 * PH)
                dve.wait_ge(smexp_ready, 1)
                dve.sem_inc(smexp_ready, -1)
                g3 = sel[:, 2, :, :].rearrange("p t (h k) -> p (t h) k", h=PH)
                own(dve.tensor_reduce(gsm[:, :], g3, AX.X, ADD))
                own(dve.reciprocal(gsm[:, :], gsm[:, :]))
                own(dve.tensor_tensor(g3, g3, bc(gsm[:, :].unsqueeze(2), TT * PH, TOPK), MUL))
                dve.sem_inc(src_ready, 1)
                for t in range(TT):
                    dve.wait_ge(dve_full[t], 1)
                    dve.sem_inc(dve_full[t], -1)
                    dve.tensor_copy(selT[:, :, t * P:(t + 1) * P],
                                    ps2(t)[:, 0:3 * P].rearrange("p (i n) -> p i n", i=3)).then_inc(slot_free[t], 1)
                own(dve.engine_nop())
                dve.wait_ge(gelu_done, 1)
                dve.sem_inc(gelu_done, -1)
                dve.sem_inc(choices_ready, 1)
                av = arena[:, :].rearrange("p (e n) -> p n e", n=S)

                def onehots(i, s):
                    at = 8 * i + 4 * s
                    dve.tensor_tensor(ohB[:, s, :, :], bc(iota[:, :].unsqueeze(1), 4, P),
                                      bc(selT[:, 1, bass.ds(at, 4)].unsqueeze(2), 4, P), ALU.is_equal)
                    for n in range(4):
                        last = dve.tensor_scalar(ohA[:, s, n, :], iota[:, :], selT[:, 0, bass.ds(at + n, 1)],
                                                 selT[:, 2, bass.ds(at + n, 1)], ALU.is_equal, MUL)
                    last.then_inc(oneh_ready, 1)

                onehots(0, 0)
                onehots(0, 1)
                with dve.Fori(1, S // 8) as i:
                    for s in (0, 1):
                        dve.wait_ge(oneh_used[s], 1)
                        dve.sem_inc(oneh_used[s], -1)
                        onehots(i, s)
                for s in (0, 1):
                    dve.wait_ge(oneh_used[s], 1)
                    dve.sem_inc(oneh_used[s], -1)
                dve.wait_ge(gates_done, 1)
                dve.sem_inc(gates_done, -1)

                def stage(c, j):
                    w = arena[:, bass.ts(2 * c + j, S)]
                    own(dve.tensor_copy(wst[0][:, j, :], w))
                    dve.tensor_tensor(wst[1][:, j, :], w, wst[0][:, j, :].bitcast(F32),
                                      SUB).then_inc(wst_ready[j], 1)

                def weights(c, s):
                    for j in range(2):
                        dve.wait_ge(wst_used[j], 1)
                        dve.sem_inc(wst_used[j], -1)
                        dve.sem_inc(parts_free[2 * j + 1], 1)
                        stage(c, j)
                        low(s, 2 * j)
                        low(s, 2 * j + 1, 2)

                for j in range(2):
                    stage(0, j)
                    low(0, 2 * j)
                    low(0, 2 * j + 1, 2)
                with dve.Fori(0, NPAIR // 2 - 1) as i:
                    weights(2 * i + 1, 1)
                    weights(2 * i + 2, 0)
                weights(NPAIR - 1, 1)
                for j in range(2):
                    dve.wait_ge(wst_used[j], 1)
                    dve.sem_inc(wst_used[j], -1)
                    dve.sem_inc(parts_free[2 * j + 1], 1)
                dve.wait_ge(acc_ready, 1)
                dve.sem_inc(acc_ready, -1)
                layer_norm(acc, h, 0)

            dve.sem_inc(arena_free, 1)
            dve.sem_inc(arena_free2, 1)
            rms_norm(h, tmp1, 1)
            dve.sem_inc(src_ready, 1)
            low_xT()
            for i in range(9):
                dve.wait_ge(consts_in[i], 16)
            own(dve.tensor_copy(posv[:, :], pos_f[:, :].bitcast(I32)))
            a3 = angs[:, :, :].rearrange("p q (a f) -> p q a f", a=3)
            own(dve.tensor_tensor(a3[:, 0, :, :], bc(posv[:, :].unsqueeze(2), 3, 32),
                                  bc(invf[:, :].unsqueeze(1), 3, 32), MUL))
            magic = 1.5 * 2.0 ** 23
            own(dve.tensor_scalar(angs[:, 1, :], angs[:, 0, :], 1 / (2 * math.pi), magic, MUL, ADD))
            own(dve.tensor_scalar(angs[:, 1, :], angs[:, 1, :], magic, None, SUB))
            c1 = 6.28125
            c2 = round((2 * math.pi - c1) * 2 ** 20) / 2 ** 20
            c3 = 2 * math.pi - c1 - c2
            for at, (src, c) in enumerate(((0, c1), (2, c2), (3, c3))):
                own(dve.scalar_tensor_tensor(angs[:, 2 + at, :], angs[:, 1, :], -c, angs[:, src, :], MUL, ADD))
            pi = float(np.float32(3.1415925))
            own(dve.tensor_scalar(angs[:, 2, :], angs[:, 4, :], pi, -pi, ALU.min, MAX))
            own(dve.tensor_scalar(angs[:, 3, :], angs[:, 4, :], math.pi / 2, None, ADD))
            own(dve.tensor_scalar(angs[:, 5, :], angs[:, 3, :], math.pi, -2 * math.pi, ALU.is_gt, MUL))
            own(dve.tensor_tensor(angs[:, 3, :], angs[:, 3, :], angs[:, 5, :], ADD))
            own(dve.tensor_scalar(angs[:, 3, :], angs[:, 3, :], pi, -pi, ALU.min, MAX))
            dve.sem_inc(ang_ready, 1)
            dve.wait_ge(trig_ready, 1)
            dve.sem_inc(trig_ready, -1)
            for half in range(2):
                c = slice(32 * half, 32 * half + 32)
                dve.tensor_copy(rope2[:, 0, :, c], a3[:, 7, :, :])
                dve.tensor_scalar(rope2[:, 1, :, c], a3[:, 6, :, :], 1.0 if half else -1.0, None, MUL)
            own(dve.engine_nop())
            with dve.Fori(0, N_CONV // 2) as i:
                for s in (0, 1):
                    low(s, 3)
                    take_rows(s)
                    dve.tensor_copy(convT[:, bass.ds(4 * i + 2 * s, 2), :],
                                    PS[:, 2 * s:2 * s + 2, 0:S]).then_inc(slot_free[s], 1)
            with dve.Fori(0, (N_PROJ2 - 2) // 2) as i:
                for s in (0, 1):
                    low(s, 3)
                    take_rows(s)
                    dve.tensor_copy(proj2[:, :, bass.ds(512 * i + 256 * s, 256)],
                                    PS[:, 2 * s:2 * s + 2, 0:CW]).then_inc(slot_free[s], 1)
            for s, w in ((0, CW), (1, 24)):
                low(s, 3)
                take_rows(s)
                dve.tensor_copy(proj2[:, :, 1024 + 256 * s:1024 + 256 * s + w],
                                PS[:, 2 * s:2 * s + 2, 0:w]
                                ).then_inc(slot_free[s], 1)
            own(dve.engine_nop())
            dve.sem_inc(src_ready, 1)
            own(dve.tensor_copy(gate[:, :, :], proj2[:, :, 1280:1304]))
            dve.sem_inc(gate_arg, 1)
            dve.wait_ge(gate_exp, 1)
            dve.sem_inc(gate_exp, -1)
            own(dve.tensor_scalar(gate[:, :, :], gate[:, :, :], 1.0, None, ADD))
            own(dve.reciprocal(gate[:, :, :], gate[:, :, :]))
            dve.memset(kcT[:, :], 0.0)
            own(dve.memset(kblk[:, :, :, :], 0.0))
            dve.wait_ge(evac_done, 1)
            dve.sem_inc(evac_done, -1)
            for kv in range(2):
                for g in range(2):
                    rows = slice(HD * g, HD * g + HD)
                    v = kcvT[rows, kv, :].rearrange("p (m j) -> p j m", j=16)
                    for jh in range(2):
                        dve.tensor_tensor(
                            kblk[rows, kv, 16 * jh:16 * jh + 16, NCMP * g:NCMP * g + NCMP], v[:, :, jh:jh + NCMP],
                            peT[rows, kv, 16 * jh:16 * jh + 16].unsqueeze(2).to_broadcast([HD, 16, NCMP]), ADD)
                own(dve.engine_nop())
                dve.sem_inc(kb_ready, 1)
            for t in range(TT):
                for at, to, nh in ((0, 0, 8), (768, 512, 2), (1024, 640, 2)):
                    rope(proj2[:, t, at:at + HD * nh].rearrange("p (h d) -> p h d", d=HD),
                         qkr2[:, t, to:to + HD * nh].rearrange("p (h d) -> p h d", d=HD),
                         rope2[:, 0, t, :], rope2[:, 1, t, :], 1, 32,
                         tmp1[:, t, to:to + HD * nh].rearrange("p (h d) -> p h d", d=HD),
                         tmp2[:, t, to:to + HD * nh].rearrange("p (h d) -> p h d", d=HD))
            own(dve.engine_nop())
            dve.sem_inc(src_ready, 1)
            for w, at in ((0, 896), (1, 1152)):
                dve.tensor_copy(vaug[:, :, 2 * w:2 * w + 2, 0:HD],
                                proj2[:, :, at:at + 128].rearrange("p t (g d) -> p t g d", g=2))
            own(dve.memset(vaug[:, :, :, HD:HD + 1], 1.0))
            dve.sem_inc(vals_ready, 1)
            own(dve.tensor_tensor(zT[:, :, :], convT[:, 4:8, :], convT[:, 8:12, :], MUL))
            for b in range(4):
                dve.tensor_scalar(convT[:, 4 + b, :], zT[:, b, :], convw[:, b, 2:3], None, MUL)
            own(dve.engine_nop())
            for lag in (1, 2):
                for b in range(4):
                    c = convT[:, 4 + b, lag:S]
                    dve.scalar_tensor_tensor(c, zT[:, b, 0:S - lag], convw[:, b, 2 - lag:3 - lag], c, MUL, ADD)
                own(dve.engine_nop())
            own(dve.tensor_tensor(zT[:, :, :], convT[:, 0:4, :], convT[:, 4:8, :], MUL))
            own(dve.tensor_tensor(convT[:, 0:4, :], zT[:, :, :], zT[:, :, :], MUL))
            dve.wait_ge(evac_done, 1)
            dve.sem_inc(evac_done, -1)
            for hb in range(2):
                dve.tensor_copy(hidx[:, hb, :].rearrange("p (g r n) -> p g r n", g=2, r=4),
                                hidT[:, 1, hb, :].rearrange("p (g n) -> p g n", g=2).unsqueeze(2)
                                .to_broadcast([P, 2, 4, NCMP]))
            own(dve.engine_nop())
            dve.sem_inc(kb_ready, 1)
            dve.wait_ge(dve_full[0], 1)
            dve.sem_inc(dve_full[0], -1)
            own(dve.tensor_copy(krow[0:NCMP, :], PS[0:NCMP, 0, 0:2 * HD]))
            dve.sem_inc(slot_free[0], 1)
            hv = lambda x: x[0:NCMP, 0:2 * HD].rearrange("p (h d) -> p h d", d=HD)
            rope(hv(krow), hv(kcmp), rope2[0:NCMP, 0, 2, :], rope2[0:NCMP, 1, 2, :], 1, 32,
                 hv(tmp1[:, 0, :]), hv(tmp2[:, 0, :]))
            own(dve.engine_nop())
            dve.sem_inc(src_ready, 1)
            dve.wait_ge(dve_full[1], 1)
            dve.sem_inc(dve_full[1], -1)
            own(dve.tensor_copy(v120[0:120, :], PS[0:120, 2, 0:HD]))
            dve.sem_inc(slot_free[1], 1)
            own(dve.tensor_tensor(bd[0:120, :].rearrange("p (h d) -> p h d", d=HD),
                                  v120[0:120, :].unsqueeze(1).to_broadcast([120, 8, HD]),
                                  hmask[0:120, :].unsqueeze(2).to_broadcast([120, 8, HD]), MUL))
            dve.wait_ge(dve_full[1], 1)
            dve.sem_inc(dve_full[1], -1)
            own(dve.tensor_scalar(sc_c[:, :, :], PS[:, 2, 0:240].rearrange("p (t n) -> p t n", t=TT), SQ, None, MUL))
            dve.sem_inc(slot_free[1], 1)
            for t in range(TT):
                x = sc_c[:, t, :].rearrange("p (h n) -> p h n", n=NCMP)
                own(dve.tensor_tensor(x, x, bc(cmpbias[:, t, :].unsqueeze(1), 8, NCMP), ADD))
                own(dve.tensor_reduce(mx_c[:, t, :], x, AX.X, MAX))
                own(dve.tensor_tensor(x, x, bc(mx_c[:, t, :].unsqueeze(2), 8, NCMP), SUB))
            dve.sem_inc(shifted_ready, 1)
            dve.wait_ge(cmp_exp, 1)
            dve.sem_inc(cmp_exp, -1)
            for t in range(TT):
                x = pr_c[:, t, :].rearrange("p (h n) -> p h n", n=NCMP)
                dve.tensor_tensor(x, x, bc(cmpmask[:, t, :].unsqueeze(1), 8, NCMP), MUL)
            own(dve.engine_nop())
            dve.sem_inc(pcT_ready, 1)
            gh = gate[:, :, :].rearrange("p t (h c) -> p t h c", c=3)
            for t, s in ((0, 1), (1, 0)):
                dve.wait_ge(dve_full[s], 1)
                dve.sem_inc(dve_full[s], -1)
                own(dve.tensor_scalar(dn_c[:, t, :], PS[:, 2 * s + 1, 0:8], 1e-30, None, MAX))
                own(dve.reciprocal(dn_c[:, t, :], dn_c[:, t, :]))
                own(dve.tensor_tensor(dn_c[:, t, :], dn_c[:, t, :], gh[:, t, :, 0], MUL))
                dve.tensor_tensor(o_all[:, t, 0:512].rearrange("p (h d) -> p h d", d=HD),
                                  PS[:, 2 * s, :].rearrange("p (h d) -> p h d", d=HD),
                                  bc(dn_c[:, t, :].unsqueeze(2), 8, HD), MUL).then_inc(slot_free[s], 1)
            own(dve.engine_nop())
            dve.sem_inc(src_ready, 1)
            dve.wait_ge(dve_full[1], 1)
            dve.sem_inc(dve_full[1], -1)
            own(dve.tensor_scalar(ss[:, :], PS[:, 2, 0:S], 1 / 512, 1e-6, MUL, ADD))
            dve.sem_inc(slot_free[1], 1)
            dve.sem_inc(var2_ready, 1)
            dve.wait_ge(std2_ready, 1)
            dve.sem_inc(std2_ready, -1)
            own(dve.reciprocal(ss[:, :], ss[:, :]))
            for b in range(4):
                dve.scalar_tensor_tensor(zT[:, b, :], zT[:, b, :], convw[:, b, 3:4], ss[:, :], MUL, MUL)
            own(dve.engine_nop())
            own(dve.tensor_copy(xh[:, 0:4, :], zT[:, :, :]))
            own(dve.tensor_tensor(xl[:, 0:4, :], zT[:, :, :], xh[:, 0:4, :].bitcast(F32), SUB))

            def finish2(u, s):
                w, g, t = u // 4, u // 2 % 2, u % 2
                v = ps2(s)[:, 0:260].rearrange("p (r n) -> p r n", r=4)
                own(dve.reciprocal(den[:, u % 2, :], v[:, :, HD]))
                own(dve.tensor_tensor(den[:, u % 2, :], den[:, u % 2, :], gh[:, t, 4 * g:4 * g + 4, 1 + w], MUL))
                x = tmp1[:, u % 2, 0:256].rearrange("p (r d) -> p r d", r=4)
                own(dve.tensor_tensor(x, v[:, :, 0:HD], bc(den[:, u % 2, :].unsqueeze(2), 4, HD), MUL))
                dve.sem_inc(slot_free[s], 1)
                o = o_all[:, t, 256 * g:256 * g + 256].rearrange("p (r d) -> p r d", r=4)
                own(dve.tensor_tensor(o, o, x, ADD))

            attention(8, lambda u, s: shift(u, s, bc(causal[:, u % 2, :].unsqueeze(1), 4, S), SQ), finish2)
            rms_norm(o_all, o_all, 0, 512)
            dve.sem_inc(src_ready, 1)
            low_xT(4, 4)

            def rows_to(dst):
                with dve.Fori(0, 2) as i:
                    for s in (0, 1):
                        low(s, 3)
                        take_rows(s)
                        dve.tensor_copy(dst[:, :, bass.ds(512 * i + 256 * s, 256)],
                                        PS[:, 2 * s:2 * s + 2, 0:CW]
                                        ).then_inc(slot_free[s], 1)
                own(dve.engine_nop())

            rows_to(o_all)
            residual_rms(o_all, 1)
            dve.sem_inc(arena_free2, 1)
            rms_norm(h, tmp1, 0)
            dve.sem_inc(src_ready, 1)
            low_xT()
            dve.wait_ge(mem_in, 16)
            rms_norm(memr, o_all, 1)
            low_parts(4)
            dve.sem_inc(src_ready, 1)
            low_xT()
            low_parts(8)

            def finish3(t, s):
                own(dve.reciprocal(den[:, t, :], PS[:, 4 + t, 0:4]))
                dve.tensor_tensor(o_all[:, t, :].rearrange("p (r d) -> p r d", r=4),
                                  ps2(s).rearrange("p (r d) -> p r d", r=4),
                                  bc(den[:, t, :].unsqueeze(2), 4, S), MUL).then_inc(slot_free[s], 1)

            attention(TT, shift, finish3)
            own(dve.engine_nop())
            dve.sem_inc(src_ready, 1)
            low_xT()
            rows_to(o_all)
            residual_rms(o_all, 0)
            rms_norm(h, tmp1, 1)
            dve.sem_inc(src_ready, 1)
            low_xT()
            dve.sem_inc(act_used, 2)
            with dve.Fori(0, NFB // 2) as i:
                for s in (0, 1):
                    low(s, 3)
                    dve.wait_ge(silu_done, 1)
                    dve.sem_inc(silu_done, -1)
                    dve.tensor_tensor(ffT[:, 2 * i + s, :], sil[:, s, :], PS[:, 2 * s + 1, 0:S],
                                      MUL).then_inc(slot_free[s], 1)
                    own(dve.engine_nop())
                    dve.sem_inc(act_used, 1)
            dve.sem_inc(ffn_ready, 1)
            dve.wait_ge(acc_ready, 1)
            dve.sem_inc(acc_ready, -1)
            own(dve.tensor_copy(o_all[:, :, :], acc[:, :, :]))
            residual_rms(o_all, 0)
            dve.sem_inc(out_ready, 1)


def by_chunk(w):
    n = w.shape[-1]
    return w.reshape(KB, P, n // CW, CW).transpose(2, 1, 0, 3).reshape(n // CW, P, CHUNK)


def rows_of_tiles(a):
    return np.ascontiguousarray(a.reshape(TT, P, *a.shape[1:]).swapaxes(0, 1))


def shape_constants():
    f = np.float32
    t = np.arange(S)
    dist = np.abs(t[:, None] - t[None, :])
    slopes = (2.0 ** (-(np.arange(1, 9, dtype=f) * 8.0 / 8))).astype(f)
    bias = np.where(dist[:, None, :] <= 128, -(slopes[None, :, None] * dist[:, None, :].astype(f)), f(NEG))
    inv = (f(10000.0) ** (-np.arange(16, dtype=f) / f(16))).astype(f)
    pos = np.stack([t // 64, t % 64], -1).astype(f)
    ang = (pos[:, :, None] * inv).astype(f)
    cos = np.stack([np.cos(ang)] * 2, 2).reshape(S, HD)
    sin = np.stack([-np.sin(ang), np.sin(ang)], 2).reshape(S, HD)
    valid = (np.arange(NCMP)[None, :] * 16 + CMPJ - 1) <= t[:, None]
    head = np.zeros((P, 8), f)
    head[np.arange(120), np.arange(120) // NCMP] = 1.0
    return {
        "c_biasB": rows_of_tiles(bias.astype(f)),
        "c_ropeA": np.ascontiguousarray(
            np.stack([rows_of_tiles(cos), rows_of_tiles(sin)], 1).astype(f)),
        "c_causal": rows_of_tiles(np.where(t[None, :] <= t[:, None], f(0), f(NEG))),
        "c_cmpbias": rows_of_tiles(np.where(valid, f(0), f(NEG))),
        "c_cmpmask": rows_of_tiles(valid.astype(f)),
        "c_hmask": head,
        "c_invf": (f(10000.0) ** (-np.arange(32, dtype=f) / f(32))).astype(f),
    }


def layout(x):
    a = dict(shape_constants())
    heads = lambda at: [at + HD * i + j for i in PERM for j in range(HD)]
    cols = heads(0) + list(range(512, 768)) + heads(768) + list(range(1280, 1536))
    w = x["w_in"][:, :, cols]
    a["w_in"] = np.stack([by_chunk(m) for m in w])
    a["w_o"] = np.stack([by_chunk(m) for m in x["w_o"]])
    a["peer_wq"] = np.stack([by_chunk(m) for m in x["peer_wq"]])
    a["peer_keys"] = x["peer_keys"].transpose(0, 4, 1, 2, 3).reshape(DEPTH, P, PH, 2 * NK)
    a["peer_u"] = x["peer_u"].reshape(DEPTH, NK, NPAIR, 2, KB, P).transpose(0, 2, 5, 3, 4, 1).reshape(
        DEPTH, NPAIR, P, CHUNK)
    a["peer_v"] = x["peer_v"].reshape(DEPTH, NK, NPAIR, CHUNK).transpose(0, 2, 1, 3)
    a["gn_g"] = np.concatenate([x["gn_a_g"], x["gn_b_g"]], 1)
    a["qk_g"] = np.concatenate([x["qn_g"], x["kn_g"]], 1)
    for n in ("x", "ln_in_g", "ln_in_b", "sink", "ln1_g", "ln1_b", "ln2_g", "ln2_b", "mem_2",
              "norm_mix_pre_2", "norm_attn_out_2", "norm_mix_post_2", "norm_x_pre_2", "norm_mem_2",
              "norm_x_post_2", "norm_ffn_pre_2", "norm_ffn_post_2"):
        a[n] = x[n]
    p = np.arange(P)
    a["pos_2"] = x["positions_2"][0][np.stack([p, P + p, CMPJ - 1 + 16 * np.minimum(p, NCMP - 1)], 1)]
    w = x["w_in_2"]
    cols = list(range(1536)) + heads(1536) + list(range(2048, w.shape[1]))
    wide = np.zeros((D, (N_CONV + N_PROJ2) * CW), w.dtype)
    wide[:, :len(cols)] = w[:, cols]
    a["w_in_2"] = by_chunk(wide)
    w1 = np.stack([x["w1_kc_2"], x["w1_vc_2"]]).reshape(2, 4, 8, HD, CW).transpose(0, 1, 3, 2, 4)
    a["w1_2"] = np.concatenate([w1, w1], 2).reshape(8, P, CHUNK)
    a["w2_2"] = np.stack([x["w2_kc_2"], x["w2_vc_2"]]).reshape(2, 2, P, HD).transpose(2, 0, 1, 3)
    pe = np.stack([x["pe_kc_2"], x["pe_vc_2"]]).transpose(2, 0, 1)
    a["pe_2"] = np.concatenate([pe, pe], 0)
    a["conv_2"] = np.concatenate([x["conv_w_2"], x["norm_conv_out_2"][None]], 0).reshape(4, 4, P).transpose(2, 1, 0)
    for n in ("w_out_2", "w_q_x_2", "w_kv_x_2", "w_o_x_2"):
        a[n] = by_chunk(x[n])
    w = x["w_gate_up_2"]
    a["w_gate_up_2"] = by_chunk(w.reshape(D, 2, NFB, P).transpose(0, 2, 1, 3).reshape(D, 2 * FF))
    a["w_down_2"] = x["w_down_2"].reshape(NFB // 2, 2, P, D).transpose(0, 2, 1, 3).reshape(NFB // 2, P, CHUNK)
    return {k: np.ascontiguousarray(v) for k, v in a.items()}


def kernel(**inputs):
    import concourse.bacc as bacc
    from concourse.bass_utils import run_bass_kernel_spmd

    arrays = layout({k: np.asarray(v) for k, v in inputs.items()})
    nc = bacc.Bacc("TRN2", target_bir_lowering=False, num_devices=1)
    aps = {k: nc.dram_tensor(f"in_{k}", v.shape, mybir.dt.from_np(v.dtype), kind="ExternalInput").ap()
           for k, v in arrays.items()}
    out = nc.dram_tensor("out", (1, S, D), mybir.dt.float32, kind="ExternalOutput").ap()
    build(nc, aps, out)
    r = run_bass_kernel_spmd(nc, [{f"in_{k}": v for k, v in arrays.items()}], core_ids=[0])
    return r.results[0]["out"]
```

```python
import math

import numpy as np
import concourse.bass as bass
from concourse import mybir
from contextlib import ExitStack

P = 128
D = 1024
S = 256
DEPTH = 2
KB = D // P
TT = S // P
HD = 64
CW = 256
CHUNK = KB * CW
N_IN, N_O, N_WQ = 6, 4, 8
NK = 128
QW = CHUNK // 4
NPAIR = NK // 2
PH, TOPK = 8, 16
N_CONV, N_PROJ2 = 6, 6
P2W = 1304
NCMP = 15
CMPJ = 32
FF = 2816
NFB = FF // P
XH = 4
ALPHA = (2.0 * DEPTH) ** 0.25
NEG = -1e30
ARENA = NK * S
TAIL = 26624
SQ = 0.125
PERM = [0, 4, 1, 5, 2, 6, 3, 7]


def build(nc, A, out):
    F32, U32, I32, F32R = mybir.dt.float32, mybir.dt.uint32, mybir.dt.int32, mybir.dt.float32r
    ALU, ACT, AX = mybir.AluOpType, mybir.ActivationFunctionType, mybir.AxisListType
    MUL, ADD, SUB, MAX = ALU.mult, ALU.add, ALU.subtract, ALU.max
    ctx = ExitStack()
    with ctx:
        def sb(name, shape, dt=F32):
            return ctx.enter_context(nc.sbuf_tensor(name, shape, dt))

        def sem(name):
            return ctx.enter_context(nc.semaphore(name))

        arena = sb("arena", [P, ARENA])

        def region(off, *shape):
            n = int(np.prod(shape))
            assert off + n <= ARENA
            v = arena[:, off:off + n]
            if len(shape) == 2:
                v = v.rearrange("p (a b) -> p a b", a=shape[0])
            if len(shape) == 3:
                v = v.rearrange("p (a b c) -> p a b c", a=shape[0], b=shape[1])
            if len(shape) == 4:
                v = v.rearrange("p (a b c d) -> p a b c d", a=shape[0], b=shape[1], c=shape[2])
            return v

        ring = sb("ring", [P, 2, CHUNK])
        h = sb("h", [P, TT, D])
        wh = sb("wh", [P, 4, QW], F32R)
        wl = sb("wl", [P, 4, QW], F32R)
        xh = sb("xh", [P, KB, S], F32R)
        xl = sb("xl", [P, KB, S], F32R)
        gains0 = sb("gains0", [P, 2, D])
        gains1 = region(4352, 2, D)
        gains2 = region(10240, 1, D)
        ident = sb("ident", [P, P])
        identa = sb("identa", [P, P])
        iota = sb("iota", [P, P])
        iota16 = sb("iota16", [P, TOPK])
        mhalf = sb("mhalf", [P, 1])
        ones = sb("ones", [P, P])
        qkg = sb("qkg", [P, DEPTH, 2 * HD])
        sinks = sb("sinks", [P, DEPTH, 8])
        ve2 = sb("ve2", [P, 20])
        rstd2 = sb("rstd2", [P, 20])
        ropeA = region(6400, 2, TT, HD)
        stats = sb("stats", [P, TT, 2, 6])
        mv = sb("mv", [P, TT, 2])
        ve = sb("ve", [P, 2 * TT * 8])
        rstd = sb("rstd", [P, 2 * TT * 8])
        peer_k = region(TAIL, PH, 2 * NK)
        qTc = region(31232, 2, 2, S)
        scc = [region(28672, 4, NK), region(29184, 4, NK)]
        scr = region(29696, 4, NK)
        s16 = region(30208, PH, 4 * TOPK)
        i16 = region(30720, PH, 4 * TOPK)
        s16c = sb("s16c", [P, 4, TOPK])
        i16c = sb("i16c", [P, 4, TOPK], U32)
        qsc = sb("qsc", [P, 2 * HD + 8])
        cand = peer_k[:, 0:2, :].rearrange("p t (i k) -> p t i k", i=1)[:, :, 0, :]
        candr = peer_k[:, 2:4, :].rearrange("p t (i k) -> p t i k", i=1)[:, :, 0, :]
        oneh = peer_k[:, 4:6, :].rearrange("p a b -> p (a b)").rearrange("p (a b) -> p a b", b=TOPK)
        t16 = sb("t16", [P, TT * TOPK])
        p16 = sb("p16", [P, TT * TOPK], U32)
        pj = sb("pj", [P, 2, TT * TOPK], U32)
        pf = sb("pf", [P, 2, TT * TOPK])
        sel = sb("sel", [P, 3, TT, PH * TOPK])
        selT = sb("selT", [P, 3, S])
        gsm = sb("gsm", [P, TT * PH])
        ohA = gains0[:, 0, :].rearrange("p (s n k) -> p s n k", s=2, n=4)
        ohB = gains0[:, 1, :].rearrange("p (s n k) -> p s n k", s=2, n=4)
        gst = sb("gst", [P, 2, 4 * NK])
        wst = [m[:, 0:2, :] for m in (xh, xl)]
        PS = ctx.enter_context(nc.psum_tensor("PS", [P, 8, 512], F32))

        def ps2(s):
            return PS[:, 2 * s:2 * s + 2, :].rearrange("p a b -> p (a b)")

        acc = PS[:, 4:8, :].rearrange("p (t c) n -> p t (c n)", t=TT)

        chunk_in = [sem(f"chunk_in{s}") for s in (0, 1)]
        high_ready = [sem(f"high_ready{q}") for q in range(4)]
        parts_ready = [sem(f"parts_ready{q}") for q in range(4)]
        parts_free = [sem(f"parts_free{q}") for q in range(4)]
        xh_ready = [sem(f"xh_ready{s}") for s in (0, 1)]
        chunk_free = [sem(f"chunk_free{s}") for s in (0, 1)]
        act_full = [sem(f"act_full{s}") for s in range(4)]
        dve_full = [sem(f"dve_full{s}") for s in range(4)]
        slot_free = [sem(f"slot_free{s}") for s in range(4)]
        src_ready = sem("src_ready")
        rotated_ready = sem("rotated_ready")
        scores_ready = sem("scores_ready")
        scores_used = sem("scores_used")
        var_ready = sem("var_ready")
        rstd_ready = sem("rstd_ready")
        gain_in = [sem(f"gain_in{s}") for s in range(4)]
        gain_free = [sem(f"gain_free{s}") for s in (0, 1)]
        consts_in = [sem(f"consts_in{i}") for i in range(24)]
        consts_dve, consts_pe = sem("consts_dve"), sem("consts_pe")
        keys_in, keys_free = sem("keys_in"), sem("keys_free")
        rope_in = sem("rope_in")
        bias_in = sem("bias_in")
        arena_free = sem("arena_free")
        mem_free = sem("mem_free")
        shifted_ready = sem("shifted_ready")
        probs_ready = sem("probs_ready")
        sinkarg_ready, sinkexp_ready = sem("sinkarg_ready"), sem("sinkexp_ready")
        vals_ready = sem("vals_ready")
        evac_done = sem("evac_done")
        oneh_ready = sem("oneh_ready")
        choices_ready = sem("choices_ready")
        gates_ready = [sem(f"gates_ready{s}") for s in (0, 1)]
        gates_used = [sem(f"gates_used{s}") for s in (0, 1)]
        oneh_used = [sem(f"oneh_used{s}") for s in (0, 1)]
        gates_done = sem("gates_done")
        routing_done = sem("routing_done")
        wst_ready = [sem(f"wst_ready{s}") for s in (0, 1)]
        wst_used = [sem(f"wst_used{s}") for s in (0, 1)]
        acc_ready = sem("acc_ready")
        gelu_done = sem("gelu_done")
        smarg_ready, smexp_ready = sem("smarg_ready"), sem("smexp_ready")
        mem_in = sem("mem_in")
        memgain_in = sem("memgain_in")
        ang_ready, trig_ready = sem("ang_ready"), sem("trig_ready")
        gate_arg, gate_exp = sem("gate_arg"), sem("gate_exp")
        kb_ready = sem("kb_ready")
        hid_ready = sem("hid_ready")
        pcT_ready, cmp_exp = sem("pcT_ready"), sem("cmp_exp")
        var2_ready, std2_ready = sem("var2_ready"), sem("std2_ready")
        silu_done, act_used = sem("silu_done"), sem("act_used")
        out_ready, out_done = sem("out_ready"), sem("out_done")
        x_in = sem("x_in")
        dve_own, act_own, pool_own = sem("dve_own"), sem("act_own"), sem("pool_own")

        proj = region(0, TT, 1536)
        qkr = region(3072, TT, 640)
        tmp1 = region(28672, TT, D)
        tmp2 = region(30720, TT, D)
        qkT = region(8448, 2, 6, S)
        vaug = region(11520, TT, 4, 65)
        biasB = region(12288, TT, 8, S)
        o_all = region(16384, TT, D)
        shf = region(18432, 2, 4, S)
        prb = region(20480, 2, 4, S)
        prT = region(22528, 2, 8, P)
        mx = region(24576, 2, 4)
        den = region(24584, 2, 4)
        snk = region(24600, 4, 4)
        esk = region(24616, 4, 4)
        mxn = region(24632, 2, 4)
        zT = region(0, 4, S)
        convT = region(1024, 12, S)
        proj2 = region(4096, TT, P2W)
        qkr2 = region(6704, TT, 768)
        kcvT = region(8240, 2, S)
        w2k = region(8752, 2, 2, HD)
        qk2T = region(26560, 6, S)
        causal = region(12288, TT, S)
        cmpbias = region(12800, TT, NCMP)
        cmpmask = region(12830, TT, NCMP)
        hmask = region(12860, 8)
        peT = region(12868, 2, CMPJ)
        convw = region(12932, 4, 4)
        rope2 = region(12948, 2, 3, HD)
        angs = region(13332, 8, 96)
        pos_f = region(14100, 3)
        invf = region(14103, 32)
        gate = region(14135, TT, 24)
        hid = region(28096, 2, CW)
        hidT = region(14183, 2, 2, 2 * NCMP)
        hidx = region(14303, 2, 120)
        kcmp = region(14543, 2 * HD)
        kcT = region(9144, 2 * NCMP)
        sc_c = region(14686, TT, 120)
        pr_c = region(14926, TT, 120)
        prT_c = region(15166, TT, P)
        mx_c = region(15422, TT, 8)
        dn_c = region(15438, TT, 8)
        bd = region(15454, 512)
        v120 = region(15966, HD)
        ss = region(16030, S)
        posv = region(16290, 3)
        krow = region(9008, 2 * HD)
        kblk = region(24640, 2, CMPJ, 2 * NCMP)
        memr = region(0, TT, D)
        gainm = region(24640, 1, D)[:, 0, :]
        qxT = region(4096, KB, S)
        kxT = region(6144, KB, S)
        vx = region(8192, TT, D)
        ffT = region(0, NFB, S)
        sil = region(6144, 2, S)

        def rope(engine, own, x, y, cos, sin, a, f, t1, t2):
            n, nh = x.shape[0], x.shape[1]
            engine.tensor_tensor(t1, x, cos.unsqueeze(1).to_broadcast([n, nh, HD]), MUL)
            xs = x.rearrange("p h (a b f) -> p h a b f", a=a, b=2)
            ys = t2.rearrange("p h (a b f) -> p h a b f", a=a, b=2)
            sn = sin.rearrange("p (a b f) -> p a b f", a=a, b=2)
            last = None
            for b in range(2):
                last = engine.tensor_tensor(ys[:, :, :, b, :], xs[:, :, :, 1 - b, :],
                                            sn[:, :, b, :].unsqueeze(1).to_broadcast([n, nh, a, f]), MUL)
            own(last)
            engine.tensor_tensor(y, t1, t2, ADD)

        block = ctx.enter_context(nc.Block())

        @block.sync
        def _(sp):
            def stream(src, n):
                with sp.Fori(0, n // 2) as i:
                    for s in (0, 1):
                        sp.wait_ge(chunk_free[s], 2)
                        sp.sem_inc(chunk_free[s], -2)
                        sp.dma_start(ring[:, s, :], src(2 * i + s)).then_inc(chunk_in[s], 16)

            def gain(at, *rows, block2=False):
                sp.wait_ge(gain_free[at], 1)
                sp.sem_inc(gain_free[at], -1)
                dst = (gains0, gains1, gains2)[at + block2 * at]
                for i, g in enumerate(rows):
                    sp.dma_start(dst[:, i, 0:g.shape[-1]],
                                 g.partition_broadcast(P)).then_inc(gain_in[2 * at + i], 16)

            for s in (0, 1):
                sp.sem_inc(chunk_free[s], 2)
            gain(0, A["ln_in_g"], A["ln_in_b"])
            with sp.Fori(0, DEPTH) as l:
                stream(lambda c: A["w_in"][l, c], N_IN)
                sp.wait_ge(arena_free, 1)
                sp.sem_inc(arena_free, -1)
                sp.dma_start(ropeA[:, :, :, :], A["c_ropeA"]).then_inc(rope_in, 16)
                gain(1, A["gn_g"][l])
                sp.dma_start(biasB[:, :, :, :], A["c_biasB"]).then_inc(bias_in, 16)
                sp.wait_ge(keys_free, 1)
                sp.sem_inc(keys_free, -1)
                sp.dma_start(peer_k[:, :, :], A["peer_keys"][l]).then_inc(keys_in, 16)
                stream(lambda c: A["w_o"][l, c], N_O)
                gain(1, A["ln1_g"][l], A["ln1_b"][l])
                stream(lambda c: A["peer_wq"][l, c], N_WQ)
                stream(lambda c: A["peer_u"][l, c], NPAIR)
                stream(lambda c: A["peer_v"][l, c], NPAIR)
                gain(0, A["ln2_g"][l], A["ln2_b"][l])
            stream(lambda c: A["w_in_2"][c], 2)
            sp.wait_ge(arena_free, 1)
            sp.sem_inc(arena_free, -1)
            gain(1, A["norm_mix_pre_2"], block2=True)
            for i, (dst, src) in enumerate((
                    (causal[:, :, :], A["c_causal"]), (cmpbias[:, :, :], A["c_cmpbias"]),
                    (cmpmask[:, :, :], A["c_cmpmask"]), (hmask[:, :], A["c_hmask"]),
                    (peT[:, :, :], A["pe_2"]), (convw[:, :, :], A["conv_2"]),
                    (w2k[:, :, :, :], A["w2_2"]), (invf[:, :], A["c_invf"].partition_broadcast(P)))):
                sp.dma_start(dst, src).then_inc(consts_in[i], 16)
            sp.dma_start(pos_f[:, :].bitcast(I32), A["pos_2"]).then_inc(consts_in[8], 16)
            stream(lambda c: A["w_in_2"][2 + c], N_CONV + N_PROJ2 - 2)
            gain(0, A["norm_attn_out_2"])
            stream(lambda c: A["w1_2"][c], 8)
            gain(1, A["norm_mix_post_2"], block2=True)
            stream(lambda c: A["w_out_2"][c], 4)
            gain(0, A["norm_x_pre_2"])
            stream(lambda c: A["w_q_x_2"][c], 4)
            stream(lambda c: A["w_kv_x_2"][c], 8)
            gain(0, A["norm_x_post_2"])
            stream(lambda c: A["w_o_x_2"][c], 4)
            gain(1, A["norm_ffn_pre_2"], block2=True)
            stream(lambda c: A["w_gate_up_2"][c], NFB)
            gain(0, A["norm_ffn_post_2"])
            stream(lambda c: A["w_down_2"][c], NFB // 2 - 1)
            sp.wait_ge(chunk_free[0], 2)
            sp.sem_inc(chunk_free[0], -2)
            sp.dma_start(ring[:, 0, :], A["w_down_2"][NFB // 2 - 1]).then_inc(chunk_in[0], 16)
            sp.wait_ge(out_ready, 1)
            sp.sem_inc(out_ready, -1)
            sp.dma_start(out.rearrange("b (t p) d -> p (b t) d", p=P), h[:, :, :]).then_inc(out_done, 16)
            sp.wait_ge(out_done, 16)

        @block.gpsimd
        def _(pool):
            def own(ins):
                ins.then_inc(pool_own, 1)
                pool.wait_ge(pool_own, 1)
                pool.sem_inc(pool_own, -1)

            own(pool.memset(mhalf[:, :], -0.5))
            own(pool.memset(ones[:, :], 1.0))
            own(pool.memset(ident[:, :], 0.0))
            own(pool.memset(identa[:, :], 0.0))
            for m, v in ((ident, 1.0), (identa, ALPHA)):
                own(pool.affine_select(out=m[:, :], in_=m[:, :], compare_op=ALU.not_equal, fill=v,
                                       base=0, pattern=[[-1, P]], channel_multiplier=1))
            own(pool.iota(iota[:, :], pattern=[[1, P]], base=0, channel_multiplier=0,
                          allow_small_or_imprecise_dtypes=True))
            own(pool.iota(iota16[:, :], pattern=[[1, TOPK]], base=0, channel_multiplier=0,
                          allow_small_or_imprecise_dtypes=True))
            pool.sem_inc(consts_dve, 1)
            pool.sem_inc(consts_pe, 1)

            def power(n, at=0):
                pool.wait_ge(var_ready, 1)
                pool.sem_inc(var_ready, -1)
                pool.tensor_tensor(rstd[:, at:at + n], ve[:, at:at + n], mhalf[:, :].to_broadcast([P, n]),
                                   ALU.pow).then_inc(rstd_ready, 1)

            power(TT)
            def low_parts(n):
                def chunk(s):
                    for q in range(3):
                        pool.wait_ge(high_ready[q], 1)
                        pool.sem_inc(high_ready[q], -1)
                        pool.tensor_tensor(wl[:, q, :], ring[:, s, q * QW:(q + 1) * QW],
                                           wh[:, q, :].bitcast(F32), SUB).then_inc(
                                               parts_ready[q] if q < 2 else pool_own, 1)
                    pool.wait_ge(pool_own, 1)
                    pool.sem_inc(pool_own, -1)
                    pool.sem_inc(parts_ready[2], 1)
                    pool.sem_inc(chunk_free[s], 1)

                with pool.Fori(0, n // 2):
                    for s in (0, 1):
                        chunk(s)
                if n % 2:
                    chunk(0)

            with pool.Fori(0, DEPTH):
                low_parts(N_IN)
                pool.wait_ge(var_ready, 1)
                pool.sem_inc(var_ready, -1)
                own(pool.tensor_tensor(rstd2[:, :], ve2[:, :], mhalf[:, :].to_broadcast([P, 20]), ALU.pow))
                pool.wait_ge(rope_in, 16)
                pool.sem_inc(rope_in, -16)
                for t in range(TT):
                    x = proj[:, t, 0:640].rearrange("p (h d) -> p h d", d=HD)
                    own(pool.tensor_tensor(x, x, rstd2[:, 10 * t:10 * t + 10].unsqueeze(2)
                                           .to_broadcast([P, 10, HD]), MUL))
                    pool.tensor_tensor(x[:, 0:8, :], x[:, 0:8, :],
                                       qsc[:, 0:HD].unsqueeze(1).to_broadcast([P, 8, HD]), MUL)
                    own(pool.tensor_tensor(x[:, 8:10, :], x[:, 8:10, :],
                                           qsc[:, HD:2 * HD].unsqueeze(1).to_broadcast([P, 2, HD]), MUL))
                    rope(pool, own, x, qkr[:, t, :].rearrange("p (h d) -> p h d", d=HD),
                         ropeA[:, 0, t, :], ropeA[:, 1, t, :], 2, 16,
                         tmp2[:, 0, 0:640].rearrange("p (h d) -> p h d", d=HD),
                         tmp2[:, 1, 0:640].rearrange("p (h d) -> p h d", d=HD))
                    own(pool.engine_nop())
                pool.sem_inc(rotated_ready, 1)
                power(16)
                power(16, 16)
                low_parts(N_O)
                power(TT)
                low_parts(N_WQ)
                low_parts(NPAIR)
                pool.wait_ge(choices_ready, 1)
                pool.sem_inc(choices_ready, -1)
                av = arena[:, :].rearrange("p (e n) -> p n e", n=S)
                with pool.Fori(0, S // 8) as i:
                    for s in (0, 1):
                        pool.wait_ge(gates_ready[s], 1)
                        pool.sem_inc(gates_ready[s], -1)
                        a = av[:, bass.ds(8 * i + 4 * s, 4), :]
                        pool.tensor_tensor(a, a, gst[:, s, :].rearrange("p (n e) -> p n e", n=4),
                                           MUL).then_inc(gates_used[s], 1)
                power(TT)
            power(TT)
            low_parts(N_CONV + N_PROJ2)
            pool.wait_ge(mem_free, 1)
            pool.sem_inc(mem_free, -1)
            pool.dma_start(memr[:, :, :], A["mem_2"][0].rearrange("(t p) d -> p t d", p=P)).then_inc(mem_in, 16)
            pool.dma_start(gainm[:, :], A["norm_mem_2"].partition_broadcast(P)).then_inc(memgain_in, 16)
            power(TT)
            power(TT)
            low_parts(4)
            power(TT)
            power(TT)
            low_parts(4)
            low_parts(8)
            low_parts(4)
            power(TT)
            power(TT)
            low_parts(NFB)
            low_parts(NFB // 2)
            power(TT)

        @block.tensor
        def _(pe):
            def evacuated():
                for s in (0, 1):
                    pe.wait_ge(slot_free[s], 1)

            def transposes(s, full, pairs):
                pe.wait_ge(slot_free[s], 1)
                pe.sem_inc(slot_free[s], -1)
                for dst, src in pairs:
                    n = src.shape[0]
                    last = pe.transpose(dst, src, ident[0:n, 0:n])
                last.then_inc(full[s], 1)

            def to_xT(src):
                for t in range(TT):
                    pe.wait_ge(src_ready, 1)
                    pe.sem_inc(src_ready, -1)
                    transposes(t, act_full, [(ps2(t)[:, k * P:(k + 1) * P], src[:, t, k * P:(k + 1) * P])
                                             for k in range(KB)])
                evacuated()

            def rows_by_chunk(s, full, width=CW):
                pe.wait_ge(slot_free[s], 1)
                pe.sem_inc(slot_free[s], -1)
                for q in range(4):
                    pe.wait_ge(parts_ready[q], 1)
                    pe.sem_inc(parts_ready[q], -1)
                    for t in range(TT):
                        for k in range(2):
                            for i, (x, w) in enumerate(((xh, wh), (xh, wl), (xl, wh))):
                                last = pe.matmul(PS[:, 2 * s + t, 0:width], x[:, 2 * q + k, t * P:(t + 1) * P],
                                                 w[:, q, k * CW:k * CW + width], start=q + k + i == 0,
                                                 stop=q + k + i == 6)
                    if q < 3:
                        last.then_inc(parts_free[q], 1)
                last.then_inc(full[s], 1)

            def chunk_by_cols(s, full):
                pe.wait_ge(slot_free[s], 1)
                pe.sem_inc(slot_free[s], -1)
                for q in range(4):
                    pe.wait_ge(parts_ready[q], 1)
                    pe.sem_inc(parts_ready[q], -1)
                    for b in range(2):
                        for k in range(2):
                            for i, (w, x) in enumerate(((wh, xh), (wh, xl), (wl, xh))):
                                last = pe.matmul(PS[:, 2 * s + b, 0:S],
                                                 w[:, q, k * CW + b * P:k * CW + (b + 1) * P],
                                                 x[:, 2 * q + k, :], start=q + k + i == 0, stop=q + k + i == 6)
                    if q < 3:
                        last.then_inc(parts_free[q], 1)
                last.then_inc(full[s], 1)

            def loop2(n, f, *a):
                with pe.Fori(0, n // 2):
                    for s in (0, 1):
                        f(s, *a)

            def weigh(begin=False, end=False):
                for j in range(2):
                    pe.wait_ge(wst_ready[j], 1)
                    pe.sem_inc(wst_ready[j], -1)
                    for c in range(2):
                        q = 2 * j + c
                        pe.wait_ge(parts_ready[q], 1)
                        pe.sem_inc(parts_ready[q], -1)
                        for t in range(TT):
                            for i, (x, w) in enumerate(((0, wh), (0, wl), (1, wh))):
                                last = pe.matmul(acc[:, t, c * 512:(c + 1) * 512],
                                                 wst[x][:, j, t * P:(t + 1) * P], w[:, q, :],
                                                 start=begin and j + i == 0, stop=end and j == 1 and i == 2)
                        if c == 0:
                            last.then_inc(parts_free[q], 1)
                    last.then_inc(wst_used[j], 1)

            def attention(units, score, value, turn=None):
                def scores(u):
                    s = u % 2
                    pe.wait_ge(slot_free[s], 1)
                    pe.sem_inc(slot_free[s], -1)
                    for r in range(4):
                        prods = score(u, r)
                        for i, (a, b) in enumerate(prods):
                            last = pe.matmul(ps2(s)[:, r * S:(r + 1) * S], a, b, start=i == 0,
                                             stop=i == len(prods) - 1)
                    last.then_inc(dve_full[s], 1)

                def turned(u):
                    pe.wait_ge(probs_ready, 1)
                    pe.sem_inc(probs_ready, -1)
                    transposes(2, act_full, [(ps2(2)[:, i * P:(i + 1) * P],
                                              prb[:, u % 2, i // 2, (i % 2) * P:(i % 2 + 1) * P])
                                             for i in range(8)])

                scores(0)
                scores(1)
                turned(0)
                for u in range(units):
                    second = turn and u + 2 == units // 2
                    if second:
                        turn()
                    elif u + 2 < units:
                        scores(u + 2)
                    if u + 1 < units:
                        turned(u + 1)
                    else:
                        pe.wait_ge(slot_free[2], 1)
                    pe.wait_ge(slot_free[3], 1)
                    pe.sem_inc(slot_free[3], -1)
                    for r in range(4):
                        for o, v in value(u, r):
                            for st in range(TT):
                                last = pe.matmul(o, prT[:, u % 2, 2 * r + st, :], v(st), start=st == 0,
                                                 stop=st == TT - 1)
                    last.then_inc(dve_full[3], 1)
                    if second:
                        evacuated()
                        scores(u + 2)

            pe.wait_ge(consts_pe, 1)
            pe.sem_inc(consts_pe, -1)
            with pe.Fori(0, DEPTH):
                to_xT(h)
                loop2(N_IN, rows_by_chunk, dve_full)
                def turn_qk(src):
                    for t in range(TT):
                        transposes(t, act_full, [(ps2(t)[:, j * P:(j + 1) * P], src[:, t, j * P:(j + 1) * P])
                                                 for j in range(5)])

                def turn_global():
                    pe.wait_ge(rotated_ready, 1)
                    pe.sem_inc(rotated_ready, -1)
                    turn_qk(qkr)

                pe.wait_ge(src_ready, 1)
                pe.sem_inc(src_ready, -1)
                turn_qk(proj[:, :, 768:1408])
                evacuated()
                pe.wait_ge(vals_ready, 1)
                pe.sem_inc(vals_ready, -1)

                def score(u, r):
                    ab, g, t = 1 - u // 4, u // 2 % 2, u % 2
                    rows = slice(HD * g, HD * g + HD)
                    return [(qkT[rows, ab, r, t * P:(t + 1) * P], qkT[rows, ab, 4, :])]

                def value(u, r):
                    at = 2 * (1 - u // 4) + u // 2 % 2
                    return [(ps2(3)[:, r * 65:(r + 1) * 65], lambda st: vaug[:, st, at, :])]

                attention(8, score, value, turn_global)
                to_xT(o_all)
                loop2(N_O, rows_by_chunk, dve_full)
                to_xT(h)
                pe.wait_ge(keys_in, 16)

                def key_scores(c, s):
                    pe.wait_ge(slot_free[1], 1)
                    pe.sem_inc(slot_free[1], -1)
                    for t in range(TT):
                        for p in range(2):
                            last = pe.matmul(PS[:, 2, (2 * t + p) * NK:(2 * t + p + 1) * NK],
                                             qTc[:, s, p, t * P:(t + 1) * P],
                                             peer_k[:, c, p * NK:(p + 1) * NK], start=True, stop=True)
                    last.then_inc(act_full[1], 1)

                chunk_by_cols(0, act_full)
                with pe.Fori(0, N_WQ // 2 - 1) as i:
                    for s in (0, 1):
                        chunk_by_cols(0, act_full)
                        key_scores(2 * i + s, s)
                chunk_by_cols(0, act_full)
                key_scores(N_WQ - 2, 0)
                pe.wait_ge(slot_free[0], 1)
                key_scores(N_WQ - 1, 1)
                pe.wait_ge(keys_in, 16)
                pe.sem_inc(keys_in, -16)
                def experts():
                    for j in range(2):
                        pe.wait_ge(slot_free[j], 1)
                        pe.sem_inc(slot_free[j], -1)
                        for q in (2 * j, 2 * j + 1):
                            pe.wait_ge(parts_ready[q], 1)
                            pe.sem_inc(parts_ready[q], -1)
                            for k in range(4):
                                at = 4 * (q % 2) + k
                                for i, (w, x) in enumerate(((wh, xh), (wh, xl), (wl, xh))):
                                    last = pe.matmul(PS[:, 2 * j, 0:S], w[:, q, k * P:(k + 1) * P], x[:, at, :],
                                                     start=at + i == 0, stop=at + i == 9)
                            if q % 2 == 0:
                                last.then_inc(parts_free[q], 1)
                        last.then_inc(act_full[j], 1)

                with pe.Fori(0, NPAIR):
                    experts()
                pe.wait_ge(src_ready, 1)
                pe.sem_inc(src_ready, -1)
                for t in range(TT):
                    transposes(t, dve_full, [(ps2(t)[:, i * P:(i + 1) * P], sel[:, i, t, :]) for i in range(3)])
                with pe.Fori(0, S // 8):
                    for s in (0, 1):
                        pe.wait_ge(oneh_ready, 1)
                        pe.sem_inc(oneh_ready, -1)
                        pe.wait_ge(slot_free[s], 1)
                        pe.sem_inc(slot_free[s], -1)
                        for n in range(4):
                            last = pe.matmul(PS[:, 2 * s, n * P:(n + 1) * P], ohA[:, s, n, :], ohB[:, s, n, :],
                                             start=True, stop=True)
                        last.then_inc(act_full[s], 1)
                for t in range(TT):
                    for c in range(2):
                        pe.matmul(acc[:, t, c * 512:(c + 1) * 512], identa[:, :], h[:, t, c * 512:(c + 1) * 512],
                                  start=True, stop=False)

                with pe.Fori(0, NPAIR - 1):
                    weigh()
                weigh(end=True)
                pe.drain().then_inc(acc_ready, 1)

            pe.wait_ge(src_ready, 2)
            pe.sem_inc(src_ready, -2)
            to_xT(tmp1)
            loop2(N_CONV, chunk_by_cols, dve_full)
            loop2(N_PROJ2 - 2, rows_by_chunk, dve_full)
            pe.wait_ge(src_ready, 1)
            pe.sem_inc(src_ready, -1)
            for t in range(TT):
                transposes(t, act_full, [(ps2(t)[:, i * P:(i + 1) * P], proj2[:, t, 512 + i * P:512 + (i + 1) * P])
                                         for i in range(2)])
            rows_by_chunk(0, dve_full)
            rows_by_chunk(1, dve_full, 24)
            for kv in range(2):
                pe.wait_ge(kb_ready, 1)
                pe.sem_inc(kb_ready, -1)
                pe.wait_ge(slot_free[kv], 1)
                pe.sem_inc(slot_free[kv], -1)
                for c in range(4):
                    s = c % 2
                    pe.wait_ge(chunk_in[s], 16)
                    pe.sem_inc(chunk_in[s], -16)
                    for j in range(8):
                        last = pe.matmul(PS[0:2 * NCMP, 2 * kv, 0:CW], kblk[:, kv, 8 * c + j, :],
                                         ring[:, s, j * CW:(j + 1) * CW], start=c + j == 0, stop=c + j == 10)
                    if c < 3:
                        last.then_inc(chunk_free[s], 2)
                last.then_inc(act_full[kv], 1)
            pe.wait_ge(src_ready, 1)
            pe.sem_inc(src_ready, -1)
            evacuated()
            for t in range(TT):
                transposes(t, act_full, [(ps2(t)[:, j * P:(j + 1) * P], qkr2[:, t, j * P:(j + 1) * P])
                                         for j in range(6)])
            pe.wait_ge(hid_ready, 1)
            pe.sem_inc(hid_ready, -1)
            transposes(0, act_full, [(PS[:, 0, (2 * kv + hb) * 2 * NCMP:(2 * kv + hb + 1) * 2 * NCMP],
                                      hid[0:2 * NCMP, kv, hb * P:(hb + 1) * P])
                                     for kv in range(2) for hb in range(2)])
            pe.wait_ge(kb_ready, 1)
            pe.sem_inc(kb_ready, -1)
            pe.wait_ge(slot_free[0], 1)
            pe.sem_inc(slot_free[0], -1)
            for g in range(2):
                for hb in range(2):
                    last = pe.matmul(PS[0:NCMP, 0, g * HD:(g + 1) * HD], hidT[:, 0, hb, g * NCMP:(g + 1) * NCMP],
                                     w2k[:, 0, hb, :], start=hb == 0, stop=hb == 1)
            last.then_inc(dve_full[0], 1)
            pe.wait_ge(slot_free[1], 1)
            pe.sem_inc(slot_free[1], -1)
            for hb in range(2):
                last = pe.matmul(PS[0:120, 2, 0:HD], hidx[:, hb, :], w2k[:, 1, hb, :], start=hb == 0, stop=hb == 1)
            last.then_inc(dve_full[1], 1)
            pe.wait_ge(src_ready, 1)
            pe.sem_inc(src_ready, -1)
            transposes(0, act_full, [(PS[:, 0, 0:NCMP], kcmp[0:NCMP, :])])
            pe.wait_ge(slot_free[1], 1)
            pe.sem_inc(slot_free[1], -1)
            pe.wait_ge(slot_free[0], 1)
            for t in range(TT):
                o = PS[:, 2, t * 120:(t + 1) * 120].rearrange("p (g r n) -> p g r n", g=2, r=4)
                for r in range(4):
                    last = pe.matmul(o[:, :, r, :], qk2T[:, r, t * P:(t + 1) * P], kcT[:, :],
                                     start=True, stop=True)
            last.then_inc(dve_full[1], 1)
            pe.wait_ge(pcT_ready, 1)
            pe.sem_inc(pcT_ready, -1)
            transposes(0, act_full, [(PS[0:120, 0, t * P:(t + 1) * P], pr_c[:, t, :]) for t in range(TT)])
            pe.wait_ge(slot_free[0], 1)
            for t, s in ((0, 1), (1, 0)):
                pe.wait_ge(slot_free[s], 1)
                pe.sem_inc(slot_free[s], -1)
                pe.matmul(PS[:, 2 * s, :], prT_c[0:120, t, :], bd[0:120, :], start=True, stop=True)
                pe.matmul(PS[:, 2 * s + 1, 0:8], prT_c[0:120, t, :], hmask[0:120, :], start=True,
                          stop=True).then_inc(dve_full[s], 1)
            pe.wait_ge(src_ready, 1)
            pe.sem_inc(src_ready, -1)
            pe.wait_ge(slot_free[1], 1)
            pe.sem_inc(slot_free[1], -1)
            for b in range(4):
                last = pe.matmul(PS[:, 2, 0:S], ones[:, :], convT[:, b, :], start=b == 0, stop=b == 3)
            last.then_inc(dve_full[1], 1)

            def score2(u, r):
                w, g, t = u // 4, u // 2 % 2, u % 2
                rows = slice(HD * g, HD * g + HD)
                return [(qk2T[rows, r, t * P:(t + 1) * P], qk2T[rows, 4 + w, :])]

            pe.wait_ge(vals_ready, 1)
            pe.sem_inc(vals_ready, -1)
            attention(8, score2, lambda u, r: [(ps2(3)[:, r * 65:(r + 1) * 65],
                                                lambda st: vaug[:, st, u // 2, :])])
            for t in range(TT):
                pe.wait_ge(src_ready, 1)
                pe.sem_inc(src_ready, -1)
                transposes(t, act_full, [(ps2(t)[:, k * P:(k + 1) * P], o_all[:, t, k * P:(k + 1) * P])
                                         for k in range(4)])
            evacuated()
            loop2(4, rows_by_chunk, dve_full)
            to_xT(tmp1)
            loop2(4, chunk_by_cols, act_full)
            to_xT(memr)
            loop2(4, chunk_by_cols, act_full)
            loop2(4, rows_by_chunk, act_full)
            evacuated()

            def score3(t, r):
                return [(qxT[:, 2 * r + b, t * P:(t + 1) * P], kxT[:, 2 * r + b, :]) for b in range(2)]

            def value3(t, r):
                pe.wait_ge(slot_free[t], 1)
                return [(PS[:, 2 * t, r:r + 1], lambda st: ones[:, 0:1]),
                        (ps2(3)[:, r * S:(r + 1) * S], lambda st: vx[:, st, r * S:(r + 1) * S])]

            attention(TT, score3, value3)
            to_xT(o_all)
            loop2(4, rows_by_chunk, dve_full)
            to_xT(tmp1)
            loop2(NFB, chunk_by_cols, act_full)
            weigh(begin=True)
            with pe.Fori(0, NFB // 2 - 2):
                weigh()
            weigh(end=True)
            pe.drain().then_inc(acc_ready, 1)

        @block.scalar
        def _(act):
            def high(s, q):
                if q == 0:
                    act.wait_ge(chunk_in[s], 16)
                    act.sem_inc(chunk_in[s], -16)
                act.wait_ge(parts_free[q], 1)
                act.sem_inc(parts_free[q], -1)
                act.activation(wh[:, q, :], ring[:, s, q * QW:(q + 1) * QW], ACT.Copy).then_inc(high_ready[q], 1)

            def high_parts(n, between=None, result=None, peel=0, late=None):
                for q in range(4):
                    high(0, q)
                if between:
                    between()

                def chunk(c, s, later=True):
                    for q in range(3):
                        high(s, q)
                    if result:
                        result(c - 1, 1 - s)
                    high(s, 3)
                    if late and later:
                        late(c - 2, s)

                if peel:
                    chunk(1, 1, False)
                    chunk(2, 0)
                if n > 2:
                    with act.Fori(peel, (n - 1) // 2) as i:
                        chunk(2 * i + 1, 1)
                        chunk(2 * i + 2, 0)
                if n % 2 == 0:
                    chunk(n - 1, 1)
                if result:
                    result(n - 1, (n - 1) % 2)
                if late:
                    late(n - 2, n % 2)
                    late(n - 1, 1 - n % 2)

            def evac(s, dst, src, parts=None):
                act.wait_ge(act_full[s], 1)
                act.sem_inc(act_full[s], -1)
                if parts is not None:
                    act.sem_inc(parts_free[3], 1)
                act.activation(dst, src, ACT.Copy).then_inc(slot_free[s], 1)

            def to_xT(nk=KB, k0=0):
                for t in range(TT):
                    act.wait_ge(act_full[t], 1)
                    act.sem_inc(act_full[t], -1)
                    act.activation(xh[:, k0:k0 + nk, t * P:(t + 1) * P],
                                   ps2(t)[:, 0:nk * P].rearrange("p (k n) -> p k n", k=nk),
                                   ACT.Copy).then_inc(xh_ready[t], 1)

            def halves(s):
                return PS[:, 2 * s:2 * s + 2, 0:CW]

            def attention(units, scale, sink=lambda u: False, turned=None):
                def exps(u):
                    act.wait_ge(shifted_ready, 1)
                    act.sem_inc(shifted_ready, -1)
                    raw = scale(u)
                    for r in range(4):
                        src = shf[:, u % 2, r, :] if raw is None else ps2(u % 2)[:, r * S:(r + 1) * S]
                        last = act.activation(prb[:, u % 2, r, :], src, ACT.Exp, scale=raw or 1.0,
                                              bias=mxn[:, u % 2, r:r + 1])
                    if raw is None:
                        last.then_inc(probs_ready, 1)
                    else:
                        last.then_inc(act_own, 1)
                        act.wait_ge(act_own, 1)
                        act.sem_inc(act_own, -1)
                        act.sem_inc(probs_ready, 1)
                        act.sem_inc(slot_free[u % 2], 1)
                    if sink(u):
                        act.wait_ge(sinkarg_ready, 1)
                        act.sem_inc(sinkarg_ready, -1)
                        act.activation(esk[:, u % 4, :], snk[:, u % 4, :], ACT.Exp).then_inc(sinkexp_ready, 1)

                exps(0)
                for u in range(units):
                    half = turned and u + 1 == units // 2
                    if u + 1 < units and not half:
                        exps(u + 1)
                    evac(2, prT[:, u % 2, :, :], ps2(2).rearrange("p (a b) -> p a b", a=8))
                    if half:
                        exps(u + 1)
                    if turned and u + 2 == units // 2:
                        turned()

            act.dma_start(h[:, :, :], A["x"][0].rearrange("(t p) d -> p t d", p=P)).then_inc(x_in, 16)
            act.dma_start(qkg[:, :, :], A["qk_g"].partition_broadcast(P)).then_inc(consts_in[20], 16)
            act.dma_start(sinks[:, :, :], A["sink"].partition_broadcast(P)).then_inc(consts_in[21], 16)
            for q in range(4):
                act.sem_inc(parts_free[q], 1)
            with act.Fori(0, DEPTH):
                high_parts(N_IN, to_xT)
                def qk_out(ab):
                    for t in range(TT):
                        evac(t, qkT[:, ab, 0:5, t * P:(t + 1) * P],
                             ps2(t)[:, 0:640].rearrange("p (k n) -> p k n", k=5))

                qk_out(1)
                attention(8, lambda u: None if u < 4 else SQ, lambda u: u < 4, lambda: qk_out(0))
                high_parts(N_O, to_xT)

                def scores_out(c, s):
                    act.wait_ge(act_full[1], 1)
                    act.sem_inc(act_full[1], -1)
                    act.wait_ge(scores_used, 1)
                    act.sem_inc(scores_used, -1)
                    act.activation(scc[s][:, :, :], PS[:, 2, :].rearrange("p (a n) -> p a n", a=4),
                                   ACT.Copy).then_inc(act_own, 1)
                    act.wait_ge(act_own, 1)
                    act.sem_inc(act_own, -1)
                    act.sem_inc(slot_free[1], 1)
                    act.sem_inc(scores_ready, 1)

                high_parts(N_WQ, to_xT, lambda c, s: evac(0, qTc[:, s, :, :], halves(0), s), 1, scores_out)

                def expert(c, s, j):
                    act.wait_ge(act_full[j], 1)
                    act.sem_inc(act_full[j], -1)
                    act.sem_inc(parts_free[2 * j + 1], 1)
                    act.activation(arena[:, bass.ts(2 * c + j, S)], PS[:, 2 * j, 0:S],
                                   ACT.Gelu).then_inc(slot_free[j], 1)

                def experts(c, s):
                    high(s, 0)
                    expert(c - 1, 1 - s, 0)
                    high(s, 1)
                    high(s, 2)
                    expert(c - 1, 1 - s, 1)
                    high(s, 3)

                for q in range(4):
                    high(0, q)
                early = TAIL // (4 * S)
                experts(1, 1)
                experts(2, 0)
                with act.Fori(1, early) as i:
                    experts(2 * i + 1, 1)
                    experts(2 * i + 2, 0)
                act.wait_ge(routing_done, 1)
                act.sem_inc(routing_done, -1)
                with act.Fori(early, NPAIR // 2 - 1) as i:
                    experts(2 * i + 1, 1)
                    experts(2 * i + 2, 0)
                experts(NPAIR - 1, 1)
                expert(NPAIR - 1, 1, 0)
                expert(NPAIR - 1, 1, 1)
                act.drain().then_inc(gelu_done, 1)
                act.wait_ge(smarg_ready, 1)
                act.sem_inc(smarg_ready, -1)
                act.activation(sel[:, 2, :, :], sel[:, 2, :, :], ACT.Exp).then_inc(smexp_ready, 1)
                for s in (0, 1):
                    act.sem_inc(gates_used[s], 1)
                with act.Fori(0, S // 8):
                    for s in (0, 1):
                        act.wait_ge(act_full[s], 1)
                        act.sem_inc(act_full[s], -1)
                        act.sem_inc(oneh_used[s], 1)
                        act.wait_ge(gates_used[s], 1)
                        act.sem_inc(gates_used[s], -1)
                        act.activation(gst[:, s, :], PS[:, 2 * s, :], ACT.Copy).then_inc(act_own, 1)
                        act.wait_ge(act_own, 1)
                        act.sem_inc(act_own, -1)
                        act.sem_inc(gates_ready[s], 1)
                        act.sem_inc(slot_free[s], 1)
                for s in (0, 1):
                    act.wait_ge(gates_used[s], 1)
                    act.sem_inc(gates_used[s], -1)
                act.sem_inc(gates_done, 1)
                high_parts(NPAIR)
            def to_xT_and_trig():
                to_xT()
                act.wait_ge(ang_ready, 1)
                act.sem_inc(ang_ready, -1)
                act.activation(angs[:, 6, :], angs[:, 2, :], ACT.Sin)
                act.activation(angs[:, 7, :], angs[:, 3, :], ACT.Sin).then_inc(trig_ready, 1)

            def raw_out():
                for t in range(TT):
                    evac(t, kcvT[:, :, t * P:(t + 1) * P], ps2(t)[:, 0:2 * P].rearrange("p (k n) -> p k n", k=2))
                act.drain().then_inc(evac_done, 1)

            high_parts(N_CONV + N_PROJ2 - 2, to_xT_and_trig)
            high_parts(2, raw_out)
            act.wait_ge(gate_arg, 1)
            act.sem_inc(gate_arg, -1)
            act.activation(gate[:, :, :], gate[:, :, :], ACT.Exp, scale=-1.0).then_inc(gate_exp, 1)
            for kv in range(2):
                act.wait_ge(act_full[kv], 1)
                act.sem_inc(act_full[kv], -1)
                act.sem_inc(chunk_free[1], 2)
                act.activation(hid[0:2 * NCMP, kv, :], PS[0:2 * NCMP, 2 * kv, 0:CW],
                               ACT.Silu).then_inc(slot_free[kv], 1)
            act.drain().then_inc(hid_ready, 1)
            for t in range(TT):
                evac(t, qk2T[:, :, t * P:(t + 1) * P], ps2(t)[:, 0:768].rearrange("p (k n) -> p k n", k=6))
            evac(0, hidT[:, :, :, :], PS[:, 0, 0:8 * NCMP].rearrange("p (a b n) -> p a b n", a=2, b=2))
            act.drain().then_inc(evac_done, 1)
            act.wait_ge(act_full[0], 1)
            act.sem_inc(act_full[0], -1)
            act.activation(kcT[0:HD, 0:NCMP], PS[0:HD, 0, 0:NCMP], ACT.Copy)
            act.activation(kcT[HD:P, NCMP:2 * NCMP], PS[HD:P, 0, 0:NCMP], ACT.Copy).then_inc(slot_free[0], 1)
            act.wait_ge(shifted_ready, 1)
            act.sem_inc(shifted_ready, -1)
            act.activation(pr_c[:, :, :], sc_c[:, :, :], ACT.Exp).then_inc(cmp_exp, 1)
            evac(0, prT_c[0:120, :, :], PS[0:120, 0, 0:2 * P].rearrange("p (t n) -> p t n", t=TT))
            act.wait_ge(var2_ready, 1)
            act.sem_inc(var2_ready, -1)
            act.activation(ss[:, :], ss[:, :], ACT.Sqrt).then_inc(std2_ready, 1)
            attention(8, lambda u: None)
            high_parts(4, lambda: to_xT(nk=4, k0=4))
            high_parts(4, to_xT, lambda c, s: evac(s, qxT[:, bass.ds(2 * c, 2), :], halves(s), s))
            high_parts(4, to_xT, lambda c, s: evac(s, kxT[:, bass.ds(2 * c, 2), :], halves(s), s))
            high_parts(4, None, lambda c, s: evac(s, vx[:, :, bass.ds(CW * c, CW)], halves(s), s))
            attention(TT, lambda u: 1.0 / 16)
            high_parts(4, to_xT)

            def silu(c, s):
                act.wait_ge(act_full[s], 1)
                act.sem_inc(act_full[s], -1)
                act.sem_inc(parts_free[3], 1)
                act.wait_ge(act_used, 1)
                act.sem_inc(act_used, -1)
                act.activation(sil[:, s, :], PS[:, 2 * s, 0:S], ACT.Silu).then_inc(silu_done, 1)

            high_parts(NFB, to_xT, silu, peel=1)
            high_parts(NFB // 2)

        @block.vector
        def _(dve):
            def own(ins):
                ins.then_inc(dve_own, 1)
                dve.wait_ge(dve_own, 1)
                dve.sem_inc(dve_own, -1)

            def bc(ap, *shape):
                return ap.to_broadcast([P, *shape])

            def power(n, scale, eps, sums):
                dve.tensor_scalar(ve[:, 0:n], sums, scale, eps, MUL, ADD).then_inc(var_ready, 1)
                dve.wait_ge(rstd_ready, 1)
                dve.sem_inc(rstd_ready, -1)

            def layer_norm(src, dst, at):
                for t in range(TT):
                    for c in range(2):
                        dve.bn_stats(stats[:, t, c, :], src[:, t, c * 512:(c + 1) * 512])
                own(dve.engine_nop())
                for t in range(TT):
                    dve.bn_aggr(mv[:, t, :], stats[:, t, :, :])
                own(dve.engine_nop())
                dve.tensor_scalar(ve[:, 0:TT], mv[:, :, 1], 1.0, 1e-5, MUL, ADD).then_inc(var_ready, 1)
                for i in range(2):
                    dve.wait_ge(gain_in[2 * at + i], 16)
                    dve.sem_inc(gain_in[2 * at + i], -16)
                g = (gains0, gains1)[at]
                for t in range(TT):
                    dve.scalar_tensor_tensor(tmp2[:, t, :], src[:, t, :], mv[:, t, 0:1], g[:, 0, :], SUB, MUL)
                own(dve.engine_nop())
                dve.wait_ge(rstd_ready, 1)
                dve.sem_inc(rstd_ready, -1)
                for t in range(TT):
                    dve.scalar_tensor_tensor(dst[:, t, :], tmp2[:, t, :], rstd[:, t:t + 1], g[:, 1, :],
                                             MUL, ADD).then_inc(src_ready, 1)
                own(dve.engine_nop())
                dve.sem_inc(gain_free[at], 1)

            def rms_norm(src, dst, at, width=D, ready=True):
                for t in range(TT):
                    dve.tensor_tensor_reduce(out=tmp2[:, t, 0:width], in0=src[:, t, 0:width], in1=src[:, t, 0:width],
                                             scale=1.0, scalar=0.0, op0=MUL, op1=ADD, accum_out=mv[:, t, 0:1])
                own(dve.engine_nop())
                power(TT, 1.0 / width, 1e-6, mv[:, :, 0])
                dve.wait_ge(gain_in[2 * at], 16)
                dve.sem_inc(gain_in[2 * at], -16)
                for t in range(TT):
                    part = dve.scalar_tensor_tensor(dst[:, t, 0:width], src[:, t, 0:width], rstd[:, t:t + 1],
                                                    (gains0, gains2)[at][:, 0, 0:width], MUL, MUL)
                    if ready:
                        part.then_inc(src_ready, 1)
                own(dve.engine_nop())
                dve.sem_inc(gain_free[at], 1)

            def residual_rms(src, at):
                rms_norm(src, tmp1, at, ready=False)
                own(dve.tensor_tensor(h[:, :, :], h[:, :, :], tmp1[:, :, :], ADD))

            def take_rows(s):
                dve.wait_ge(dve_full[s], 1)
                dve.sem_inc(dve_full[s], -1)
                dve.sem_inc(parts_free[3], 1)

            def low(s, q, freed=1):
                dve.wait_ge(high_ready[q], 1)
                dve.sem_inc(high_ready[q], -1)
                part = dve.tensor_tensor(wl[:, q, :], ring[:, s, q * QW:(q + 1) * QW],
                                         wh[:, q, :].bitcast(F32), SUB)
                if q < 3:
                    part.then_inc(parts_ready[q], 1)
                else:
                    own(part)
                    dve.sem_inc(parts_ready[3], 1)
                    dve.sem_inc(chunk_free[s], freed)

            def low_parts(n):
                with dve.Fori(0, n // 2):
                    for s in (0, 1):
                        low(s, 3)
                if n % 2:
                    low(0, 3)

            def low_xT(nk=KB, k0=0):
                for t in range(TT):
                    dve.wait_ge(xh_ready[t], 1)
                    dve.sem_inc(xh_ready[t], -1)
                    dve.tensor_tensor(xl[:, k0:k0 + nk, t * P:(t + 1) * P],
                                      ps2(t)[:, 0:nk * P].rearrange("p (k n) -> p k n", k=nk),
                                      xh[:, k0:k0 + nk, t * P:(t + 1) * P].bitcast(F32), SUB
                                      ).then_inc(slot_free[t], 1)

            def attention(units, first, finish):
                def scores(u):
                    s = u % 2
                    dve.wait_ge(dve_full[s], 1)
                    dve.sem_inc(dve_full[s], -1)
                    first(u, s)

                scores(0)
                scores(1)
                for u in range(units):
                    if u + 2 < units:
                        scores(u + 2)
                    dve.wait_ge(dve_full[3], 1)
                    dve.sem_inc(dve_full[3], -1)
                    finish(u, 3)

            def shift(u, s, scale, biased=None, sink=None):
                b = u % 2
                sc = ps2(s).rearrange("p (r n) -> p r n", r=4)
                if biased is None:
                    own(dve.tensor_reduce(mx[:, b, :], sc, AX.X, MAX))
                    dve.tensor_scalar(mxn[:, b, :], mx[:, b, :], -scale, None, MUL).then_inc(shifted_ready, 1)
                    return
                own(dve.scalar_tensor_tensor(shf[:, b, :, :], sc, scale, biased, MUL, ADD))
                dve.sem_inc(slot_free[s], 1)
                own(dve.tensor_reduce(mx[:, b, :], shf[:, b, :, :], AX.X, MAX))
                if sink is not None:
                    own(dve.tensor_tensor(mx[:, b, :], mx[:, b, :], sink, MAX))
                dve.tensor_scalar(mxn[:, b, :], mx[:, b, :], -1.0, None, MUL).then_inc(shifted_ready, 1)
                if sink is not None:
                    dve.tensor_tensor(snk[:, u % 4, :], sink, mx[:, b, :], SUB).then_inc(sinkarg_ready, 1)

            dve.wait_ge(consts_dve, 1)
            dve.sem_inc(consts_dve, -1)
            for s in range(4):
                dve.sem_inc(slot_free[s], 1)
            for s in (0, 1):
                dve.sem_inc(gain_free[s], 1)
            dve.sem_inc(keys_free, 1)
            dve.sem_inc(scores_used, 2)
            dve.wait_ge(x_in, 16)
            dve.sem_inc(x_in, -16)
            layer_norm(h, h, 0)
            for i in (20, 21):
                dve.wait_ge(consts_in[i], 16)
                dve.sem_inc(consts_in[i], -16)
            with dve.Fori(0, DEPTH) as l:
                dve.sem_inc(arena_free, 1)
                low_xT()
                with dve.Fori(0, N_IN // 2) as i:
                    for s in (0, 1):
                        low(s, 3)
                        take_rows(s)
                        dve.tensor_copy(proj[:, :, bass.ds(512 * i + 256 * s, 256)],
                                        PS[:, 2 * s:2 * s + 2, 0:CW]
                                        ).then_inc(slot_free[s], 1)
                own(dve.engine_nop())
                dve.sem_inc(src_ready, 1)
                own(dve.tensor_copy(qsc[:, 0:2 * HD], qkg[:, l, :]))
                own(dve.tensor_copy(qsc[:, 2 * HD:2 * HD + 8], sinks[:, l, :]))
                qk = proj[:, :, 0:640]
                sq = tmp1[:, :, 0:640]
                own(dve.tensor_tensor(sq, qk, qk, MUL))
                own(dve.tensor_reduce(ve[:, 0:20].rearrange("p (t h) -> p t h", t=TT),
                                      sq.rearrange("p t (h d) -> p t h d", d=HD), AX.X, ADD))
                dve.tensor_scalar(ve2[:, :], ve[:, 0:20], 1.0 / HD, 1e-6, MUL, ADD).then_inc(var_ready, 1)
                for ab in range(2):
                    at = 640 if ab == 0 else 1408
                    dve.tensor_copy(vaug[:, :, 2 * ab:2 * ab + 2, 0:HD],
                                    proj[:, :, at:at + 128].rearrange("p t (g d) -> p t g d", g=2))
                own(dve.memset(vaug[:, :, :, HD:HD + 1], 1.0))
                dve.sem_inc(vals_ready, 1)
                dve.wait_ge(bias_in, 16)
                dve.sem_inc(bias_in, -16)

                def first(u, s):
                    ab, g, t = 1 - u // 4, u // 2 % 2, u % 2
                    if ab == 0:
                        shift(u, s, SQ)
                    else:
                        shift(u, s, SQ, biasB[:, t, 4 * g:4 * g + 4, :], qsc[:, 2 * HD + 4 * g:2 * HD + 4 * g + 4])

                def finish(u, s):
                    ab, g, t = 1 - u // 4, u // 2 % 2, u % 2
                    v = ps2(s)[:, 0:260].rearrange("p (r n) -> p r n", r=4)
                    if ab:
                        dve.wait_ge(sinkexp_ready, 1)
                        dve.sem_inc(sinkexp_ready, -1)
                        own(dve.tensor_tensor(den[:, u % 2, :], v[:, :, HD], esk[:, u % 4, :], ADD))
                        own(dve.reciprocal(den[:, u % 2, :], den[:, u % 2, :]))
                    else:
                        own(dve.reciprocal(den[:, u % 2, :], v[:, :, HD]))
                    at = 512 * ab + 256 * g
                    o = o_all[:, t, at:at + 256].rearrange("p (r d) -> p r d", r=4)
                    own(dve.tensor_tensor(o, v[:, :, 0:HD], bc(den[:, u % 2, :].unsqueeze(2), 4, HD), MUL))
                    dve.sem_inc(slot_free[s], 1)
                    sq = tmp1[:, 0, 0:256].rearrange("p (r d) -> p r d", r=4)
                    own(dve.tensor_tensor(sq, o, o, MUL))
                    k = 16 * (1 - ab) + 8 * t + 4 * g
                    dve.tensor_reduce(ve[:, k:k + 4], sq, AX.X, ADD)
                    dve.tensor_tensor(o_all[:, t, at:at + 256], o_all[:, t, at:at + 256], gains1[:, 0, at:at + 256],
                                      MUL)

                    if u % 4 == 3:
                        own(dve.engine_nop())
                        c = slice(16 * (1 - ab), 16 * (1 - ab) + 16)
                        dve.tensor_scalar(ve[:, c], ve[:, c], 1.0 / HD, 1e-6, MUL, ADD).then_inc(var_ready, 1)
                    if u == 5 or u == 7:
                        dve.wait_ge(rstd_ready, 1)
                        dve.sem_inc(rstd_ready, -1)
                        ab = 1 if u == 5 else 0
                        for t in range(TT):
                            x = o_all[:, t, 512 * ab:512 * ab + 512].rearrange("p (h d) -> p h d", d=HD)
                            k = 16 * (1 - ab) + 8 * t
                            part = dve.tensor_tensor(x, x, bc(rstd[:, k:k + 8].unsqueeze(2), 8, HD), MUL)
                            if ab == 0:
                                part.then_inc(src_ready, 1)

                dve.wait_ge(gain_in[2], 16)
                dve.sem_inc(gain_in[2], -16)
                attention(8, first, finish)
                dve.sem_inc(gain_free[1], 1)
                low_xT()
                with dve.Fori(0, N_O // 2) as i:
                    for s in (0, 1):
                        low(s, 3)
                        take_rows(s)
                        c = bass.ds(512 * i + 256 * s, 256)
                        dve.scalar_tensor_tensor(h[:, :, c], h[:, :, c], ALPHA,
                                                 PS[:, 2 * s:2 * s + 2, 0:CW], MUL,
                                                 ADD).then_inc(slot_free[s], 1)
                own(dve.engine_nop())
                layer_norm(h, h, 1)
                low_xT()
                def best_keys(c, s):
                    dve.wait_ge(scores_ready, 1)
                    dve.sem_inc(scores_ready, -1)
                    for a in range(4):
                        dve.max(s16c[:, a, 0:8], scc[s][:, a, :])
                    own(dve.engine_nop())
                    for a in range(4):
                        dve.max_index(i16c[:, a, 0:8], s16c[:, a, 0:8], scc[s][:, a, :])
                        dve.match_replace(scr[:, a, :], s16c[:, a, 0:8], scc[s][:, a, :], -3e38)
                    own(dve.engine_nop())
                    for a in range(4):
                        dve.max(s16c[:, a, 8:16], scr[:, a, :])
                    own(dve.engine_nop())
                    for a in range(4):
                        dve.max_index(i16c[:, a, 8:16], s16c[:, a, 8:16], scr[:, a, :])
                    own(dve.engine_nop())
                    dve.tensor_copy(s16[:, c, :], s16c[:, :, :].rearrange("p a k -> p (a k)"))
                    own(dve.tensor_copy(i16[:, c, :], i16c[:, :, :].rearrange("p a k -> p (a k)")))
                    dve.sem_inc(scores_used, 1)

                low(0, 3)
                low(1, 3)
                with dve.Fori(0, N_WQ // 2 - 1) as i:
                    for s in (0, 1):
                        low(s, 3)
                        best_keys(2 * i + s, s)
                best_keys(N_WQ - 2, 0)
                best_keys(N_WQ - 1, 1)
                with dve.Fori(0, PH // 2) as cc:
                    for u in (0, 3):
                        c = 2 * cc + u // 3
                        sv = s16[:, c, :].rearrange("p (t a k) -> p t a k", t=TT, a=2)
                        iv = i16[:, c, :].rearrange("p (t a k) -> p t a k", t=TT, a=2)
                        for t in range(TT):
                            dve.tensor_tensor(cand[:, t, :].rearrange("p (i j) -> p i j", i=TOPK),
                                              bc(sv[:, t, 0, :].unsqueeze(2), TOPK, TOPK),
                                              bc(sv[:, t, 1, :].unsqueeze(1), TOPK, TOPK), ADD)
                        own(dve.engine_nop())
                        low(u % 2, 3)
                        for t in range(TT):
                            dve.max(t16[:, TOPK * t:TOPK * t + 8], cand[:, t, :])
                        own(dve.engine_nop())
                        for t in range(TT):
                            k = TOPK * t
                            dve.max_index(p16[:, k:k + 8], t16[:, k:k + 8], cand[:, t, :])
                            dve.match_replace(candr[:, t, :], t16[:, k:k + 8], cand[:, t, :], -3e38)
                        own(dve.engine_nop())
                        for t in range(TT):
                            dve.max(t16[:, TOPK * t + 8:TOPK * t + 16], candr[:, t, :])
                        own(dve.engine_nop())
                        for t in range(TT):
                            k = TOPK * t + 8
                            dve.max_index(p16[:, k:k + 8], t16[:, k:k + 8], candr[:, t, :])
                        own(dve.engine_nop())
                        low((u + 1) % 2, 3)
                        dve.tensor_scalar(pj[:, 0, :], p16[:, :], 4, None, ALU.logical_shift_right)
                        own(dve.tensor_scalar(pj[:, 1, :], p16[:, :], 15, None, ALU.bitwise_and))
                        own(dve.tensor_copy(pf[:, :, :], pj[:, :, :]))
                        for a in range(2):
                            own(dve.tensor_tensor(oneh[:, :, :], bc(iota16[:, :].unsqueeze(1), TT * TOPK, TOPK),
                                                  bc(pf[:, a, :].unsqueeze(2), TT * TOPK, TOPK), ALU.is_equal))
                            for t in range(TT):
                                x = oneh[:, TOPK * t:TOPK * t + TOPK, :]
                                dve.tensor_tensor(x, x, bc(iv[:, t, a, :].unsqueeze(1), TOPK, TOPK), MUL)
                            own(dve.engine_nop())
                            own(dve.tensor_reduce(sel[:, a, :, bass.ts(c, TOPK)],
                                                  oneh[:, :, :].rearrange("p (t k) j -> p t k j", t=TT), AX.X, ADD))
                        low((u + 2) % 2, 3)
                        for t in range(TT):
                            dve.tensor_scalar(sel[:, 2, t, bass.ts(c, TOPK)], t16[:, TOPK * t:TOPK * t + TOPK],
                                              t16[:, TOPK * t:TOPK * t + 1], None, SUB)
                        own(dve.engine_nop())
                dve.sem_inc(keys_free, 1)
                dve.sem_inc(routing_done, 1)
                dve.sem_inc(smarg_ready, 1)
                low_parts(NPAIR - 3 * PH)
                dve.wait_ge(smexp_ready, 1)
                dve.sem_inc(smexp_ready, -1)
                g3 = sel[:, 2, :, :].rearrange("p t (h k) -> p (t h) k", h=PH)
                own(dve.tensor_reduce(gsm[:, :], g3, AX.X, ADD))
                own(dve.reciprocal(gsm[:, :], gsm[:, :]))
                own(dve.tensor_tensor(g3, g3, bc(gsm[:, :].unsqueeze(2), TT * PH, TOPK), MUL))
                dve.sem_inc(src_ready, 1)
                for t in range(TT):
                    dve.wait_ge(dve_full[t], 1)
                    dve.sem_inc(dve_full[t], -1)
                    dve.tensor_copy(selT[:, :, t * P:(t + 1) * P],
                                    ps2(t)[:, 0:3 * P].rearrange("p (i n) -> p i n", i=3)).then_inc(slot_free[t], 1)
                own(dve.engine_nop())
                dve.wait_ge(gelu_done, 1)
                dve.sem_inc(gelu_done, -1)
                dve.sem_inc(choices_ready, 1)
                av = arena[:, :].rearrange("p (e n) -> p n e", n=S)

                def onehots(i, s):
                    at = 8 * i + 4 * s
                    dve.tensor_tensor(ohB[:, s, :, :], bc(iota[:, :].unsqueeze(1), 4, P),
                                      bc(selT[:, 1, bass.ds(at, 4)].unsqueeze(2), 4, P), ALU.is_equal)
                    for n in range(4):
                        last = dve.tensor_scalar(ohA[:, s, n, :], iota[:, :], selT[:, 0, bass.ds(at + n, 1)],
                                                 selT[:, 2, bass.ds(at + n, 1)], ALU.is_equal, MUL)
                    last.then_inc(oneh_ready, 1)

                onehots(0, 0)
                onehots(0, 1)
                with dve.Fori(1, S // 8) as i:
                    for s in (0, 1):
                        dve.wait_ge(oneh_used[s], 1)
                        dve.sem_inc(oneh_used[s], -1)
                        onehots(i, s)
                for s in (0, 1):
                    dve.wait_ge(oneh_used[s], 1)
                    dve.sem_inc(oneh_used[s], -1)
                dve.wait_ge(gates_done, 1)
                dve.sem_inc(gates_done, -1)

                def stage(c, j):
                    w = arena[:, bass.ts(2 * c + j, S)]
                    own(dve.tensor_copy(wst[0][:, j, :], w))
                    dve.tensor_tensor(wst[1][:, j, :], w, wst[0][:, j, :].bitcast(F32),
                                      SUB).then_inc(wst_ready[j], 1)

                def weights(c, s):
                    for j in range(2):
                        dve.wait_ge(wst_used[j], 1)
                        dve.sem_inc(wst_used[j], -1)
                        dve.sem_inc(parts_free[2 * j + 1], 1)
                        stage(c, j)
                        low(s, 2 * j)
                        low(s, 2 * j + 1, 2)

                for j in range(2):
                    stage(0, j)
                    low(0, 2 * j)
                    low(0, 2 * j + 1, 2)
                with dve.Fori(0, NPAIR // 2 - 1) as i:
                    weights(2 * i + 1, 1)
                    weights(2 * i + 2, 0)
                weights(NPAIR - 1, 1)
                for j in range(2):
                    dve.wait_ge(wst_used[j], 1)
                    dve.sem_inc(wst_used[j], -1)
                    dve.sem_inc(parts_free[2 * j + 1], 1)
                dve.wait_ge(acc_ready, 1)
                dve.sem_inc(acc_ready, -1)
                layer_norm(acc, h, 0)

            dve.sem_inc(arena_free, 1)
            rms_norm(h, tmp1, 1)
            low_xT()
            for i in range(9):
                dve.wait_ge(consts_in[i], 16)
            own(dve.tensor_copy(posv[:, :], pos_f[:, :].bitcast(I32)))
            a3 = angs[:, :, :].rearrange("p q (a f) -> p q a f", a=3)
            own(dve.tensor_tensor(a3[:, 0, :, :], bc(posv[:, :].unsqueeze(2), 3, 32),
                                  bc(invf[:, :].unsqueeze(1), 3, 32), MUL))
            magic = 1.5 * 2.0 ** 23
            own(dve.tensor_scalar(angs[:, 1, :], angs[:, 0, :], 1 / (2 * math.pi), magic, MUL, ADD))
            own(dve.tensor_scalar(angs[:, 1, :], angs[:, 1, :], magic, None, SUB))
            c1 = 6.28125
            c2 = round((2 * math.pi - c1) * 2 ** 20) / 2 ** 20
            c3 = 2 * math.pi - c1 - c2
            for at, (src, c) in enumerate(((0, c1), (2, c2), (3, c3))):
                own(dve.scalar_tensor_tensor(angs[:, 2 + at, :], angs[:, 1, :], -c, angs[:, src, :], MUL, ADD))
            pi = float(np.float32(3.1415925))
            own(dve.tensor_scalar(angs[:, 2, :], angs[:, 4, :], pi, -pi, ALU.min, MAX))
            own(dve.tensor_scalar(angs[:, 3, :], angs[:, 4, :], math.pi / 2, None, ADD))
            own(dve.tensor_scalar(angs[:, 5, :], angs[:, 3, :], math.pi, -2 * math.pi, ALU.is_gt, MUL))
            own(dve.tensor_tensor(angs[:, 3, :], angs[:, 3, :], angs[:, 5, :], ADD))
            own(dve.tensor_scalar(angs[:, 3, :], angs[:, 3, :], pi, -pi, ALU.min, MAX))
            dve.sem_inc(ang_ready, 1)
            dve.wait_ge(trig_ready, 1)
            dve.sem_inc(trig_ready, -1)
            for half in range(2):
                c = slice(32 * half, 32 * half + 32)
                dve.tensor_copy(rope2[:, 0, :, c], a3[:, 7, :, :])
                dve.tensor_scalar(rope2[:, 1, :, c], a3[:, 6, :, :], 1.0 if half else -1.0, None, MUL)
            own(dve.engine_nop())
            with dve.Fori(0, N_CONV // 2) as i:
                for s in (0, 1):
                    low(s, 3)
                    take_rows(s)
                    dve.tensor_copy(convT[:, bass.ds(4 * i + 2 * s, 2), :],
                                    PS[:, 2 * s:2 * s + 2, 0:S]).then_inc(slot_free[s], 1)
            with dve.Fori(0, (N_PROJ2 - 2) // 2) as i:
                for s in (0, 1):
                    low(s, 3)
                    take_rows(s)
                    dve.tensor_copy(proj2[:, :, bass.ds(512 * i + 256 * s, 256)],
                                    PS[:, 2 * s:2 * s + 2, 0:CW]).then_inc(slot_free[s], 1)
            own(dve.engine_nop())
            dve.sem_inc(src_ready, 1)
            low(0, 3)
            dve.memset(kcT[:, :], 0.0)
            own(dve.memset(kblk[:, :, :, :], 0.0))
            take_rows(0)
            dve.tensor_copy(proj2[:, :, 1024:1024 + CW], PS[:, 0:2, 0:CW]).then_inc(slot_free[0], 1)
            low(1, 3)
            dve.wait_ge(evac_done, 1)
            dve.sem_inc(evac_done, -1)

            def blocks(kv):
                for g in range(2):
                    rows = slice(HD * g, HD * g + HD)
                    v = kcvT[rows, kv, :].rearrange("p (m j) -> p j m", j=16)
                    for jh in range(2):
                        dve.tensor_tensor(
                            kblk[rows, kv, 16 * jh:16 * jh + 16, NCMP * g:NCMP * g + NCMP], v[:, :, jh:jh + NCMP],
                            peT[rows, kv, 16 * jh:16 * jh + 16].unsqueeze(2).to_broadcast([HD, 16, NCMP]), ADD)
                own(dve.engine_nop())
                dve.sem_inc(kb_ready, 1)

            blocks(0)
            take_rows(1)
            dve.tensor_copy(proj2[:, :, 1280:1304], PS[:, 2:4, 0:24]).then_inc(slot_free[1], 1)
            own(dve.engine_nop())
            own(dve.tensor_copy(gate[:, :, :], proj2[:, :, 1280:1304]))
            dve.sem_inc(gate_arg, 1)
            blocks(1)
            dve.wait_ge(gate_exp, 1)
            dve.sem_inc(gate_exp, -1)
            own(dve.tensor_scalar(gate[:, :, :], gate[:, :, :], 1.0, None, ADD))
            own(dve.reciprocal(gate[:, :, :], gate[:, :, :]))
            for t in range(TT):
                for at, to, nh in ((0, 0, 8), (768, 512, 2), (1024, 640, 2)):
                    rope(dve, own, proj2[:, t, at:at + HD * nh].rearrange("p (h d) -> p h d", d=HD),
                         qkr2[:, t, to:to + HD * nh].rearrange("p (h d) -> p h d", d=HD),
                         rope2[:, 0, t, :], rope2[:, 1, t, :], 1, 32,
                         tmp1[:, t, to:to + HD * nh].rearrange("p (h d) -> p h d", d=HD),
                         tmp2[:, t, to:to + HD * nh].rearrange("p (h d) -> p h d", d=HD))
            own(dve.engine_nop())
            dve.sem_inc(src_ready, 1)
            for w, at in ((0, 896), (1, 1152)):
                dve.tensor_copy(vaug[:, :, 2 * w:2 * w + 2, 0:HD],
                                proj2[:, :, at:at + 128].rearrange("p t (g d) -> p t g d", g=2))
            own(dve.memset(vaug[:, :, :, HD:HD + 1], 1.0))
            dve.sem_inc(vals_ready, 1)
            own(dve.tensor_tensor(zT[:, :, :], convT[:, 4:8, :], convT[:, 8:12, :], MUL))
            for b in range(4):
                dve.tensor_scalar(convT[:, 4 + b, :], zT[:, b, :], convw[:, b, 2:3], None, MUL)
            own(dve.engine_nop())
            for lag in (1, 2):
                for b in range(4):
                    c = convT[:, 4 + b, lag:S]
                    dve.scalar_tensor_tensor(c, zT[:, b, 0:S - lag], convw[:, b, 2 - lag:3 - lag], c, MUL, ADD)
                own(dve.engine_nop())
            own(dve.tensor_tensor(zT[:, :, :], convT[:, 0:4, :], convT[:, 4:8, :], MUL))
            own(dve.tensor_tensor(convT[:, 0:4, :], zT[:, :, :], zT[:, :, :], MUL))
            dve.wait_ge(evac_done, 1)
            dve.sem_inc(evac_done, -1)
            for hb in range(2):
                dve.tensor_copy(hidx[:, hb, :].rearrange("p (g r n) -> p g r n", g=2, r=4),
                                hidT[:, 1, hb, :].rearrange("p (g n) -> p g n", g=2).unsqueeze(2)
                                .to_broadcast([P, 2, 4, NCMP]))
            own(dve.engine_nop())
            dve.sem_inc(kb_ready, 1)
            dve.wait_ge(dve_full[0], 1)
            dve.sem_inc(dve_full[0], -1)
            own(dve.tensor_copy(krow[0:NCMP, :], PS[0:NCMP, 0, 0:2 * HD]))
            dve.sem_inc(slot_free[0], 1)
            hv = lambda x: x[0:NCMP, 0:2 * HD].rearrange("p (h d) -> p h d", d=HD)
            rope(dve, own, hv(krow), hv(kcmp), rope2[0:NCMP, 0, 2, :], rope2[0:NCMP, 1, 2, :], 1, 32,
                 hv(tmp1[:, 0, :]), hv(tmp2[:, 0, :]))
            own(dve.engine_nop())
            dve.sem_inc(src_ready, 1)
            dve.wait_ge(dve_full[1], 1)
            dve.sem_inc(dve_full[1], -1)
            own(dve.tensor_copy(v120[0:120, :], PS[0:120, 2, 0:HD]))
            dve.sem_inc(slot_free[1], 1)
            own(dve.tensor_tensor(bd[0:120, :].rearrange("p (h d) -> p h d", d=HD),
                                  v120[0:120, :].unsqueeze(1).to_broadcast([120, 8, HD]),
                                  hmask[0:120, :].unsqueeze(2).to_broadcast([120, 8, HD]), MUL))
            dve.wait_ge(dve_full[1], 1)
            dve.sem_inc(dve_full[1], -1)
            own(dve.tensor_scalar(sc_c[:, :, :], PS[:, 2, 0:240].rearrange("p (t n) -> p t n", t=TT), SQ, None, MUL))
            dve.sem_inc(slot_free[1], 1)
            for t in range(TT):
                x = sc_c[:, t, :].rearrange("p (h n) -> p h n", n=NCMP)
                own(dve.tensor_tensor(x, x, bc(cmpbias[:, t, :].unsqueeze(1), 8, NCMP), ADD))
                own(dve.tensor_reduce(mx_c[:, t, :], x, AX.X, MAX))
                own(dve.tensor_tensor(x, x, bc(mx_c[:, t, :].unsqueeze(2), 8, NCMP), SUB))
            dve.sem_inc(shifted_ready, 1)
            dve.wait_ge(cmp_exp, 1)
            dve.sem_inc(cmp_exp, -1)
            for t in range(TT):
                x = pr_c[:, t, :].rearrange("p (h n) -> p h n", n=NCMP)
                dve.tensor_tensor(x, x, bc(cmpmask[:, t, :].unsqueeze(1), 8, NCMP), MUL)
            own(dve.engine_nop())
            dve.sem_inc(pcT_ready, 1)
            gh = gate[:, :, :].rearrange("p t (h c) -> p t h c", c=3)
            for t, s in ((0, 1), (1, 0)):
                dve.wait_ge(dve_full[s], 1)
                dve.sem_inc(dve_full[s], -1)
                own(dve.tensor_scalar(dn_c[:, t, :], PS[:, 2 * s + 1, 0:8], 1e-30, None, MAX))
                own(dve.reciprocal(dn_c[:, t, :], dn_c[:, t, :]))
                own(dve.tensor_tensor(dn_c[:, t, :], dn_c[:, t, :], gh[:, t, :, 0], MUL))
                dve.tensor_tensor(o_all[:, t, 0:512].rearrange("p (h d) -> p h d", d=HD),
                                  PS[:, 2 * s, :].rearrange("p (h d) -> p h d", d=HD),
                                  bc(dn_c[:, t, :].unsqueeze(2), 8, HD), MUL).then_inc(slot_free[s], 1)
            own(dve.engine_nop())
            dve.sem_inc(src_ready, 1)
            dve.wait_ge(dve_full[1], 1)
            dve.sem_inc(dve_full[1], -1)
            own(dve.tensor_scalar(ss[:, :], PS[:, 2, 0:S], 1 / 512, 1e-6, MUL, ADD))
            dve.sem_inc(slot_free[1], 1)
            dve.sem_inc(var2_ready, 1)
            dve.wait_ge(std2_ready, 1)
            dve.sem_inc(std2_ready, -1)
            own(dve.reciprocal(ss[:, :], ss[:, :]))
            for b in range(4):
                dve.scalar_tensor_tensor(zT[:, b, :], zT[:, b, :], convw[:, b, 3:4], ss[:, :], MUL, MUL)
            own(dve.engine_nop())
            own(dve.tensor_copy(xh[:, 0:4, :], zT[:, :, :]))
            own(dve.tensor_tensor(xl[:, 0:4, :], zT[:, :, :], xh[:, 0:4, :].bitcast(F32), SUB))
            dve.sem_inc(mem_free, 1)

            def finish2(u, s):
                w, g, t = u // 4, u // 2 % 2, u % 2
                v = ps2(s)[:, 0:260].rearrange("p (r n) -> p r n", r=4)
                own(dve.reciprocal(den[:, u % 2, :], v[:, :, HD]))
                own(dve.tensor_tensor(den[:, u % 2, :], den[:, u % 2, :], gh[:, t, 4 * g:4 * g + 4, 1 + w], MUL))
                x = tmp1[:, u % 2, 0:256].rearrange("p (r d) -> p r d", r=4)
                own(dve.tensor_tensor(x, v[:, :, 0:HD], bc(den[:, u % 2, :].unsqueeze(2), 4, HD), MUL))
                dve.sem_inc(slot_free[s], 1)
                o = o_all[:, t, 256 * g:256 * g + 256].rearrange("p (r d) -> p r d", r=4)
                own(dve.tensor_tensor(o, o, x, ADD))
                if u == 3:
                    dve.wait_ge(mem_in, 16)
                    for i in range(TT):
                        dve.tensor_tensor_reduce(out=tmp2[:, i, :], in0=memr[:, i, :], in1=memr[:, i, :],
                                                 scale=1.0, scalar=0.0, op0=MUL, op1=ADD, accum_out=mv[:, i, 0:1])
                    own(dve.engine_nop())
                    dve.tensor_scalar(ve[:, 0:TT], mv[:, :, 0], 1.0 / D, 1e-6, MUL, ADD).then_inc(var_ready, 1)
                if u == 5:
                    dve.wait_ge(rstd_ready, 1)
                    dve.sem_inc(rstd_ready, -1)
                    dve.wait_ge(memgain_in, 16)
                    for i in range(TT):
                        dve.scalar_tensor_tensor(memr[:, i, :], memr[:, i, :], rstd[:, i:i + 1], gainm,
                                                 MUL, MUL)
                    own(dve.engine_nop())

            attention(8, lambda u, s: shift(u, s, SQ, bc(causal[:, u % 2, :].unsqueeze(1), 4, S)), finish2)
            rms_norm(o_all, o_all, 0, 512)
            low_xT(4, 4)

            def rows_to(dst):
                with dve.Fori(0, 2) as i:
                    for s in (0, 1):
                        low(s, 3)
                        take_rows(s)
                        dve.tensor_copy(dst[:, :, bass.ds(512 * i + 256 * s, 256)],
                                        PS[:, 2 * s:2 * s + 2, 0:CW]
                                        ).then_inc(slot_free[s], 1)
                own(dve.engine_nop())

            rows_to(o_all)
            residual_rms(o_all, 1)
            rms_norm(h, tmp1, 0)
            low_xT()
            dve.sem_inc(src_ready, 2)
            low_parts(4)
            low_xT()
            low_parts(8)

            def finish3(t, s):
                own(dve.reciprocal(den[:, t, :], PS[:, 2 * t, 0:4]))
                dve.tensor_tensor(o_all[:, t, :].rearrange("p (r d) -> p r d", r=4),
                                  ps2(s).rearrange("p (r d) -> p r d", r=4),
                                  bc(den[:, t, :].unsqueeze(2), 4, S), MUL).then_inc(slot_free[s], 1)

            attention(TT, lambda t, s: shift(t, s, 1.0 / 16), finish3)
            own(dve.engine_nop())
            dve.sem_inc(src_ready, 2)
            low_xT()
            rows_to(o_all)
            residual_rms(o_all, 0)
            rms_norm(h, tmp1, 1)
            low_xT()
            dve.sem_inc(act_used, 2)
            with dve.Fori(0, NFB // 2) as i:
                for s in (0, 1):
                    low(s, 3)
                    dve.wait_ge(silu_done, 1)
                    dve.sem_inc(silu_done, -1)
                    dve.tensor_tensor(ffT[:, 2 * i + s, :], sil[:, s, :], PS[:, 2 * s + 1, 0:S],
                                      MUL).then_inc(slot_free[s], 1)
                    own(dve.engine_nop())
                    dve.sem_inc(act_used, 1)

            def stage_down(c, j):
                f = ffT[:, 2 * c + j, :]
                own(dve.tensor_copy(wst[0][:, j, :], f))
                dve.tensor_tensor(wst[1][:, j, :], f, wst[0][:, j, :].bitcast(F32),
                                  SUB).then_inc(wst_ready[j], 1)

            for j in range(2):
                stage_down(0, j)
            low(0, 3)
            with dve.Fori(0, NFB // 4) as i:
                for s in (1, 0):
                    for j in range(2):
                        dve.wait_ge(wst_used[j], 1)
                        dve.sem_inc(wst_used[j], -1)
                        dve.sem_inc(parts_free[2 * j + 1], 1)
                        stage_down(2 * i + 2 - s, j)
                    low(s, 3)
            dve.wait_ge(acc_ready, 1)
            dve.sem_inc(acc_ready, -1)
            own(dve.tensor_copy(o_all[:, :, :], acc[:, :, :]))
            residual_rms(o_all, 0)
            dve.sem_inc(out_ready, 1)


def by_chunk(w):
    n = w.shape[-1]
    return w.reshape(KB, P, n // CW, CW).transpose(2, 1, 0, 3).reshape(n // CW, P, CHUNK)


def rows_of_tiles(a):
    return np.ascontiguousarray(a.reshape(TT, P, *a.shape[1:]).swapaxes(0, 1))


def shape_constants():
    f = np.float32
    t = np.arange(S)
    dist = np.abs(t[:, None] - t[None, :])
    slopes = (2.0 ** (-(np.arange(1, 9, dtype=f) * 8.0 / 8))).astype(f)
    bias = np.where(dist[:, None, :] <= 128, -(slopes[None, :, None] * dist[:, None, :].astype(f)), f(NEG))
    inv = (f(10000.0) ** (-np.arange(16, dtype=f) / f(16))).astype(f)
    pos = np.stack([t // 64, t % 64], -1).astype(f)
    ang = (pos[:, :, None] * inv).astype(f)
    cos = np.stack([np.cos(ang)] * 2, 2).reshape(S, HD)
    sin = np.stack([-np.sin(ang), np.sin(ang)], 2).reshape(S, HD)
    valid = (np.arange(NCMP)[None, :] * 16 + CMPJ - 1) <= t[:, None]
    head = np.zeros((P, 8), f)
    head[np.arange(120), np.arange(120) // NCMP] = 1.0
    return {
        "c_biasB": rows_of_tiles(bias.astype(f)),
        "c_ropeA": np.ascontiguousarray(
            np.stack([rows_of_tiles(cos), rows_of_tiles(sin)], 1).astype(f)),
        "c_causal": rows_of_tiles(np.where(t[None, :] <= t[:, None], f(0), f(NEG))),
        "c_cmpbias": rows_of_tiles(np.where(valid, f(0), f(NEG))),
        "c_cmpmask": rows_of_tiles(valid.astype(f)),
        "c_hmask": head,
        "c_invf": (f(10000.0) ** (-np.arange(32, dtype=f) / f(32))).astype(f),
    }


def layout(x):
    a = dict(shape_constants())
    heads = lambda at: [at + HD * i + j for i in PERM for j in range(HD)]
    cols = heads(0) + list(range(512, 768)) + heads(768) + list(range(1280, 1536))
    w = x["w_in"][:, :, cols]
    a["w_in"] = np.stack([by_chunk(m) for m in w])
    a["w_o"] = np.stack([by_chunk(m) for m in x["w_o"]])
    a["peer_wq"] = np.stack([by_chunk(m) for m in x["peer_wq"]])
    a["peer_keys"] = x["peer_keys"].transpose(0, 4, 1, 2, 3).reshape(DEPTH, P, PH, 2 * NK)
    a["peer_u"] = x["peer_u"].reshape(DEPTH, NK, NPAIR, 2, KB, P).transpose(0, 2, 5, 3, 4, 1).reshape(
        DEPTH, NPAIR, P, CHUNK)
    a["peer_v"] = x["peer_v"].reshape(DEPTH, NK, NPAIR, CHUNK).transpose(0, 2, 1, 3)
    a["gn_g"] = np.concatenate([x["gn_a_g"], x["gn_b_g"]], 1)
    a["qk_g"] = np.concatenate([x["qn_g"], x["kn_g"]], 1)
    for n in ("x", "ln_in_g", "ln_in_b", "sink", "ln1_g", "ln1_b", "ln2_g", "ln2_b", "mem_2",
              "norm_mix_pre_2", "norm_attn_out_2", "norm_mix_post_2", "norm_x_pre_2", "norm_mem_2",
              "norm_x_post_2", "norm_ffn_pre_2", "norm_ffn_post_2"):
        a[n] = x[n]
    p = np.arange(P)
    a["pos_2"] = x["positions_2"][0][np.stack([p, P + p, CMPJ - 1 + 16 * np.minimum(p, NCMP - 1)], 1)]
    w = x["w_in_2"]
    cols = list(range(1536)) + heads(1536) + list(range(2048, w.shape[1]))
    wide = np.zeros((D, (N_CONV + N_PROJ2) * CW), w.dtype)
    wide[:, :len(cols)] = w[:, cols]
    a["w_in_2"] = by_chunk(wide)
    w1 = np.stack([x["w1_kc_2"], x["w1_vc_2"]]).reshape(2, 4, 8, HD, CW).transpose(0, 1, 3, 2, 4)
    a["w1_2"] = np.concatenate([w1, w1], 2).reshape(8, P, CHUNK)
    a["w2_2"] = np.stack([x["w2_kc_2"], x["w2_vc_2"]]).reshape(2, 2, P, HD).transpose(2, 0, 1, 3)
    pe = np.stack([x["pe_kc_2"], x["pe_vc_2"]]).transpose(2, 0, 1)
    a["pe_2"] = np.concatenate([pe, pe], 0)
    a["conv_2"] = np.concatenate([x["conv_w_2"], x["norm_conv_out_2"][None]], 0).reshape(4, 4, P).transpose(2, 1, 0)
    for n in ("w_out_2", "w_q_x_2", "w_kv_x_2", "w_o_x_2"):
        a[n] = by_chunk(x[n])
    w = x["w_gate_up_2"]
    a["w_gate_up_2"] = by_chunk(w.reshape(D, 2, NFB, P).transpose(0, 2, 1, 3).reshape(D, 2 * FF))
    a["w_down_2"] = x["w_down_2"].reshape(NFB // 2, 2, P, D).transpose(0, 2, 1, 3).reshape(NFB // 2, P, CHUNK)
    return {k: np.ascontiguousarray(v) for k, v in a.items()}


def kernel(**inputs):
    import concourse.bacc as bacc
    from concourse.bass_utils import run_bass_kernel_spmd

    arrays = layout({k: np.asarray(v) for k, v in inputs.items()})
    nc = bacc.Bacc("TRN2", target_bir_lowering=False, num_devices=1)
    aps = {k: nc.dram_tensor(f"in_{k}", v.shape, mybir.dt.from_np(v.dtype), kind="ExternalInput").ap()
           for k, v in arrays.items()}
    out = nc.dram_tensor("out", (1, S, D), mybir.dt.float32, kind="ExternalOutput").ap()
    build(nc, aps, out)
    r = run_bass_kernel_spmd(nc, [{f"in_{k}": v for k, v in arrays.items()}], core_ids=[0])
    return r.results[0]["out"]
```
